# Optimizing a Trainium2 kernel written in Bass

```python
import math
import jax, jax.numpy as jnp
from jax import lax
import numpy as np

D_MODEL = 2048
BATCH = 1
SEQ = 512
DEPTH = 1

CHUNK = 64
SSM_WIDTH = D_MODEL // 2
SSM_GROUP = 16
N_SSM_GROUPS = SSM_WIDTH // SSM_GROUP
SSM_STATE = 64
DT_MIN = 1e-3
DT_MAX = 1e-1
HEAD_DIM = 64
N_HEADS = (D_MODEL // 2) // HEAD_DIM
N_KV_HEADS = max(1, N_HEADS // 8)
Q_PER_KV = N_HEADS // N_KV_HEADS
ATTN_WIDTH = N_HEADS * HEAD_DIM
KV_WIDTH = N_KV_HEADS * HEAD_DIM
WINDOW = 128
WINDOW_CHUNKS = WINDOW // CHUNK
KEY_BLOCK = WINDOW_CHUNKS * CHUNK
D_FF = -(-8 * D_MODEL // (3 * 256)) * 256
OFF_U = 0
OFF_Q = OFF_U + SSM_WIDTH
OFF_K = OFF_Q + ATTN_WIDTH
OFF_V = OFF_K + KV_WIDTH
OFF_GA = OFF_V + KV_WIDTH
OFF_GB = OFF_GA + D_MODEL
IN_WIDTH = OFF_GB + D_MODEL
RMS_EPS = 1e-6
NEG_INF = -1e30

kernel_name = 'hybrid_s5_swa_sink_chunk_encoder'

def rms_norm(x, g):
    xf = x.astype(jnp.float32)
    y = xf * lax.rsqrt(jnp.mean(xf * xf, axis=-1, keepdims=True) + RMS_EPS)
    return (y * g.astype(jnp.float32)).astype(x.dtype)

def s5_mixer(u, lam_re, lam_im, log_dt, b_re, b_im, c_re, c_im, d_skip, w_glu, b_glu):
    bsz, seq, _ = u.shape
    ug = u.reshape(bsz, seq, N_SSM_GROUPS, SSM_GROUP)
    dt = jnp.exp(log_dt)[:, None]
    mag = jnp.exp(lam_re * dt)
    ang = lam_im * dt
    a_re = mag * jnp.cos(ang)
    a_im = mag * jnp.sin(ang)
    den = lam_re * lam_re + lam_im * lam_im
    nr = a_re - 1.0
    f_re = ((nr * lam_re + a_im * lam_im) / den)[..., None]
    f_im = ((a_im * lam_re - nr * lam_im) / den)[..., None]
    bb_re = f_re * b_re - f_im * b_im
    bb_im = f_re * b_im + f_im * b_re
    x_re = jnp.einsum('gpc,blgc->blgp', bb_re, ug)
    x_im = jnp.einsum('gpc,blgc->blgp', bb_im, ug)
    ar = jnp.broadcast_to(a_re, (1, seq) + a_re.shape)
    ai = jnp.broadcast_to(a_im, (1, seq) + a_im.shape)

    def combine(e1, e2):
        a1r, a1i, b1r, b1i = e1
        a2r, a2i, b2r, b2i = e2
        return (a1r * a2r - a1i * a2i,
                a1r * a2i + a1i * a2r,
                a2r * b1r - a2i * b1i + b2r,
                a2r * b1i + a2i * b1r + b2i)

    _, _, h_re, h_im = lax.associative_scan(combine, (ar, ai, x_re, x_im), axis=1)
    y = (jnp.einsum('gcp,blgp->blgc', c_re, h_re)
         - jnp.einsum('gcp,blgp->blgc', c_im, h_im)
         + d_skip * ug).reshape(bsz, seq, SSM_WIDTH)
    z = jax.nn.gelu(y)
    return z * jax.nn.sigmoid(z @ w_glu + b_glu)

def alibi_bias():
    dist = np.abs(np.arange(CHUNK)[:, None] + (WINDOW_CHUNKS - 1) * CHUNK
                  - np.arange(KEY_BLOCK)[None, :]).astype(np.float32)
    slopes = (2.0 ** (-8.0 * np.arange(1, N_HEADS + 1) / N_HEADS)).astype(np.float32)
    bias = -(slopes.reshape(N_KV_HEADS, Q_PER_KV)[:, :, None, None] * dist[None, None])
    return jnp.asarray(bias, dtype=jnp.float32)

def band(t, n_chunks):
    parts = []
    for w in range(WINDOW_CHUNKS - 1, 0, -1):
        parts.append(jnp.pad(t, ((0, 0), (w, 0), (0, 0), (0, 0), (0, 0)))[:, :n_chunks])
    parts.append(t)
    return jnp.concatenate(parts, axis=2)

def sink_window_attention(q, k, v, sinks):
    bsz, seq, _ = q.shape
    n_chunks = seq // CHUNK
    q = q.reshape(bsz, n_chunks, CHUNK, N_KV_HEADS, Q_PER_KV, HEAD_DIM)
    k = k.reshape(bsz, n_chunks, CHUNK, N_KV_HEADS, HEAD_DIM)
    v = v.reshape(bsz, n_chunks, CHUNK, N_KV_HEADS, HEAD_DIM)
    kb = band(k, n_chunks)
    vb = band(v, n_chunks)
    s = jnp.einsum('bnqhgd,bnkhd->bhgnqk', q, kb).astype(jnp.float32) * (HEAD_DIM ** -0.5)
    s = s + alibi_bias()[:, :, None]
    key_chunk = (np.arange(n_chunks)[:, None] - (WINDOW_CHUNKS - 1)
                 + np.arange(KEY_BLOCK)[None, :] // CHUNK)
    valid = jnp.asarray(key_chunk >= 0)[:, None, :]
    s = jnp.where(valid, s, NEG_INF)
    sk = sinks.astype(jnp.float32).reshape(N_KV_HEADS, Q_PER_KV, 1, 1, 1)
    m = jnp.maximum(jnp.max(s, axis=-1, keepdims=True), sk)
    p = jnp.exp(s - m)
    denom = jnp.sum(p, axis=-1, keepdims=True) + jnp.exp(sk - m)
    probs = (p / denom).astype(v.dtype)
    o = jnp.einsum('bhgnqk,bnkhd->bnqhgd', probs, vb)
    return o.reshape(bsz, seq, ATTN_WIDTH)

def setup_inputs(seed: int = 0) -> dict:
    key = jax.random.key(seed)
    ks = jax.random.split(key, 24)
    f32 = jnp.float32

    def nrm(k, shape, scale):
        return jax.random.normal(k, shape, f32) * scale

    nl, g, p, c = DEPTH, N_SSM_GROUPS, SSM_STATE, SSM_GROUP
    n_idx = jnp.arange(p, dtype=f32)
    return {
        'x': nrm(ks[0], (BATCH, SEQ, D_MODEL), 1.0),
        'norm1_g': 1.0 + nrm(ks[1], (nl, D_MODEL), 0.01),
        'w_in': nrm(ks[2], (nl, D_MODEL, IN_WIDTH), D_MODEL ** -0.5),
        'lam_re': -0.5 + nrm(ks[3], (nl, g, p), 0.01),
        'lam_im': math.pi * n_idx + nrm(ks[4], (nl, g, p), 0.01),
        'log_dt': jax.random.uniform(ks[5], (nl, g), f32, math.log(DT_MIN), math.log(DT_MAX)),
        'b_re': nrm(ks[6], (nl, g, p, c), c ** -0.5),
        'b_im': nrm(ks[7], (nl, g, p, c), c ** -0.5),
        'c_re': nrm(ks[8], (nl, g, c, p), p ** -0.5),
        'c_im': nrm(ks[9], (nl, g, c, p), p ** -0.5),
        'd_skip': nrm(ks[10], (nl, g, c), 1.0),
        'w_glu': nrm(ks[11], (nl, SSM_WIDTH, SSM_WIDTH), SSM_WIDTH ** -0.5),
        'b_glu': nrm(ks[12], (nl, SSM_WIDTH), 0.01),
        'sinks': nrm(ks[13], (nl, N_HEADS), 1.0),
        'w_a': nrm(ks[14], (nl, SSM_WIDTH, D_MODEL), SSM_WIDTH ** -0.5),
        'w_b': nrm(ks[15], (nl, ATTN_WIDTH, D_MODEL), ATTN_WIDTH ** -0.5),
        'w_o': nrm(ks[16], (nl, D_MODEL, D_MODEL), D_MODEL ** -0.5),
        'norm2_g': 1.0 + nrm(ks[17], (nl, D_MODEL), 0.01),
        'w_gate': nrm(ks[18], (nl, D_MODEL, D_FF), D_MODEL ** -0.5),
        'w_up': nrm(ks[19], (nl, D_MODEL, D_FF), D_MODEL ** -0.5),
        'w_down': nrm(ks[20], (nl, D_FF, D_MODEL), D_FF ** -0.5),
        'normf_g': 1.0 + nrm(ks[21], (D_MODEL,), 0.01),
    }

def reference(x, norm1_g, w_in, lam_re, lam_im, log_dt, b_re, b_im, c_re, c_im, d_skip,
              w_glu, b_glu, sinks, w_a, w_b, w_o, norm2_g, w_gate, w_up, w_down, normf_g):
    for l in range(DEPTH):
        h = rms_norm(x, norm1_g[l])
        proj = h @ w_in[l]
        u = proj[..., OFF_U:OFF_Q]
        q = proj[..., OFF_Q:OFF_K]
        k = proj[..., OFF_K:OFF_V]
        v = proj[..., OFF_V:OFF_GA]
        gate_a = jax.nn.sigmoid(proj[..., OFF_GA:OFF_GB])
        gate_b = jax.nn.sigmoid(proj[..., OFF_GB:IN_WIDTH])
        y_a = s5_mixer(u, lam_re[l], lam_im[l], log_dt[l], b_re[l], b_im[l],
                       c_re[l], c_im[l], d_skip[l], w_glu[l], b_glu[l])
        y_b = sink_window_attention(q, k, v, sinks[l])
        merged = gate_a * (y_a @ w_a[l]) + gate_b * (y_b @ w_b[l])
        x = x + merged @ w_o[l]
        h2 = rms_norm(x, norm2_g[l])
        x = x + (jax.nn.silu(h2 @ w_gate[l]) * (h2 @ w_up[l])) @ w_down[l]
    return rms_norm(x, normf_g)


_drawn_inputs = setup_inputs


def setup_inputs(seed=0):
    import zlib

    import numpy as np

    out = dict(_drawn_inputs(seed))
    spreads = {}
    factors = {'norm1_g': 8.0,
     'lam_re': 64.0,
     'b_re': 2.934,
     'b_im': 2.974,
     'c_re': 2.954,
     'c_im': 2.958,
     'b_glu': 60.434,
     'sinks': 3.484,
     'norm2_g': 31.38,
     'normf_g': 30.548}
    for name, (base, spread) in spreads.items():
        noise = np.random.default_rng([zlib.crc32(name.encode()), seed]).standard_normal(out[name].shape)
        drawn = base * np.exp(spread * noise) if base else spread * noise
        out[name] = __import__('jax').numpy.asarray(drawn.astype(out[name].dtype))
    for name, factor in factors.items():
        out[name] = (out[name] * factor).astype(out[name].dtype)
    return out
```

```python
import math
from contextlib import ExitStack

import numpy as np

import concourse.bass as bass
from concourse import mybir

F32 = mybir.dt.float32
F32R = mybir.dt.float32r
ACT = mybir.ActivationFunctionType
ALU = mybir.AluOpType
AX = mybir.AxisListType

P = 128
D = 2048
T = 512
TT = T // P
KT = D // P
HALF = 1024
HT = HALF // P
IN_W = 6400
OFF_Q, OFF_K, OFF_V, OFF_GATE = 1024, 2048, 2176, 2304
DFF = 5632
UNIT = KT * P
NG, GC, NS = 64, 16, 64
L = 8
M = T // L
GP = NG // 2
GB = 8
NBLK = GP // GB
NCH, CH = 8, 64
PAIRS, HD = 8, 64
KEYS = 128
FB, FT = 4, 11
DK = [4, 4, 3]
NB = D // 512
EPS = 1e-6
NEG = -1e30
GELU_C = math.sqrt(2.0 / math.pi)
ROUND = 1.5 * 2.0 ** 23
TWO_PI = [6.28125, 0.0019340515136718750, 1.2556659146e-6]
KPAD = 7 * GC + L * GC

U_KV = 16
U_GATE = 18
U_GLU = 50
U_AB = 54
U_O = 70
U_FF = 86
FB_UNITS = 2 * FT + NB * len(DK)
U_END = U_FF + FB * FB_UNITS


class Chain:

    def __init__(self, eng, sem):
        self.eng, self.sem, self.base, self.n, self.saved = eng, sem, 0, 0, []

    def __call__(self, ins):
        ins.then_inc(self.sem, 1)
        self.n += 1
        self.eng.wait_ge(self.sem, self.base + self.n)

    def enter(self, j, per):
        self.saved.append(self.base + self.n)
        self.base, self.n = self.saved[-1] + j * per, 0

    def leave(self, times, per):
        assert self.n == per, (self.n, per)
        self.base, self.n = self.saved.pop() + times * per, 0


def build(nc, x, norm1_g, w_in, lam_re, lam_im, log_dt, b_re, b_im, c_re, c_im, d_skip, w_glu, b_glu,
          sinks, w_a, w_b, w_o, norm2_g, w_gate, w_up, w_down, normf_g, ident_c, alibi_c,
          u_s, cout_s, kp_s, y_s, gate_s, out):
    ctx = ExitStack()
    with ctx:
        base = -(-nc.sbuf_base // 32) * 32
        end = nc.sbuf_usable_end

        def at(name, shape, kb, dt=F32):
            off = base + int(kb * 1024)
            assert off + 4 * int(np.prod(shape[1:])) <= end, name
            return nc.alloc_sbuf_tensor_at(name, shape, dt, offset=off)

        def sem(name):
            return ctx.enter_context(nc.semaphore(name))

        raw = at("raw", [P, 2, UNIT], 0)
        w_hi = at("w_hi", [P, 2, UNIT], 16, F32R)
        w_lo = at("w_lo", [P, 2, UNIT], 32, F32R)
        act_hi = at("act_hi", [P, KT, T], 48, F32R)
        act_lo = at("act_lo", [P, KT, T], 80, F32R)
        ident = at("ident", [P, P], 112)
        vec_t = at("vec_t", [P, 48], 112.5)
        b_half = at("b_half", [P, HT], 112.6875)
        stat = at("stat", [P, 4, TT], 112.71875)
        sink = at("sink", [P, PAIRS], 112.78125)
        sink_raw = at("sink_raw", [P, 2 * PAIRS], 112.9375)
        row_max = at("row_max", [P, PAIRS], 112.8125)
        neg_max = at("neg_max", [P, PAIRS], 112.84375)
        den = at("den", [P, PAIRS], 112.875)
        sink_e = at("sink_e", [P, PAIRS], 112.90625)
        vec_raw = at("vec_raw", [48, P], 113)
        ar8 = at("ar8", [P, 2, GP], 113.5)
        ai8 = at("ai8", [P, 2, GP], 113.75)
        A = 114
        xt = at("xt", [P, TT, D], A)
        x1 = at("x1", [P, TT, D], A)
        q_t = at("q_t", [P, PAIRS, T], A)
        cout = at("cout", [P, 2, GB, L + 1, GC], A + 16)
        tmp = at("tmp", [P, GB * (L + 1) * GC], A + 25)
        bb_pad = at("bb_pad", [P, 2, GB, 2 * GC], A + 29.5)
        k_pad = at("k_pad", [P, 2, CH + T], A + 16)
        v_t = at("v_t", [P, CH + T], A + 20.5)
        q_c = at("q_c", [P, PAIRS, CH], A + 22.75)
        k_c = at("k_c", [P, 2, KEYS], A + 24.75)
        v_ct = at("v_ct", [P, KEYS], A + 25.75)
        v_c = at("v_c", [P, P], A + 26.25)
        gate_o = at("gate_o", [P, 2, T], A + 27)
        state = at("state", [P, M, 2, GP], A + 32)
        b_sb = at("b_sb", [P, 2, GP, GC], A + 48)
        c_sb = at("c_sb", [P, 2, GP, GC], A + 52)
        powers = at("powers", [P, L + 1, 2, GP], A + 56)
        ab_f = at("ab_f", [P, 4, GP], A + 58.25)
        p_tmp = at("p_tmp", [P, 5, GP], A + 58.75)
        sc_t = at("sc_t", [P, 2, 2, GP], A + 90)
        par = at("par", [GP, 4, 2, NS * GC], A + 60)
        lam = at("lam", [GP, 16, 2, NS], A + 32)
        dt_r = at("dt_r", [GP, 2], A + 92)
        bin_t = at("bin_t", [P, 2, GB, P], A + 60)
        k_row = at("k_row", [GP, GB, KPAD], A + 68)
        u2 = at("u2", [P, 2 * GB, M], A + 76)
        u_p = at("u_p", [P, 2, L, M], A + 80)
        b_in = at("b_in", [P, 2, GB, L, GC], A + 84)
        bias = at("bias", [P, PAIRS, KEYS], A + 48)
        score = at("score", [P, PAIRS, KEYS], A + 52)
        prob = at("prob", [P, PAIRS, KEYS], A + 56)
        prob_t = at("prob_t", [P, PAIRS, P], A + 60)
        cy = at("cy", [P, 2, GB, P], A + 64)
        toe = at("toe", [P, 2 * GB, P], A + 72)
        u2y = at("u2y", [P, 2 * GB, M], A + 80)
        y_sb = at("y_sb", [P, 2, GB, M], A + 84)
        st_c = at("st_c", [P, 2, GB, M], A + 88)
        yb_hi = at("yb_hi", [P, HT, T], A + 32, F32R)
        yb_lo = at("yb_lo", [P, HT, T], A + 48, F32R)
        ya_hi = at("ya_hi", [P, HT, T], A, F32R)
        ya_lo = at("ya_lo", [P, HT, T], A + 16, F32R)
        zz = at("zz", [P, HT, T], A + 64)
        y_in = at("y_in", [P, 2, T], A + 80)
        u_in = at("u_in", [P, 2, T], A + 84)
        g_v = at("g_v", [P, 2, T], A + 88)
        gate_in = at("gate_in", [P, 2, 2, T], A + 80)
        mrg = at("mrg", [P, 2, T], A + 88)
        xn = at("xn", [P, TT, D], A + 32)
        m_hi = at("m_hi", [P, FT, T], A + 32, F32R)
        m_lo = at("m_lo", [P, FT, T], A + 54, F32R)
        ff_t = at("ff_t", [P, T], A + 76)
        ff_m = at("ff_m", [P, T], A + 78)
        normf = at("normf", [P, D], A + 84)

        bank = [ctx.enter_context(nc.psum_tensor(f"bank{i}", [P, 512], F32)) for i in range(8)]

        raw_here = [sem("raw_here0"), sem("raw_here1")]
        hi_ready = sem("hi_ready")
        lo_ready = sem("lo_ready")
        units_done = sem("units_done")
        read_out = sem("read_out")
        x_here = [sem(f"x_here{t}") for t in range(TT)]
        const_here, par_here, dt_here = sem("const_here"), sem("par_here"), sem("dt_here")
        dve_own, pool_own = sem("dve_own"), sem("pool_own")
        ssq_ready, var_ready = sem("ssq_ready"), sem("var_ready")
        root_ready, rstd_ready = sem("root_ready"), sem("rstd_ready")
        xn_ready = sem("xn_ready")
        tr_done = sem("tr_done")
        nhi_ready, nlo_ready = sem("nhi_ready"), sem("nlo_ready")
        par_t, par_out = sem("par_t"), sem("par_out")
        dt_exp, mag_arg, mag_ready = sem("dt_exp"), sem("mag_arg"), sem("mag_ready")
        ang_ready, sin_ready, af_ready = sem("ang_ready"), sem("sin_ready"), sem("af_ready")
        vec_ready = sem("vec_ready")
        powers_ready = sem("powers_ready")
        tab_c, tab_b = sem("tab_c"), sem("tab_b")
        bint_done, bint_ready = sem("bint_done"), sem("bint_ready")
        k_done, krow_ready, krow_zero = sem("k_done"), sem("krow_ready"), sem("krow_zero")
        u_stored, u2_here, tab_stored = sem("u_stored"), sem("u2_here"), sem("tab_stored")
        x_done, state_in = sem("x_done"), sem("state_in")
        pads, kv_ev, kv_dup, bias_here = sem("pads"), sem("kv_ev"), sem("kv_dup"), sem("bias_here")
        staged, scores_done, neg_ready = sem("staged"), sem("scores_done"), sem("neg_ready")
        exps, vc_ready, prob_ready = sem("exps"), sem("vc_ready"), sem("prob_ready")
        pt_done, pt_ready, pv_done, yb_ready = sem("pt_done"), sem("pt_ready"), sem("pv_done"), sem("yb_ready")
        gate_st = [sem("gate_st0"), sem("gate_st1")]
        ytab_here, st_staged = sem("ytab_here"), sem("st_staged")
        y_done, y_ev, y_stored = sem("y_done"), sem("y_ev"), sem("y_stored")
        yin_here = [sem("yin_here0"), sem("yin_here1")]
        y_arg, y_tanh, zz_ready = sem("y_arg"), sem("y_tanh"), sem("zz_ready")
        zhi_ready, zlo_ready = sem("zhi_ready"), sem("zlo_ready")
        ybhi_ready, yblo_ready = sem("ybhi_ready"), sem("yblo_ready")
        glu_t, glu_m = sem("glu_t"), sem("glu_m")
        yahi_ready, yalo_ready = sem("yahi_ready"), sem("yalo_ready")
        gin_here = [sem("gin_here0"), sem("gin_here1")]
        mrg_ready, mhi_ready, mlo_ready = sem("mrg_ready"), sem("mhi_ready"), sem("mlo_ready")
        xres_here, normf_here = sem("xres_here"), sem("normf_here")
        tok_done = sem("tok_done")
        tok_free = sem("tok_free")
        ff_read, up_read = sem("ff_read"), sem("up_read")
        ff_tanh = sem("ff_tanh")
        ffhi_ready, fflo_ready = sem("ffhi_ready"), sem("fflo_ready")
        out_ready, out_st = sem("out_ready"), sem("out_st")

        def k_rows(w):
            return w[0].rearrange("(k p) n -> p k n", p=P)

        win_v, glu_v, wa_v, wb_v = k_rows(w_in), k_rows(w_glu), k_rows(w_a), k_rows(w_b)
        wo_v, wg_v, wu_v, wd_v = k_rows(w_o), k_rows(w_gate), k_rows(w_up), k_rows(w_down)
        x_v = x[0].rearrange("(t p) n -> p t n", p=P)
        out_v = out[0].rearrange("(t p) n -> p t n", p=P)

        def slot(tile, p, width):
            return tile[:, p, :].rearrange("p (k n) -> p k n", n=width)

        def arrived(q, p):
            return 16 * q + 16

        block = ctx.enter_context(nc.Block())

        def apart(eng):
            eng.wait_ge(vec_ready, 1)

        @block.sync
        def _(sp):
            for t in range(TT):
                sp.dma_start(xt[:, t, :], x_v[:, t, :]).then_inc(x_here[t], 16)

            def load(u, p, src, dst, first=False):
                if not first:
                    sp.wait_ge(lo_ready, u - 1)
                sp.dma_start(dst, src).then_inc(raw_here[p], 16)

            def load_in(b, first=False):
                cols = [b * P, b * P + NBLK * P, b * (2 * P) + OFF_Q, b * (2 * P) + (OFF_Q + P)]
                for i, c in enumerate(cols):
                    load(4 * b + i, i % 2, win_v[:, :, bass.ds(c, P)], slot(raw, i % 2, P), first=first and i < 2)

            load_in(0, True)
            with sp.Fori(1, NBLK) as b:
                load_in(b)
            load(U_KV, 0, win_v[:, :, OFF_K:OFF_K + P], slot(raw, 0, P))
            load(U_KV + 1, 1, win_v[:, :, OFF_V:OFF_V + P], slot(raw, 1, P))
            with sp.Fori(0, 16) as j:
                for i in range(2):
                    load(U_GATE + 2 * j + i, i, win_v[:, :, bass.ds(j * (2 * P) + (OFF_GATE + i * P), P)],
                         slot(raw, i, P))
            for i in range(4):
                load(U_GLU + i, i % 2, glu_v[:, :, i * 256:(i + 1) * 256], slot(raw, i % 2, 256))
            with sp.Fori(0, 8) as j:
                for i in range(2):
                    cols = bass.ds(j * (2 * P) + i * P, P)
                    load(U_AB + 2 * j + i, i, wa_v[:, :, cols], slot(raw, i, P)[:, 0:HT])
                    sp.dma_start(slot(raw, i, P)[:, HT:KT], wb_v[:, :, cols]).then_inc(raw_here[i], 16)
            with sp.Fori(0, NB) as n:
                for i in range(4):
                    load(U_O + 4 * n + i, i % 2, wo_v[:, 4 * i:4 * i + 4, bass.ds(n * 512, 512)],
                         slot(raw, i % 2, 512))
            with sp.Fori(0, FB) as f:
                with sp.Fori(0, FT) as j:
                    for i, w in enumerate((wg_v, wu_v)):
                        load(U_FF + i + f * FB_UNITS + j * 2, i, w[:, :, bass.ds(f * (FT * P) + j * P, P)],
                             slot(raw, i, P))
                with sp.Fori(0, 2) as n:
                    for u in range(6):
                        i, e = u // 3, u % 3
                        load(U_FF + 2 * FT + u + f * FB_UNITS + n * 6, u % 2,
                             wd_v[:, bass.ds(f * FT + 4 * e, DK[e]), bass.ds(n * 1024 + i * 512, 512)],
                             slot(raw, u % 2, 512)[:, 0:DK[e]])
            sp.wait_ge(out_st, 16 * TT)

        @block.gpsimd
        def _(pool):
            own = Chain(pool, pool_own)
            for i, v in enumerate((lam_re, lam_im)):
                pool.dma_start(lam[:, i], v[0].rearrange("(h g) p -> g h p", h=2)).then_inc(dt_here, 16)
            with nc.allow_non_contiguous_dma(reason="64 step sizes"):
                pool.dma_start(dt_r[:, :], log_dt[0].rearrange("(h g) -> g h", h=2)).then_inc(dt_here, 16)
            for r0, v, n in ((0, norm1_g[0], KT), (16, norm2_g[0], KT),
                             (32, d_skip[0].rearrange("g c -> (g c)"), HT), (40, b_glu[0], HT)):
                pool.dma_start(vec_raw[r0:r0 + n, :], v.rearrange("(k p) -> k p", p=P)).then_inc(const_here, 16)
            pool.dma_start(ident[:, :], ident_c[:, :]).then_inc(const_here, 16)
            pool.dma_start(sink_raw[:, :], sinks[0].partition_broadcast(P)).then_inc(const_here, 16)
            for i, w in enumerate((b_re, b_im)):
                pool.dma_start(par[:, i], w[0].rearrange("(h g) p c -> g h (p c)", h=2)).then_inc(par_here, 16)
            for i, w in enumerate((c_re, c_im)):
                for h in range(2):
                    pool.dma_start(par[:, 2 + i].rearrange("g a (c h p) -> g (a c) h p", h=2, p=NS)[:, :, h],
                                   w[0, GP * h:GP * h + GP]).then_inc(par_here, 16)
            pool.wait_ge(par_out, 4)
            pool.memset(k_row[:, :, 0:7 * GC], 0.0).then_inc(krow_zero, 1)

            with pool.Fori(0, NBLK) as b:
                for i in range(2):
                    pool.wait_ge(read_out, 4 * b + (i + 3))
                    apart(pool)
                    pool.dma_start(u_s[b, i * P:(i + 1) * P], u_p[:, i]).then_inc(u_stored, 16)
                pool.wait_ge(u_stored, 32 * b + 32)
                pool.wait_ge(units_done, 4 * b + 2)
                apart(pool)
                for r in range(L):
                    pool.dma_start(u2[16 * r:16 * r + 16, :, :],
                                   u_s[b, :, L - 1 - r, :].rearrange("(j c) m -> c j m", c=GC)).then_inc(u2_here, 16)
                pool.wait_ge(tab_c, b + 1)
                apart(pool)
                pool.dma_start(cout_s[b].rearrange("p r g (l c) -> p (r g) (l c)", c=GC),
                               cout[:, :, :, 1:, :].rearrange("p r g l c -> p (r g) (l c)")).then_inc(tab_stored, 16)
                pool.wait_ge(krow_ready, 2 * b + 2)
                apart(pool)
                for h in range(2):
                    pool.dma_start(kp_s[b, :, h], k_row[16 * h:16 * h + 16]).then_inc(tab_stored, 16)

            pool.wait_ge(state_in, 2 * NBLK)
            pool.wait_ge(powers_ready, 1)
            with pool.Fori(0, M - 1) as m:
                own.enter(m, 3)
                prev, cur = state[:, m], state[:, m + 1]
                pool.tensor_tensor(sc_t[:, 0], prev, ar8[:, :, :], ALU.mult)
                own(pool.tensor_tensor(sc_t[:, 1], prev, ai8[:, :, :], ALU.mult))
                own(pool.tensor_tensor(sc_t[:, 0], sc_t[:, 0], sc_t[:, 1, ::-1, :], ALU.add))
                apart(pool)
                own(pool.tensor_tensor(cur, cur, sc_t[:, 0], ALU.add))
                apart(pool)
                own.leave(M - 1, 3)
            own(pool.memset(st_c[:, :, :, 0:1], 0.0))
            pool.wait_ge(tab_stored, 16 * 3 * NBLK)
            with pool.Fori(0, NBLK) as b:
                pool.wait_ge(units_done, 4 * b + (2 + U_GATE + 12))
                apart(pool)
                pool.dma_start(cy[:, :, :, :], cout_s[b]).then_inc(ytab_here, 16)
                for r in range(L):
                    pool.dma_start(toe[16 * r:16 * r + 16],
                                   kp_s[b, :, :, :, 16 * r:16 * r + P].rearrange("c h g w -> c (h g) w")
                                   ).then_inc(ytab_here, 16)
                    pool.dma_start(u2y[16 * r:16 * r + 16, :, :],
                                   u_s[b, :, L - 1 - r, :].rearrange("(j c) m -> c j m", c=GC)).then_inc(ytab_here, 16)
                for r in range(2):
                    pool.tensor_copy(st_c[:, r, :, 1:M],
                                     state[:, 0:M - 1, r, bass.ds(b * GB, GB)].rearrange("p m g -> p g m")
                                     ).then_inc(st_staged, 1)
                pool.wait_ge(y_stored, 128 * b + 128)

            pool.wait_ge(units_done, 2 + U_GLU)
            for n in range(HT):
                if n >= 2:
                    pool.wait_ge(zz_ready, n - 1)
                h, b = n // NBLK, n % NBLK
                pool.dma_start(y_in[:, n % 2, :], y_s[b, h * P:(h + 1) * P].rearrange("c t m -> c (t m)")
                               ).then_inc(yin_here[n % 2], 16)
                pool.dma_start(u_in[:, n % 2, :], u_s[b, h * P:(h + 1) * P].rearrange("c t m -> c (t m)")
                               ).then_inc(yin_here[n % 2], 16)
            pool.wait_ge(zz_ready, HT)
            for i in range(2):
                pool.wait_ge(gate_st[i], 16 * 16)
            for i in range(2):
                for e in range(2):
                    pool.dma_start(gate_in[:, i, e, :], gate_s[16 * e + i]).then_inc(gin_here[i], 16)
            with pool.Fori(1, 8) as j:
                for i in range(2):
                    pool.wait_ge(mrg_ready, 2 * j + i - 1)
                    apart(pool)
                    for e in range(2):
                        pool.dma_start(gate_in[:, i, e, :], gate_s[2 * j + (16 * e + i)]).then_inc(gin_here[i], 16)
            pool.wait_ge(units_done, 2 + U_O)
            pool.dma_start(x1[:, :, :], x_v).then_inc(xres_here, 16)
            pool.wait_ge(mlo_ready, KT)
            pool.dma_start(normf[:, :], normf_g.partition_broadcast(P)).then_inc(normf_here, 16)

        @block.scalar
        def _(act):
            run = nc.scalar.activation

            def hi(q, p, here, n=UNIT):
                act.wait_ge(raw_here[p], here)
                act.wait_ge(units_done, 2 * q + (p + 1))
                run(w_hi[:, p, 0:n], raw[:, p, 0:n], ACT.Copy).then_inc(hi_ready, 1)

            def unit_done(q, p):
                act.wait_ge(units_done, 2 * q + (p + 3))

            def norm(src, dst, g0, c):
                for t in range(TT):
                    if c == 0:
                        act.wait_ge(x_here[t], 16)
                    run(act_lo[:, 4 * t:4 * t + 4, :].rearrange("p k n -> p (k n)"), src[:, t, :], ACT.Square,
                        accum_out=stat[:, 0, t:t + 1]).then_inc(ssq_ready, 1)
                roots(c)
                for t in (0, 1):
                    run(dst[:, t, :], src[:, t, :], ACT.Copy, scale=stat[:, 3, t:t + 1]).then_inc(xn_ready, 1)
                for k in range(KT):
                    act.wait_ge(tr_done, c * KT + k + 1)
                    run(act_hi[:, k, :], bank[k % 8][:, :], ACT.Copy, scale=vec_t[:, g0 + k:g0 + k + 1]
                        ).then_inc(nhi_ready, 1)

            def roots(c):
                act.wait_ge(var_ready, c + 1)
                run(stat[:, 2, :], stat[:, 1, :], ACT.Sqrt).then_inc(root_ready, 1)
                act.wait_ge(rstd_ready, c + 1)

            act.wait_ge(dt_here, 48)
            run(dt_r[:, :], dt_r[:, :], ACT.Exp).then_inc(dt_exp, 1)
            act.wait_ge(mag_arg, 1)
            run(lam[:, 2], lam[:, 2], ACT.Exp).then_inc(mag_ready, 1)
            act.wait_ge(ang_ready, 1)
            run(lam[:, 5], lam[:, 4], ACT.Sin, scale=0.5)
            run(lam[:, 6], lam[:, 4], ACT.Sin).then_inc(sin_ready, 1)
            act.wait_ge(vec_ready, 1)
            run(b_half[:, :], vec_t[:, 40:48], ACT.Copy, scale=0.5).then_inc(read_out, 2)
            norm(xt, xt, 0, 0)

            hi(0, 0, arrived(0, 0))

            def mixer_inputs(b, first):
                def step(i):
                    hi(2 * b + (i + 1) // 2, (i + 1) % 2, arrived(2 * b + (i + 1) // 2, 0))
                    unit_done(2 * b + i // 2, i % 2)

                for i in range(2):
                    step(i)
                    run(u_p[:, i].rearrange("p s m -> p m s"), bank[i][:, :].rearrange("p (m s) -> p m s", s=L),
                        ACT.Copy).then_inc(read_out, 1)
                for e in range(4):
                    act.wait_ge(bint_done, 4 * b + (e + 1))
                    run(bin_t[:, e // 2, 4 * (e % 2):4 * (e % 2) + 4, :],
                        bank[2 + e][:, :].rearrange("p (g w) -> p g w", w=P), ACT.Copy).then_inc(bint_ready, 1)
                act.wait_ge(k_done, b + 1)
                if first:
                    act.wait_ge(krow_zero, 1)
                else:
                    act.wait_ge(tab_stored, 48 * b)
                for e in range(2):
                    run(k_row[:, 4 * e:4 * e + 4, 7 * GC:], bank[6 + e][0:GP, :].rearrange("p (g w) -> p g w", w=P),
                        ACT.Copy).then_inc(krow_ready, 1)
                step(2)
                run(q_t[:, 2 * b, :], bank[0][:, :], ACT.Copy).then_inc(read_out, 1)
                act.wait_ge(x_done, b + 1)
                for r in range(2):
                    run(state[:, :, r, bass.ds(b * GB, GB)].rearrange("p m g -> p g m"),
                        bank[2 + r][:, :].rearrange("p (g m) -> p g m", m=M), ACT.Copy).then_inc(state_in, 1)
                step(3)
                run(q_t[:, 2 * b + 1, :], bank[1][:, :], ACT.Copy).then_inc(read_out, 1)

            mixer_inputs(0, True)
            with act.Fori(1, NBLK) as b:
                mixer_inputs(b, False)

            hi(8, 1, arrived(8, 1))
            unit_done(8, 0)
            act.wait_ge(pads, 1)
            run(k_pad[0:64, 0, CH:], bank[0][0:64, :], ACT.Copy).then_inc(kv_ev, 1)
            run(k_pad[64:P, 1, CH:], bank[0][64:P, :], ACT.Copy).then_inc(read_out, 1)
            act.wait_ge(kv_ev, 1)
            act.wait_ge(read_out, U_KV + 3)
            act.dma_start(k_pad[64:P, 0, CH:], k_pad[0:64, 0, CH:]).then_inc(kv_dup, 16)
            act.dma_start(k_pad[0:64, 1, CH:], k_pad[64:P, 1, CH:]).then_inc(kv_dup, 16)
            act.dma_start(bias[:, :, :], alibi_c[:, :, :]).then_inc(bias_here, 16)
            hi(9, 0, arrived(9, 0))
            unit_done(8, 1)
            run(v_t[:, CH:], bank[1][:, :], ACT.Copy).then_inc(read_out, 1)

            def gates(n, first=False, y=None):
                q0 = 2 * n + U_GATE // 2

                def gate(i):
                    hi(q0 + (i + 1) // 2, (i + 1) % 2, arrived(q0 + (i + 1) // 2, 0))
                    unit_done(q0 + i // 2, i % 2)
                    if not (first and i < 2):
                        act.wait_ge(gate_st[i % 2], 32 * n + 16 * (i // 2))
                    run(gate_o[:, i % 2, :], bank[i % 2][:, :], ACT.Tanh, scale=0.5).then_inc(read_out, 1)
                    act.wait_ge(read_out, 4 * n + (U_GATE + i + 3))
                    act.dma_start(gate_s[4 * n + i], gate_o[:, i % 2, :]).then_inc(gate_st[i % 2], 16)

                gate(0)
                act.wait_ge(scores_done, n + 1)
                run(v_c[:, :], bank[6][:, 0:P], ACT.Copy).then_inc(vc_ready, 1)
                act.wait_ge(neg_ready, n + 1)
                for j in range(PAIRS):
                    run(prob[:, j, :], score[:, j, :], ACT.Exp, bias=neg_max[:, j:j + 1], accum_out=den[:, j:j + 1])
                run(sink_e[:, :], sink_e[:, :], ACT.Exp).then_inc(exps, 1)
                gate(1)
                if y is not None:
                    y_part(y, 0)
                gate(2)
                for e in range(2):
                    act.wait_ge(pt_done, 2 * n + (e + 1))
                    run(prob_t[:, 4 * e:4 * e + 4, :], bank[4 + e][:, :].rearrange("p (j w) -> p j w", w=P), ACT.Copy
                        ).then_inc(pt_ready, 1)
                if y is not None:
                    y_part(y, 1)
                    act.wait_ge(y_ev, 2 * y + 2)
                    for t in range(L):
                        act.dma_start(y_s[y, :, t, :].rearrange("(j c) m -> c j m", c=GC),
                                      y_sb[16 * t:16 * t + 16].rearrange("p h g m -> p (h g) m")
                                      ).then_inc(y_stored, 16)
                gate(3)

            def y_part(b, h):
                act.wait_ge(y_done, 2 * b + (h + 1))
                run(y_sb[:, h], bank[7][:, :].rearrange("p (g m) -> p g m", m=M), ACT.Copy).then_inc(y_ev, 1)

            gates(0, first=True)
            with act.Fori(1, 4) as n:
                gates(n)
            with act.Fori(4, 8) as n:
                gates(n, y=n - 4)

            act.wait_ge(yb_ready, NCH)
            for e in range(2):
                run(yb_hi[:, 4 * e:4 * e + 4, :], q_t[:, 4 * e:4 * e + 4, :], ACT.Copy).then_inc(ybhi_ready, 1)
            for n in range(HT + 1):
                if n < HT:
                    act.wait_ge(y_arg, n + 1)
                    run(g_v[:, n % 2, :], g_v[:, n % 2, :], ACT.Tanh, scale=GELU_C).then_inc(y_tanh, 1)
                if n > 0:
                    act.wait_ge(zz_ready, n)
                    run(act_hi[:, n - 1, :], zz[:, n - 1, :], ACT.Copy, scale=0.5).then_inc(zhi_ready, 1)
            for i in range(2):
                act.wait_ge(gate_st[i], 16 * 16)
            for i in range(4):
                u = U_GLU + i
                hi((u + 1) // 2, (u + 1) % 2, arrived((u + 1) // 2, 0) + (16 if u + 1 == U_AB else 0))
                unit_done(u // 2, u % 2)
                for e in range(2):
                    n = 2 * i + e
                    if i > 0:
                        act.wait_ge(yalo_ready, n - 1)
                    run(g_v[:, e, :], bank[2 * e + i % 2][:, :], ACT.Tanh, scale=0.5, bias=b_half[:, n:n + 1]
                        ).then_inc(read_out if e else glu_t, 1)
                for e in range(2):
                    n = 2 * i + e
                    act.wait_ge(glu_m, n + 1)
                    run(ya_hi[:, n, :], g_v[:, e, :], ACT.Copy, scale=0.25).then_inc(yahi_ready, 1)

            def merge(j, last=False):
                q = U_AB // 2 + j
                for i in range(2):
                    if i == 0:
                        hi(q, 1, 32 * j + (arrived(U_AB // 2, 1) + 16))
                    elif last:
                        hi(q + 1, 0, arrived(q + 1, 0) + 128)
                    else:
                        hi(q + 1, 0, 32 * j + (arrived(U_AB // 2, 0) + 48))
                    act.wait_ge(mrg_ready, 2 * j + (i + 1))
                    run(act_hi[:, 2 * j + i, :], mrg[:, i, :], ACT.Copy, scale=0.5).then_inc(mhi_ready, 1)

            with act.Fori(0, 7) as j:
                merge(j)
            merge(7, last=True)

            def here(q):
                return 16 * q + (16 + 128)

            with act.Fori(0, NB) as n:
                for i in range(4):
                    q = 2 * n + (U_O + i + 1) // 2
                    hi(q, (i + 1) % 2, here(q))
            act.wait_ge(tok_free, 4 + NB * TT)
            norm(x1, xn, 16, 1)

            def ff_block(f, last=False):
                q0 = f * (FB_UNITS // 2) + U_FF // 2
                with act.Fori(0, FT) as j:
                    hi(q0 + j, 1, here(q0 + j))
                    unit_done(q0 + j, 0)
                    run(ff_t[:, :], bank[0][:, :], ACT.Tanh, scale=0.5).then_inc(ff_tanh, 1)
                    hi(q0 + j + 1, 0, here(q0 + j + 1))
                    act.wait_ge(up_read, f * FT + j + 2)
                    run(m_hi[:, j, :], ff_m[:, :], ACT.Copy, scale=0.5).then_inc(ffhi_ready, 1)

                def down(n, very_last=False):
                    for u in range(6):
                        if not (very_last and u == 5):
                            q = q0 + FT + 3 * n + (u + 1) // 2
                            full = u % 3 != 1
                            hi(q, (u + 1) % 2, here(q), UNIT if full else DK[2] * 512)

                if last:
                    down(0)
                    down(1, True)
                else:
                    with act.Fori(0, 2) as n:
                        down(n)

            with act.Fori(0, FB - 1) as f:
                ff_block(f)
            ff_block(FB - 1, last=True)
            act.wait_ge(tok_free, 4 + NB * TT * (FB + 1))
            for t in range(TT):
                run(act_lo[:, 4 * t:4 * t + 4, :].rearrange("p k n -> p (k n)"), x1[:, t, :], ACT.Square,
                    accum_out=stat[:, 0, t:t + 1]).then_inc(ssq_ready, 1)
            roots(2)
            for t in range(TT):
                act.wait_ge(out_ready, t + 1)
                act.dma_start(out_v[:, t, :], x1[:, t, :]).then_inc(out_st, 16)

        @block.vector
        def _(dve):
            v = nc.vector
            own = Chain(dve, dve_own)

            def lo(u, p, n=UNIT):
                dve.wait_ge(hi_ready, u + 1)
                v.tensor_tensor(w_lo[:, p, 0:n], raw[:, p, 0:n], w_hi[:, p, 0:n].bitcast(F32), ALU.subtract
                                ).then_inc(lo_ready, 1)

            def norm(src, dst, g0, c):
                rstd(c)
                for t in (2, 3):
                    v.tensor_scalar(dst[:, t, :], src[:, t, :], stat[:, 3, t:t + 1], None, ALU.mult
                                    ).then_inc(xn_ready, 1)
                for k in range(KT):
                    dve.wait_ge(nhi_ready, c * KT + k + 1)
                    v.scalar_tensor_tensor(act_lo[:, k, :], bank[k % 8][:, :], vec_t[:, g0 + k:g0 + k + 1],
                                           act_hi[:, k, :].bitcast(F32), ALU.mult, ALU.subtract
                                           ).then_inc(nlo_ready, 1)

            def rstd(c):
                dve.wait_ge(ssq_ready, TT * (c + 1))
                v.tensor_scalar(stat[:, 1, :], stat[:, 0, :], 1.0 / D, EPS, ALU.mult, ALU.add).then_inc(var_ready, 1)
                dve.wait_ge(root_ready, c + 1)
                v.reciprocal(stat[:, 3, :], stat[:, 2, :]).then_inc(rstd_ready, 1)
                dve.wait_ge(rstd_ready, c + 1)

            dve.wait_ge(dt_here, 48)
            dve.wait_ge(dt_exp, 1)
            for h in range(2):
                v.tensor_scalar(lam[:, 3, h], lam[:, 1, h], dt_r[:, h:h + 1], None, ALU.mult)
            for h in range(2):
                ins = v.tensor_scalar(lam[:, 2, h], lam[:, 0, h], dt_r[:, h:h + 1], None, ALU.mult)
            ins.then_inc(mag_arg, 1)
            dve.wait_ge(mag_arg, 1)
            own(v.tensor_scalar(lam[:, 4], lam[:, 3], 1.0 / (2.0 * math.pi), ROUND, ALU.mult, ALU.add))
            own(v.tensor_scalar(lam[:, 7], lam[:, 4], -ROUND, None, ALU.add))
            for part in TWO_PI:
                own(v.scalar_tensor_tensor(lam[:, 3], lam[:, 7], -part, lam[:, 3], ALU.mult, ALU.add))
            v.tensor_scalar(lam[:, 4], lam[:, 3], 3.1415925, -3.1415925, ALU.min, ALU.max).then_inc(ang_ready, 1)
            dve.wait_ge(sin_ready, 1)
            dve.wait_ge(mag_ready, 1)
            own(v.tensor_tensor(lam[:, 7], lam[:, 5], lam[:, 5], ALU.mult))
            own(v.tensor_scalar(lam[:, 7], lam[:, 7], -2.0, 1.0, ALU.mult, ALU.add))
            own(v.tensor_tensor(lam[:, 8], lam[:, 2], lam[:, 7], ALU.mult))
            own(v.tensor_tensor(lam[:, 9], lam[:, 2], lam[:, 6], ALU.mult))
            own(v.tensor_scalar(lam[:, 3], lam[:, 8], -1.0, None, ALU.add))
            own(v.tensor_tensor(lam[:, 4], lam[:, 0], lam[:, 0], ALU.mult))
            own(v.tensor_tensor(lam[:, 5], lam[:, 1], lam[:, 1], ALU.mult))
            own(v.tensor_tensor(lam[:, 4], lam[:, 4], lam[:, 5], ALU.add))
            own(v.reciprocal(lam[:, 12], lam[:, 4]))
            for out_, (i0, i1), (i2, i3), op in ((10, (3, 0), (9, 1), ALU.add), (11, (9, 0), (3, 1), ALU.subtract)):
                own(v.tensor_tensor(lam[:, 5], lam[:, i0], lam[:, i1], ALU.mult))
                own(v.tensor_tensor(lam[:, 6], lam[:, i2], lam[:, i3], ALU.mult))
                own(v.tensor_tensor(lam[:, 7], lam[:, 5], lam[:, 6], op))
                ins = v.tensor_tensor(lam[:, out_], lam[:, 7], lam[:, 12], ALU.mult)
                if out_ == 10:
                    own(ins)
            ins.then_inc(af_ready, 1)
            dve.wait_ge(units_done, 2)
            v.tensor_copy(vec_t[:, :], bank[7][:, 0:48]).then_inc(vec_ready, 1)
            dve.wait_ge(const_here, 96)
            for e in range(2):
                v.tensor_copy(sink[64 * e:64 * e + 64, :], sink_raw[64 * e:64 * e + 64, e::2])
            dve.wait_ge(par_t, 1)
            for i in range(4):
                dst = (b_sb if i < 2 else c_sb)[:, i % 2]
                v.tensor_copy(dst.rearrange("p g c -> p c g"), bank[i][:, :].rearrange("p (c g) -> p c g", g=GP)
                              ).then_inc(par_out, 1)
            dve.wait_ge(vec_ready, 1)
            norm(xt, xt, 0, 0)
            lo(0, 0)

            dve.wait_ge(par_t, 2)
            own(v.tensor_copy(ab_f[:, :, :], bank[2][:, 0:4 * GP].rearrange("p (k g) -> p k g", g=GP)))
            v.memset(powers[:, 0, 0, :], 1.0)
            v.memset(powers[:, 0, 1, :], 0.0)
            own(v.tensor_copy(powers[:, 1], ab_f[:, 0:2, :]))

            def times(dst, n, xs, ys):
                def part(x0, r):
                    return powers[:, x0:x0 + n, r, :]

                def one(r):
                    return powers[:, ys:ys + 1, r, :].to_broadcast([P, n, GP])

                t = p_tmp[:, 0:n, :]
                own(v.tensor_tensor(t, part(xs, 1), one(1), ALU.mult))
                own(v.tensor_tensor(part(dst, 0), part(xs, 0), one(0), ALU.mult))
                own(v.tensor_tensor(part(dst, 0), part(dst, 0), t, ALU.subtract))
                own(v.tensor_tensor(t, part(xs, 1), one(0), ALU.mult))
                own(v.tensor_tensor(part(dst, 1), part(xs, 0), one(1), ALU.mult))
                own(v.tensor_tensor(part(dst, 1), part(dst, 1), t, ALU.add))

            times(2, 1, 1, 1)
            times(3, 2, 1, 2)
            times(5, 4, 1, 4)
            for r in range(2):
                v.tensor_copy(ar8[:, r], powers[:, L, 0, :])
            v.tensor_scalar(ai8[:, 1], powers[:, L, 1, :], -1.0, None, ALU.mult)
            v.tensor_copy(ai8[:, 0], powers[:, L, 1, :]).then_inc(powers_ready, 1)
            bshape = [P, GP, GC]
            f_re = ab_f[:, 2, :].unsqueeze(2).to_broadcast(bshape)
            f_im = ab_f[:, 3, :].unsqueeze(2).to_broadcast(bshape)
            t0 = tmp[:, 0:GP * GC].rearrange("p (g c) -> p g c", c=GC)
            t1 = tmp[:, GP * GC:2 * GP * GC].rearrange("p (g c) -> p g c", c=GC)
            own(v.tensor_tensor(t0, b_sb[:, 0], f_im, ALU.mult))
            own(v.tensor_tensor(b_sb[:, 0], b_sb[:, 0], f_re, ALU.mult))
            own(v.tensor_tensor(t1, b_sb[:, 1], f_im, ALU.mult))
            own(v.tensor_tensor(b_sb[:, 0], b_sb[:, 0], t1, ALU.subtract))
            own(v.tensor_tensor(b_sb[:, 1], b_sb[:, 1], f_re, ALU.mult))
            own(v.tensor_tensor(b_sb[:, 1], b_sb[:, 1], t0, ALU.add))
            own(v.memset(bb_pad[:, :, :, :], 0.0))

            def tables(b, first):
                def blk(tile, r):
                    return tile[:, r, bass.ds(b * GB, GB), :]

                def pw(r, l0, n):
                    return powers[:, l0:l0 + n, r, bass.ds(b * GB, GB)].rearrange("p l g -> p g l")

                def product(out_, a, ar, pr, n, l0):
                    shape = [P, GB, n, GC]
                    return v.tensor_tensor(out_, blk(a, ar).unsqueeze(2).to_broadcast(shape),
                                           pw(pr, l0, n).unsqueeze(3).to_broadcast(shape), ALU.mult)

                lo(4 * b + 1, 1)
                if not first:
                    dve.wait_ge(units_done, 4 * b + 2)
                    dve.wait_ge(tab_stored, 48 * b)
                    apart(dve)
                for h in range(2):
                    rows = slice(64 * h, 64 * h + 64)
                    for r in range(2):
                        v.tensor_copy(bb_pad[rows, r, :, GC * h:GC * h + GC], b_sb[rows, r, bass.ds(b * GB, GB), :])
                ct = tmp[:, :].rearrange("p (g l c) -> p g l c", l=L + 1, c=GC)
                own(product(ct, c_sb, 1, 1, L + 1, 0))
                own(product(cout[:, 0], c_sb, 0, 0, L + 1, 0))
                own(v.tensor_tensor(cout[:, 0], cout[:, 0], ct, ALU.subtract))
                own(product(ct, c_sb, 1, 0, L + 1, 0))
                own(product(cout[:, 1], c_sb, 0, 1, L + 1, 0))
                v.scalar_tensor_tensor(cout[:, 1].rearrange("p g l c -> p (g l c)"),
                                       cout[:, 1].rearrange("p g l c -> p (g l c)"), -1.0, tmp[:, :],
                                       ALU.mult, ALU.subtract).then_inc(tab_c, 1)
                lo(4 * b + 2, 0)
                bt = tmp[:, 0:GB * L * GC].rearrange("p (g l c) -> p g l c", l=L, c=GC)
                dve.wait_ge(tab_c, b + 1)
                own(product(bt, b_sb, 1, 1, L, 0))
                own(product(b_in[:, 0], b_sb, 0, 0, L, 0))
                own(v.tensor_tensor(b_in[:, 0], b_in[:, 0], bt, ALU.subtract))
                own(product(bt, b_sb, 1, 0, L, 0))
                own(product(b_in[:, 1], b_sb, 0, 1, L, 0))
                v.tensor_tensor(b_in[:, 1], b_in[:, 1], bt, ALU.add).then_inc(tab_b, 1)
                lo(4 * b + 3, 1)
                lo(4 * b + 4, 0)

            tables(0, True)
            with dve.Fori(1, NBLK) as b:
                own.enter(b - 1, 10)
                tables(b, False)
                own.leave(NBLK - 1, 10)

            lo(U_KV + 1, 1)
            dve.wait_ge(units_done, 2 + U_KV)
            dve.wait_ge(tab_stored, 16 * 3 * NBLK)
            v.memset(v_t[:, 0:CH], 0.0)
            v.memset(k_pad[:, :, 0:CH], 0.0).then_inc(pads, 1)
            lo(U_KV + 2, 0)
            dve.wait_ge(bias_here, 16)
            dve.wait_ge(kv_dup, 32)
            dve.wait_ge(read_out, U_GATE + 2)

            def attend(n, first=False):
                u0 = 4 * n + U_GATE
                v.tensor_scalar(q_c[:, :, :], q_t[:, :, bass.ds(n * CH, CH)], HD ** -0.5, None, ALU.mult)
                v.tensor_copy(k_c[:, :, :], k_pad[:, :, bass.ds(n * CH, KEYS)])
                v.tensor_copy(v_ct[:, :], v_t[:, bass.ds(n * CH, KEYS)]).then_inc(staged, 1)
                lo(u0 + 1, 1)
                dve.wait_ge(scores_done, n + 1)
                for e in range(2):
                    own(v.tensor_tensor(score[:, 4 * e:4 * e + 4, :],
                                        bank[2 + e][:, :].rearrange("p (j w) -> p j w", w=KEYS),
                                        bias[:, 4 * e:4 * e + 4, :], ALU.add))
                if first:
                    own(v.memset(score[:, :, 0:CH], NEG))
                own(v.tensor_reduce(row_max[:, :], score[:, :, :], AX.X, ALU.max))
                own(v.tensor_tensor(row_max[:, :], row_max[:, :], sink[:, :], ALU.max))
                own(v.tensor_tensor(sink_e[:, :], sink[:, :], row_max[:, :], ALU.subtract))
                v.tensor_scalar(neg_max[:, :], row_max[:, :], -1.0, None, ALU.mult).then_inc(neg_ready, 1)
                lo(u0 + 2, 0)
                dve.wait_ge(exps, n + 1)
                own(v.tensor_tensor(den[:, :], den[:, :], sink_e[:, :], ALU.add))
                own(v.reciprocal(den[:, :], den[:, :]))
                v.tensor_tensor(prob[:, :, :], prob[:, :, :], den[:, :].unsqueeze(2).to_broadcast([P, PAIRS, KEYS]),
                                ALU.mult).then_inc(prob_ready, 1)
                lo(u0 + 3, 1)
                lo(u0 + 4, 0)
                dve.wait_ge(pv_done, n + 1)
                v.tensor_scalar(q_t[:, :, bass.ds(n * CH, CH)], bank[6][:, :].rearrange("p (j w) -> p j w", w=CH),
                                1.0, None, ALU.mult).then_inc(yb_ready, 1)

            attend(0, True)
            with dve.Fori(1, NCH) as n:
                own.enter(n - 1, 7)
                attend(n)
                own.leave(NCH - 1, 7)

            for e in range(2):
                dve.wait_ge(ybhi_ready, e + 1)
                part = slice(4 * e, 4 * e + 4)
                v.tensor_tensor(yb_lo[:, part, :], q_t[:, part, :], yb_hi[:, part, :].bitcast(F32), ALU.subtract
                                ).then_inc(yblo_ready, 1)
            for n in range(HT + 2):
                if n < HT:
                    i = n % 2
                    dve.wait_ge(yin_here[i], 32 * (n // 2 + 1))
                    own(v.scalar_tensor_tensor(y_in[:, i, :], u_in[:, i, :], vec_t[:, 32 + n:33 + n], y_in[:, i, :],
                                               ALU.mult, ALU.add))
                    own(v.tensor_tensor(g_v[:, i, :], y_in[:, i, :], y_in[:, i, :], ALU.mult))
                    own(v.tensor_scalar(g_v[:, i, :], g_v[:, i, :], 0.044715, 1.0, ALU.mult, ALU.add))
                    v.tensor_tensor(g_v[:, i, :], g_v[:, i, :], y_in[:, i, :], ALU.mult).then_inc(y_arg, 1)
                if 1 <= n <= HT:
                    i = (n - 1) % 2
                    dve.wait_ge(y_tanh, n)
                    v.scalar_tensor_tensor(zz[:, n - 1, :].rearrange("p (m t) -> p t m", t=L),
                                           g_v[:, i, :].rearrange("p (t m) -> p t m", t=L), 1.0,
                                           y_in[:, i, :].rearrange("p (t m) -> p t m", t=L), ALU.add, ALU.mult
                                           ).then_inc(zz_ready, 1)
                if n >= 2:
                    dve.wait_ge(zhi_ready, n - 1)
                    v.scalar_tensor_tensor(act_lo[:, n - 2, :], zz[:, n - 2, :], 0.5,
                                           act_hi[:, n - 2, :].bitcast(F32), ALU.mult, ALU.subtract
                                           ).then_inc(zlo_ready, 1)
            for i in range(2):
                dve.wait_ge(gate_st[i], 16 * 16)
            for i in range(4):
                u = U_GLU + i
                lo(u + 1, (u + 1) % 2)
                for e in range(2):
                    n = 2 * i + e
                    if e == 0:
                        dve.wait_ge(glu_t, i + 1)
                    else:
                        dve.wait_ge(read_out, u + 3)
                    v.scalar_tensor_tensor(g_v[:, e, :], g_v[:, e, :], 1.0, zz[:, n, :], ALU.add, ALU.mult
                                           ).then_inc(glu_m, 1)
                for e in range(2):
                    n = 2 * i + e
                    dve.wait_ge(yahi_ready, n + 1)
                    v.scalar_tensor_tensor(ya_lo[:, n, :], g_v[:, e, :], 0.25, ya_hi[:, n, :].bitcast(F32),
                                           ALU.mult, ALU.subtract).then_inc(yalo_ready, 1)
            with dve.Fori(0, 8) as j:
                own.enter(j, 2)
                for i in range(2):
                    u = 2 * j + (U_AB + i)
                    lo(u + 1, (i + 1) % 2)
                    dve.wait_ge(gin_here[i], 32 * j + 32)
                    dve.wait_ge(units_done, u + 3)
                    own(v.scalar_tensor_tensor(mrg[:, i, :], gate_in[:, i, 0, :], 1.0, bank[i][:, :],
                                               ALU.add, ALU.mult))
                    v.scalar_tensor_tensor(gate_in[:, i, 1, :], gate_in[:, i, 1, :], 1.0, bank[2 + i][:, :],
                                           ALU.add, ALU.mult).then_inc(read_out, 1)
                    dve.wait_ge(read_out, u + 3)
                    v.tensor_tensor(mrg[:, i, :], mrg[:, i, :], gate_in[:, i, 1, :], ALU.add).then_inc(mrg_ready, 1)
                    dve.wait_ge(mhi_ready, 2 * j + (i + 1))
                    v.scalar_tensor_tensor(act_lo[:, 2 * j + i, :], mrg[:, i, :], 0.5,
                                           act_hi[:, 2 * j + i, :].bitcast(F32), ALU.mult, ALU.subtract
                                           ).then_inc(mlo_ready, 1)
                own.leave(8, 2)

            def add_up(n, w, done):
                for t in range(TT):
                    if t < TT - 1:
                        dve.wait_ge(tok_done, 3 * done + (t + 1))
                    else:
                        dve.wait_ge(units_done, w)
                    cols = bass.ds(n * 512, 512)
                    v.tensor_tensor(x1[:, t, cols], x1[:, t, cols], bank[4 + t][:, :], ALU.add).then_inc(tok_free, 1)

            v.memset(stat[:, 2, :], 0.0).then_inc(tok_free, 4)
            dve.wait_ge(xres_here, 16)
            with dve.Fori(0, NB) as n:
                for i in range(4):
                    lo(4 * n + (U_O + i + 1), (i + 1) % 2)
                add_up(n, 4 * n + (U_O + 4 + 2), n)
            dve.wait_ge(tok_free, 4 + NB * TT)
            norm(x1, xn, 16, 1)
            v.memset(stat[:, 0, :], 0.0).then_inc(ff_read, 1)
            v.memset(stat[:, 1, :], 0.0).then_inc(up_read, 1)

            def ff_block(f, last=False):
                u0 = f * FB_UNITS + U_FF
                with dve.Fori(0, FT) as j:
                    t = f * FT + j
                    lo(2 * j + u0 + 1, 1)
                    dve.wait_ge(ff_tanh, t + 1)
                    v.scalar_tensor_tensor(ff_m[:, :], ff_t[:, :], 1.0, bank[0][:, :], ALU.add, ALU.mult
                                           ).then_inc(ff_read, 1)
                    lo(2 * j + u0 + 2, 0)
                    dve.wait_ge(units_done, 2 * j + u0 + 4)
                    dve.wait_ge(ff_read, t + 2)
                    v.tensor_tensor(ff_m[:, :], ff_m[:, :], bank[1][:, :], ALU.mult).then_inc(up_read, 1)
                    dve.wait_ge(up_read, t + 2)
                    dve.wait_ge(ffhi_ready, t + 1)
                    v.scalar_tensor_tensor(m_lo[:, j, :], ff_m[:, :], 0.5, m_hi[:, j, :].bitcast(F32),
                                           ALU.mult, ALU.subtract).then_inc(fflo_ready, 1)
                    dve.wait_ge(fflo_ready, t + 1)

                def down(n, very_last=False):
                    for i in range(2):
                        for e in range(3):
                            x_ = 3 * i + e
                            if not (very_last and x_ == 5):
                                lo(6 * n + (x_ + 1) + u0 + 2 * FT, (x_ + 1) % 2, DK[2] * 512 if e == 1 else UNIT)
                        add_up(2 * n + i, 6 * n + (3 * i + 3 + 2) + u0 + 2 * FT, f * NB + 2 * n + (i + NB))

                if last:
                    down(0)
                    down(1, True)
                else:
                    with dve.Fori(0, 2) as n:
                        down(n)

            with dve.Fori(0, FB - 1) as f:
                ff_block(f)
            ff_block(FB - 1, last=True)
            dve.wait_ge(normf_here, 16)
            rstd(2)
            for t in range(TT):
                v.scalar_tensor_tensor(x1[:, t, :], x1[:, t, :], stat[:, 3, t:t + 1], normf[:, :], ALU.mult, ALU.mult
                                       ).then_inc(out_ready, 1)

        @block.tensor
        def _(pe):
            mm = nc.tensor.matmul

            def three(out_, a_hi, a_lo, b_hi, b_lo, first, last):
                mm(out_, a_hi, b_hi, start=first, stop=False)
                mm(out_, a_hi, b_lo, start=False, stop=False)
                return mm(out_, a_lo, b_hi, start=False, stop=last)

            def unit_here(u):
                pe.wait_ge(lo_ready, u + 1)

            def tile_unit(u, p, out_):
                unit_here(u)
                for k in range(KT):
                    ins = three(out_, slot(w_hi, p, P)[:, k], slot(w_lo, p, P)[:, k], act_hi[:, k], act_lo[:, k],
                                k == 0, k == KT - 1)
                ins.then_inc(units_done, 1)

            def in_unit(u, p):
                pe.wait_ge(read_out, u + 1)
                tile_unit(u, p, bank[p][:, :])

            def norm(src, c):
                pe.wait_ge(xn_ready, TT * (c + 1))
                for k in range(KT):
                    if k >= 8:
                        pe.wait_ge(nlo_ready, c * KT + k - 7)
                    elif c == 0 and k < 4:
                        pe.wait_ge(par_out, k + 1)
                    for t in range(TT):
                        ins = nc.tensor.transpose(bank[k % 8][:, t * P:(t + 1) * P], src[:, t, k * P:(k + 1) * P],
                                                  ident[:, :])
                    ins.then_inc(tr_done, 1)

            pe.wait_ge(const_here, 96)
            nc.tensor.transpose(bank[7][:, 0:48], vec_raw[:, :], ident[0:48, 0:48]).then_inc(units_done, 2)
            pe.wait_ge(par_here, 96)
            for i in range(4):
                for c in range(GC):
                    if i < 2:
                        src = par[:, i].rearrange("g h (p c) -> g (h p) c", c=GC)[:, :, c]
                    else:
                        src = par[:, i].rearrange("g a n -> g (a n)")[:, c * P:(c + 1) * P]
                    ins = nc.tensor.transpose(bank[i][:, c * GP:(c + 1) * GP], src, ident[0:GP, 0:GP])
            ins.then_inc(par_t, 1)
            pe.wait_ge(vec_ready, 1)
            norm(xt, 0)
            pe.wait_ge(af_ready, 1)
            pe.wait_ge(nlo_ready, KT)
            for i in range(4):
                ins = nc.tensor.transpose(bank[2][:, i * GP:(i + 1) * GP],
                                          lam[:, 8 + i].rearrange("g h p -> g (h p)"), ident[0:GP, 0:GP])
            ins.then_inc(par_t, 1)

            with pe.Fori(0, NBLK) as b:
                for i in range(2):
                    in_unit(4 * b + i, i)
                pe.wait_ge(tab_b, b + 1)
                for e in range(4):
                    for g in range(4):
                        ins = nc.tensor.transpose(bank[2 + e][:, g * P:(g + 1) * P],
                                                  b_in[:, e // 2, 4 * (e % 2) + g].rearrange("p l c -> p (l c)"),
                                                  ident[:, :])
                    ins.then_inc(bint_done, 1)
                for g in range(GB):
                    for r in range(2):
                        ins = mm(bank[6 + g // 4][0:GP, (g % 4) * P:(g % 4 + 1) * P], bb_pad[:, r, g, :],
                                 cout[:, r, g, 0:L, :].rearrange("p l c -> p (l c)"), start=r == 0, stop=r == 1)
                ins.then_inc(k_done, 1)
                in_unit(4 * b + 2, 0)
                pe.wait_ge(bint_ready, 4 * b + 4)
                pe.wait_ge(u2_here, 128 * b + 128)
                for h in range(2):
                    for g in range(GB):
                        for r in range(2):
                            ins = mm(bank[2 + r][64 * h:64 * h + 64, g * M:(g + 1) * M],
                                     bin_t[:, r, g, 64 * h:64 * h + 64], u2[:, GB * h + g, :], start=True, stop=True)
                ins.then_inc(x_done, 1)
                in_unit(4 * b + 3, 1)

            in_unit(U_KV, 0)
            in_unit(U_KV + 1, 1)

            def gates(n, y=None):
                u0 = 4 * n + U_GATE
                in_unit(u0, 0)
                pe.wait_ge(staged, n + 1)
                nc.tensor.transpose(bank[6][:, 0:P], v_ct[:, :], ident[:, :])
                for j in range(PAIRS):
                    for e in range(2):
                        rows = slice(64 * e, 64 * e + 64)
                        ins = mm(bank[2 + j // 4][rows, (j % 4) * KEYS:(j % 4 + 1) * KEYS], q_c[rows, j, :],
                                 k_c[rows, j // 4, :], start=True, stop=True)
                ins.then_inc(scores_done, 1)
                in_unit(u0 + 1, 1)
                if y is not None:
                    y_part(y, 0)
                in_unit(u0 + 2, 0)
                pe.wait_ge(prob_ready, n + 1)
                for j in range(PAIRS):
                    ins = nc.tensor.transpose(bank[4 + j // 4][:, (j % 4) * P:(j % 4 + 1) * P], prob[:, j, :],
                                              ident[:, :])
                    if j % 4 == 3:
                        ins.then_inc(pt_done, 1)
                if y is not None:
                    y_part(y, 1)
                in_unit(u0 + 3, 1)
                pe.wait_ge(pt_ready, 2 * n + 2)
                pe.wait_ge(vc_ready, n + 1)
                for kv in range(2):
                    for e in range(2):
                        ins = mm(bank[6][64 * e:64 * e + 64, 256 * kv:256 * kv + 256], v_c[:, 64 * kv:64 * kv + 64],
                                 prob_t[:, 4 * kv:4 * kv + 4, 64 * e:64 * e + 64], start=True, stop=True)
                ins.then_inc(pv_done, 1)

            def y_part(b, h):
                if h == 0:
                    pe.wait_ge(ytab_here, 16 * 17 * b + 16 * 17)
                    pe.wait_ge(st_staged, 2 * b + 2)
                else:
                    pe.wait_ge(y_ev, 2 * b + 1)
                rows = slice(64 * h, 64 * h + 64)
                for g in range(GB):
                    o = bank[7][:, g * M:(g + 1) * M]
                    mm(o, toe[:, GB * h + g, :], u2y[:, GB * h + g, :], start=True, stop=False)
                    mm(o, cy[rows, 0, g, :], st_c[rows, 0, g, :], start=False, stop=False)
                    ins = mm(o, cy[rows, 1, g, :], st_c[rows, 1, g, :], start=False, stop=True)
                ins.then_inc(y_done, 1)

            with pe.Fori(0, 4) as n:
                gates(n)
            with pe.Fori(4, 8) as n:
                gates(n, y=n - 4)

            for i in range(4):
                u, p = U_GLU + i, i % 2
                unit_here(u)
                pe.wait_ge(read_out, u + 1)
                for k in range(HT):
                    if i == 0:
                        pe.wait_ge(zlo_ready, k + 1)
                    for e in range(2):
                        cols = slice(e * P, (e + 1) * P)
                        ins = three(bank[2 * e + p][:, :], slot(w_hi, p, 256)[:, k, cols],
                                    slot(w_lo, p, 256)[:, k, cols], act_hi[:, k], act_lo[:, k], k == 0, k == HT - 1)
                ins.then_inc(units_done, 1)
            pe.wait_ge(yblo_ready, 2)
            with pe.Fori(0, 8) as j:
                for i in range(2):
                    u = 2 * j + (U_AB + i)
                    unit_here(u)
                    pe.wait_ge(read_out, u + 1)
                    for e, (a_hi, a_lo) in ((1, (yb_hi, yb_lo)), (0, (ya_hi, ya_lo))):
                        if e == 0:
                            pe.wait_ge(yalo_ready, HT)
                        for k in range(HT):
                            ins = three(bank[2 * e + i][:, :], slot(w_hi, i, P)[:, HT * e + k],
                                        slot(w_lo, i, P)[:, HT * e + k], a_hi[:, k], a_lo[:, k], k == 0, k == HT - 1)
                    ins.then_inc(units_done, 1)

            def tok_unit(u, p, kt0, kn, s_hi, s_lo, first, last, w):
                unit_here(u)
                for t in range(TT):
                    if first:
                        pe.wait_ge(tok_free, w + (t + 1))
                    for k in range(kn):
                        toks = slice(t * P, (t + 1) * P)
                        ins = three(bank[4 + t][:, :], s_hi[:, kt0 + k, toks], s_lo[:, kt0 + k, toks],
                                    slot(w_hi, p, 512)[:, k], slot(w_lo, p, 512)[:, k],
                                    first and k == 0, last and k == kn - 1)
                    if t == TT - 1:
                        ins.then_inc(units_done, 1)
                    elif last:
                        ins.then_inc(tok_done, 1)

            with pe.Fori(0, NB) as n:
                for i in range(4):
                    pe.wait_ge(mlo_ready, 4 * i + 4)
                    tok_unit(4 * n + (U_O + i), i % 2, 4 * i, 4, act_hi, act_lo, i == 0, i == 3, 4 * n)
            norm(xn, 1)
            pe.wait_ge(nlo_ready, 2 * KT)
            with pe.Fori(0, FB) as f:
                u0 = f * FB_UNITS + U_FF
                with pe.Fori(0, FT) as j:
                    pe.wait_ge(ff_read, f * FT + j + 1)
                    tile_unit(2 * j + u0, 0, bank[0][:, :])
                    pe.wait_ge(up_read, f * FT + j + 1)
                    tile_unit(2 * j + u0 + 1, 1, bank[1][:, :])
                with pe.Fori(0, 2) as n:
                    for i in range(2):
                        for e in range(3):
                            x_ = 3 * i + e
                            pe.wait_ge(fflo_ready, f * FT + min(4 * e + 4, FT))
                            tok_unit(6 * n + x_ + u0 + 2 * FT, x_ % 2, 4 * e, DK[e], m_hi, m_lo, e == 0, e == 2,
                                     TT * NB + f * (TT * NB) + n * (2 * TT) + i * TT)


_INS = ["x", "norm1_g", "w_in", "lam_re", "lam_im", "log_dt", "b_re", "b_im", "c_re", "c_im", "d_skip", "w_glu",
        "b_glu", "sinks", "w_a", "w_b", "w_o", "norm2_g", "w_gate", "w_up", "w_down", "normf_g"]


def alibi():
    dist = np.abs(np.arange(CH)[:, None] + (KEYS - CH) - np.arange(KEYS)[None, :]).astype(np.float32)
    heads = 2 * PAIRS
    slopes = (2.0 ** (-8.0 * np.arange(1, heads + 1) / heads)).astype(np.float32)
    b = -(slopes.reshape(PAIRS, 2)[:, :, None, None] * dist)
    return np.ascontiguousarray(b.transpose(1, 2, 0, 3).reshape(P, PAIRS, KEYS), dtype=np.float32)


def kernel(**inputs):
    import concourse.bacc as _bacc
    from concourse.bass_utils import run_bass_kernel_spmd as _run

    nc = _bacc.Bacc("TRN2", target_bir_lowering=False, num_devices=1)
    arrays = {n: np.ascontiguousarray(inputs[n]) for n in _INS}
    arrays["ident_c"] = np.eye(P, dtype=np.float32)
    arrays["alibi_c"] = alibi()
    args = [nc.dram_tensor(n, a.shape, F32, kind="ExternalInput").ap() for n, a in arrays.items()]
    for n, shape in (("u_s", (NBLK, 2 * P, L, M)), ("cout_s", (NBLK, P, 2, GB, P)),
                     ("kp_s", (NBLK, GC, 2, GB, KPAD)), ("y_s", (NBLK, 2 * P, L, M)), ("gate_s", (32, P, T))):
        args.append(nc.dram_tensor(n, shape, F32).ap())
    args.append(nc.dram_tensor("out", (1, T, D), F32, kind="ExternalOutput").ap())
    build(nc, *args)
    r = _run(nc, [arrays], core_ids=[0])
    return r.results[0]["out"]
```

```python
import math
from contextlib import ExitStack

import numpy as np

import concourse.bass as bass
from concourse import mybir

F32 = mybir.dt.float32
F32R = mybir.dt.float32r
ACT = mybir.ActivationFunctionType
ALU = mybir.AluOpType
AX = mybir.AxisListType

P = 128
D = 2048
T = 512
TT = T // P
KT = D // P
HALF = 1024
HT = HALF // P
IN_W = 6400
OFF_Q, OFF_K, OFF_V, OFF_GATE = 1024, 2048, 2176, 2304
DFF = 5632
UNIT = KT * P
NG, GC, NS = 64, 16, 64
L = 8
M = T // L
GP = NG // 2
GB = 8
SCAN = 7
NBLK = GP // GB
NCH, CH = 8, 64
CH_Y, CH_Z = 2, 6
PAIRS, HD = 8, 64
KEYS = 128
FB, FT = 4, 11
DK = [4, 4, 3]
NB = D // 512
EPS = 1e-6
NEG = -1e30
GELU_C = math.sqrt(2.0 / math.pi)
ROUND = 1.5 * 2.0 ** 23
TWO_PI = [6.28125, 0.0019340515136718750, 1.2556659146e-6]
KPAD = 7 * GC + L * GC

U_KV = 16
U_GATE = 18
U_GLU = 50
U_AB = 54
U_O = 70
U_FF = 86
FB_UNITS = 2 * FT + NB * len(DK)
U_END = U_FF + FB * FB_UNITS


class Chain:

    def __init__(self, eng, sem):
        self.eng, self.sem, self.base, self.n, self.saved = eng, sem, 0, 0, []

    def count(self, ins):
        ins.then_inc(self.sem, 1)
        self.n += 1

    def __call__(self, ins):
        self.count(ins)
        self.eng.wait_ge(self.sem, self.base + self.n)

    def enter(self, j, per):
        self.saved.append(self.base + self.n)
        self.base, self.n = self.saved[-1] + j * per, 0

    def leave(self, times, per):
        assert self.n == per, (self.n, per)
        self.base, self.n = self.saved.pop() + times * per, 0


def build(nc, x, norm1_g, w_in, lam_re, lam_im, log_dt, b_re, b_im, c_re, c_im, d_skip, w_glu, b_glu,
          sinks, w_a, w_b, w_o, norm2_g, w_gate, w_up, w_down, normf_g, ident_c, alibi_c,
          u_s, cout_s, kp_s, y_s, gate_s, out):
    ctx = ExitStack()
    with ctx:
        base = -(-nc.sbuf_base // 32) * 32
        end = nc.sbuf_usable_end

        def at(name, shape, kb, dt=F32):
            off = base + int(kb * 1024)
            assert off + 4 * int(np.prod(shape[1:])) <= end, name
            return nc.alloc_sbuf_tensor_at(name, shape, dt, offset=off)

        def sem(name):
            return ctx.enter_context(nc.semaphore(name))

        raw = at("raw", [P, 2, UNIT], 0)
        w_hi = at("w_hi", [P, 2, UNIT], 16, F32R)
        w_lo = at("w_lo", [P, 2, UNIT], 32, F32R)
        act_hi = at("act_hi", [P, KT, T], 48, F32R)
        act_lo = at("act_lo", [P, KT, T], 80, F32R)
        ident = at("ident", [P, P], 112)
        vec_t = at("vec_t", [P, 48], 112.5)
        b_half = at("b_half", [P, HT], 112.6875)
        stat = at("stat", [P, 4, TT], 112.71875)
        sink = at("sink", [P, PAIRS], 112.78125)
        sink_raw = at("sink_raw", [P, 2 * PAIRS], 112.9375)
        row_max = at("row_max", [P, PAIRS], 112.8125)
        neg_max = at("neg_max", [P, PAIRS], 112.84375)
        den = at("den", [P, PAIRS], 112.875)
        sink_e = at("sink_e", [P, PAIRS], 112.90625)
        vec_raw = at("vec_raw", [48, P], 113)
        ssq_p = at("ssq_p", [P, 2, TT], 113)
        a8 = at("a8", [P, 2, 2, GP], 113.5)
        A = 114
        xt = at("xt", [P, TT, D], A)
        x1 = at("x1", [P, TT, D], A)
        q_t = at("q_t", [P, PAIRS, T], A)
        cout = at("cout", [P, 2, GB, L + 1, GC], A + 16)
        tmp = at("tmp", [P, GB * (L + 1) * GC], A + 25)
        bb_pad = at("bb_pad", [P, 2, GB, 2 * GC], A + 29.5)
        k_pad = at("k_pad", [P, 2, CH + T], A + 16)
        v_t = at("v_t", [P, CH + T], A + 20.5)
        q_c = at("q_c", [P, PAIRS, CH], A + 22.75)
        k_c = at("k_c", [P, 2, KEYS], A + 24.75)
        v_ct = at("v_ct", [P, KEYS], A + 25.75)
        v_c = at("v_c", [P, P], A + 26.25)
        gate_o = at("gate_o", [P, 2, T], A + 27)
        state = at("state", [P, M, 2, GP], A + 32)
        b_sb = at("b_sb", [P, 2, GP, GC], A + 48)
        c_sb = at("c_sb", [P, 2, GP, GC], A + 52)
        powers = at("powers", [P, L + 1, 2, GP], A + 56)
        ab_f = at("ab_f", [P, 4, GP], A + 58.25)
        p_tmp = at("p_tmp", [P, 5, GP], A + 58.75)
        sc_w = at("sc_w", [P, SCAN + 1, 2, GP], A + 88)
        sc_t = at("sc_t", [P, 2, 2, GP], A + 90)
        sc_one = at("sc_one", [P, 1, 1, 1], A + 90.5)
        par = at("par", [GP, 4, 2, NS * GC], A + 60)
        lam = at("lam", [GP, 16, 2, NS], A + 32)
        dt_r = at("dt_r", [GP, 2], A + 92)
        bs_t = at("bs_t", [P, 2, GP, GC], A + 64)
        bin_t = at("bin_t", [P, 2, GB, P], A + 60)
        k_row = at("k_row", [GP, GB, KPAD], A + 68)
        u2 = at("u2", [P, 2 * GB, M], A + 76)
        u_p = at("u_p", [P, 2, L, M], A + 80)
        b_in = at("b_in", [P, 2, GB, L, GC], A + 84)
        bias = at("bias", [P, PAIRS, KEYS], A + 48)
        score = at("score", [P, PAIRS, KEYS], A + 52)
        prob = at("prob", [P, PAIRS, KEYS], A + 56)
        prob_t = at("prob_t", [P, PAIRS, P], A + 60)
        cy = at("cy", [P, 2, GB, P], A + 64)
        toe = at("toe", [P, 2 * GB, P], A + 72)
        u2y = at("u2y", [P, 2 * GB, M], A + 80)
        y_sb = at("y_sb", [P, 2, GB, M], A + 84)
        st_c = at("st_c", [P, 2, GB, M], A + 88)
        yb_hi = at("yb_hi", [P, HT, T], A + 32, F32R)
        yb_lo = at("yb_lo", [P, HT, T], A + 48, F32R)
        ya_hi = at("ya_hi", [P, HT, T], A, F32R)
        ya_lo = at("ya_lo", [P, HT, T], A + 16, F32R)
        zz = at("zz", [P, HT, T], A + 64)
        y_in = at("y_in", [P, 2, T], A + 80)
        u_in = at("u_in", [P, 2, T], A + 84)
        g_v = at("g_v", [P, 2, T], A + 88)
        gate_in = at("gate_in", [P, 2, 2, T], A + 80)
        mrg = at("mrg", [P, 2, T], A + 88)
        xn = at("xn", [P, TT, D], A + 32)
        m_hi = at("m_hi", [P, FT, T], A + 32, F32R)
        m_lo = at("m_lo", [P, FT, T], A + 54, F32R)
        ff_t = at("ff_t", [P, T], A + 76)
        ff_m = at("ff_m", [P, T], A + 78)
        normf = at("normf", [P, D], A + 84)
        xg = at("xg", [P, TT, D], 48)

        bank = [ctx.enter_context(nc.psum_tensor(f"bank{i}", [P, 512], F32)) for i in range(8)]

        raw_here = [sem("raw_here0"), sem("raw_here1")]
        hi_ready = sem("hi_ready")
        lo_ready = sem("lo_ready")
        units_done = sem("units_done")
        read_out = sem("read_out")
        x_here = [sem(f"x_here{t}") for t in range(TT)]
        ident_here, const_here, par_here, dt_here = (sem("ident_here"), sem("const_here"), sem("par_here"),
                                                     sem("dt_here"))
        dve_own, pool_own = sem("dve_own"), sem("pool_own")
        ssq_ready, var_ready = sem("ssq_ready"), sem("var_ready")
        root_ready, rstd_ready = sem("root_ready"), sem("rstd_ready")
        xa_ready = sem("xa_ready")
        xn_ready = sem("xn_ready")
        tr_done = sem("tr_done")
        nhi_ready, nlo_ready = sem("nhi_ready"), sem("nlo_ready")
        par_t, par_out = sem("par_t"), sem("par_out")
        dt_exp, mag_arg, mag_ready = sem("dt_exp"), sem("mag_arg"), sem("mag_ready")
        ang_ready, sin_ready, af_ready = sem("ang_ready"), sem("sin_ready"), sem("af_ready")
        vec_ready = sem("vec_ready")
        powers_ready, b_scaled = sem("powers_ready"), sem("b_scaled")
        tab_c, tab_b = sem("tab_c"), sem("tab_b")
        bint_done, bint_ready = sem("bint_done"), sem("bint_ready")
        k_done, krow_ready, krow_zero = sem("k_done"), sem("krow_ready"), sem("krow_zero")
        u_stored, u2_here, tab_stored = sem("u_stored"), sem("u2_here"), sem("tab_stored")
        x_done, state_in = sem("x_done"), sem("state_in")
        pads, kv_ev, kv_dup, bias_here = sem("pads"), sem("kv_ev"), sem("kv_dup"), sem("bias_here")
        staged, scores_done, neg_ready = sem("staged"), sem("scores_done"), sem("neg_ready")
        exps, vc_ready, prob_ready = sem("exps"), sem("vc_ready"), sem("prob_ready")
        pt_done, pt_ready, pv_done, yb_ready = sem("pt_done"), sem("pt_ready"), sem("pv_done"), sem("yb_ready")
        gate_st = [sem("gate_st0"), sem("gate_st1")]
        ytab_here, st_staged = sem("ytab_here"), sem("st_staged")
        y_done, y_ev, y_stored = sem("y_done"), sem("y_ev"), sem("y_stored")
        yin_here = [sem("yin_here0"), sem("yin_here1")]
        y_arg, y_tanh, zz_ready = sem("y_arg"), sem("y_tanh"), sem("zz_ready")
        zhi_ready, zlo_ready = sem("zhi_ready"), sem("zlo_ready")
        ybhi_ready, yblo_ready = sem("ybhi_ready"), sem("yblo_ready")
        glu_t, glu_m = sem("glu_t"), sem("glu_m")
        yahi_ready, yalo_ready = sem("yahi_ready"), sem("yalo_ready")
        gin_here = [sem("gin_here0"), sem("gin_here1")]
        mrg_ready, mhi_ready, mlo_ready = sem("mrg_ready"), sem("mhi_ready"), sem("mlo_ready")
        xres_here, normf_here = sem("xres_here"), sem("normf_here")
        tok_done = sem("tok_done")
        tok_free = sem("tok_free")
        ff_read, up_read = sem("ff_read"), sem("up_read")
        ff_tanh = sem("ff_tanh")
        ffhi_ready, fflo_ready = sem("ffhi_ready"), sem("fflo_ready")
        by_g_ready = sem("by_g_ready")
        out_ready, out_st = sem("out_ready"), sem("out_st")

        def k_rows(w):
            return w[0].rearrange("(k p) n -> p k n", p=P)

        win_v, glu_v, wa_v, wb_v = k_rows(w_in), k_rows(w_glu), k_rows(w_a), k_rows(w_b)
        wo_v, wg_v, wu_v, wd_v = k_rows(w_o), k_rows(w_gate), k_rows(w_up), k_rows(w_down)
        x_v = x[0].rearrange("(t p) n -> p t n", p=P)
        out_v = out[0].rearrange("(t p) n -> p t n", p=P)

        def slot(tile, p, width):
            return tile[:, p, :].rearrange("p (k n) -> p k n", n=width)

        def arrived(q, p):
            return 16 * q + 16

        block = ctx.enter_context(nc.Block())

        def apart(eng):
            eng.wait_ge(vec_ready, 1)

        @block.sync
        def _(sp):
            for i, v in enumerate((lam_re, lam_im)):
                sp.dma_start(lam[:, i], v[0].rearrange("(h g) p -> g h p", h=2)).then_inc(dt_here, 16)
            with nc.allow_non_contiguous_dma(reason="64 step sizes"):
                sp.dma_start(dt_r[:, :], log_dt[0].rearrange("(h g) -> g h", h=2)).then_inc(dt_here, 16)
            for t in range(TT):
                sp.dma_start(xt[:, t, :], x_v[:, t, :]).then_inc(x_here[t], 16)

            def load(u, p, src, dst, first=False):
                if not first:
                    sp.wait_ge(lo_ready, u - 1)
                sp.dma_start(dst, src).then_inc(raw_here[p], 16)

            def load_in(b, first=False):
                cols = [b * P, b * P + NBLK * P, b * (2 * P) + OFF_Q, b * (2 * P) + (OFF_Q + P)]
                for i, c in enumerate(cols):
                    load(4 * b + i, i % 2, win_v[:, :, bass.ds(c, P)], slot(raw, i % 2, P), first=first and i < 2)

            load_in(0, True)
            with sp.Fori(1, NBLK) as b:
                load_in(b)
            load(U_KV, 0, win_v[:, :, OFF_K:OFF_K + P], slot(raw, 0, P))
            load(U_KV + 1, 1, win_v[:, :, OFF_V:OFF_V + P], slot(raw, 1, P))

            def load_gates(n, y=None, first=False):
                for i in range(4):
                    load(4 * n + (U_GATE + i), i % 2, win_v[:, :, bass.ds(n * (4 * P) + (OFF_GATE + i * P), P)],
                         slot(raw, i % 2, P))
                    if y is not None and i == 1:
                        if not first:
                            sp.wait_ge(y_done, 2 * y)
                        sp.dma_start(cy[:, :, :, :], cout_s[y]).then_inc(ytab_here, 16)
                        for r in range(L):
                            sp.dma_start(toe[16 * r:16 * r + 16],
                                         kp_s[y, :, :, :, 16 * r:16 * r + P].rearrange("c h g w -> c (h g) w")
                                         ).then_inc(ytab_here, 16)
                            sp.dma_start(u2y[16 * r:16 * r + 16, :, :],
                                         u_s[y, :, L - 1 - r, :].rearrange("(j c) m -> c j m", c=GC)
                                         ).then_inc(ytab_here, 16)

            with sp.Fori(0, CH_Y) as n:
                load_gates(n)
            sp.wait_ge(tab_stored, 16 * 3 * NBLK)
            load_gates(CH_Y, y=0, first=True)
            with sp.Fori(CH_Y + 1, CH_Z) as n:
                load_gates(n, y=n - CH_Y)
            with sp.Fori(CH_Z, NCH) as n:
                load_gates(n)
            for i in range(4):
                load(U_GLU + i, i % 2, glu_v[:, :, i * 256:(i + 1) * 256], slot(raw, i % 2, 256))
            with sp.Fori(0, 8) as j:
                for i in range(2):
                    cols = bass.ds(j * (2 * P) + i * P, P)
                    load(U_AB + 2 * j + i, i, wa_v[:, :, cols], slot(raw, i, P)[:, 0:HT])
                    sp.dma_start(slot(raw, i, P)[:, HT:KT], wb_v[:, :, cols]).then_inc(raw_here[i], 16)
            with sp.Fori(0, NB) as n:
                for i in range(4):
                    load(U_O + 4 * n + i, i % 2, wo_v[:, 4 * i:4 * i + 4, bass.ds(n * 512, 512)],
                         slot(raw, i % 2, 512))
            with sp.Fori(0, FB) as f:
                with sp.Fori(0, FT) as j:
                    for i, w in enumerate((wg_v, wu_v)):
                        load(U_FF + i + f * FB_UNITS + j * 2, i, w[:, :, bass.ds(f * (FT * P) + j * P, P)],
                             slot(raw, i, P))
                with sp.Fori(0, 2) as n:
                    for u in range(6):
                        i, e = u // 3, u % 3
                        load(U_FF + 2 * FT + u + f * FB_UNITS + n * 6, u % 2,
                             wd_v[:, bass.ds(f * FT + 4 * e, DK[e]), bass.ds(n * 1024 + i * 512, 512)],
                             slot(raw, u % 2, 512)[:, 0:DK[e]])
            sp.wait_ge(out_st, 16 * TT)

        @block.gpsimd
        def _(pool):
            own = Chain(pool, pool_own)
            pool.wait_ge(x_here[TT - 1], 16)
            for i, w in enumerate((b_re, b_im)):
                pool.dma_start(par[:, i], w[0].rearrange("(h g) p c -> g h (p c)", h=2)).then_inc(par_here, 16)
            for i, w in enumerate((c_re, c_im)):
                for h in range(2):
                    pool.dma_start(par[:, 2 + i].rearrange("g a (c h p) -> g (a c) h p", h=2, p=NS)[:, :, h],
                                   w[0, GP * h:GP * h + GP]).then_inc(par_here, 16)
            pool.wait_ge(par_out, 1)
            v = nc.gpsimd
            v.memset(powers[:, 0, 0, :], 1.0)
            v.memset(powers[:, 0, 1, :], 0.0)
            own(v.tensor_copy(powers[:, 1], ab_f[:, 0:2, :]))

            def times(dst, n, xs, ys):
                def part(x0, r):
                    return powers[:, x0:x0 + n, r, :]

                def one(r):
                    return powers[:, ys:ys + 1, r, :].to_broadcast([P, n, GP])

                t = p_tmp[:, 0:n, :]
                own(v.tensor_tensor(t, part(xs, 1), one(1), ALU.mult))
                own(v.tensor_tensor(part(dst, 0), part(xs, 0), one(0), ALU.mult))
                own(v.tensor_tensor(part(dst, 0), part(dst, 0), t, ALU.subtract))
                own(v.tensor_tensor(t, part(xs, 1), one(0), ALU.mult))
                own(v.tensor_tensor(part(dst, 1), part(xs, 0), one(1), ALU.mult))
                own(v.tensor_tensor(part(dst, 1), part(dst, 1), t, ALU.add))

            times(2, 1, 1, 1)
            times(3, 2, 1, 2)
            times(5, 4, 1, 4)
            for r in range(2):
                v.tensor_copy(a8[:, 0, r], powers[:, L, 0, :])
            v.tensor_copy(a8[:, 1, 0], powers[:, L, 1, :])
            v.tensor_tensor(a8[:, 1, 1], powers[:, 0, 1, :], powers[:, L, 1, :], ALU.subtract
                            ).then_inc(powers_ready, 1)
            pool.wait_ge(par_out, 5)
            bshape = [P, GP, GC]
            f_re = ab_f[:, 2, :].unsqueeze(2).to_broadcast(bshape)
            f_im = ab_f[:, 3, :].unsqueeze(2).to_broadcast(bshape)
            t0, t1 = bs_t[:, 0], bs_t[:, 1]
            own.count(v.tensor_tensor(t0, b_sb[:, 0], f_im, ALU.mult))
            own(v.tensor_tensor(t1, b_sb[:, 1], f_im, ALU.mult))
            own.count(v.tensor_tensor(b_sb[:, 0], b_sb[:, 0], f_re, ALU.mult))
            own(v.tensor_tensor(b_sb[:, 1], b_sb[:, 1], f_re, ALU.mult))
            own(v.tensor_tensor(b_sb[:, 0], b_sb[:, 0], t1, ALU.subtract))
            v.tensor_tensor(b_sb[:, 1], b_sb[:, 1], t0, ALU.add).then_inc(b_scaled, 1)
            pool.memset(k_row[:, :, 0:7 * GC], 0.0).then_inc(krow_zero, 1)

            with pool.Fori(0, NBLK) as b:
                for i in range(2):
                    pool.wait_ge(read_out, 4 * b + (i + 3))
                    apart(pool)
                    pool.dma_start(u_s[b, i * P:(i + 1) * P], u_p[:, i]).then_inc(u_stored, 16)
                pool.wait_ge(u_stored, 32 * b + 32)
                pool.wait_ge(units_done, 4 * b + 3)
                apart(pool)
                for r in range(L):
                    pool.dma_start(u2[16 * r:16 * r + 16, :, :],
                                   u_s[b, :, L - 1 - r, :].rearrange("(j c) m -> c j m", c=GC)).then_inc(u2_here, 16)
                pool.wait_ge(tab_c, b + 1)
                apart(pool)
                pool.dma_start(cout_s[b].rearrange("p r g (l c) -> p (r g) (l c)", c=GC),
                               cout[:, :, :, 1:, :].rearrange("p r g l c -> p (r g) (l c)")).then_inc(tab_stored, 16)
                pool.wait_ge(krow_ready, 2 * b + 2)
                apart(pool)
                for h in range(2):
                    pool.dma_start(kp_s[b, :, h], k_row[16 * h:16 * h + 16]).then_inc(tab_stored, 16)

            pool.wait_ge(state_in, 2 * NBLK)
            pool.wait_ge(powers_ready, 1)
            def copy(dst, src):
                shape = [P] + [int(n) for n in dst.shape[1:]]
                return pool.tensor_tensor(dst, src, sc_one[:, :, :, :].to_broadcast(shape), ALU.mult)

            own(pool.memset(sc_one[:, :, :, :], 1.0))
            own(copy(sc_w[:, 0:1], state[:, 0:1]))
            with pool.Fori(0, (M - 1) // SCAN) as m:
                own.enter(m, 3 * SCAN + 3)
                apart(pool)
                own(copy(sc_w[:, 1:], state[:, bass.ds(m * SCAN + 1, SCAN)]))
                for i in range(SCAN):
                    prev, cur = sc_w[:, i], sc_w[:, i + 1]
                    own(pool.tensor_tensor(sc_t[:, :], prev.unsqueeze(1).to_broadcast([P, 2, 2, GP]), a8[:, :],
                                           ALU.mult))
                    own(pool.tensor_tensor(cur, cur, sc_t[:, 0], ALU.add))
                    own(pool.tensor_tensor(cur, cur, sc_t[:, 1, ::-1, :], ALU.add))
                own.count(copy(sc_w[:, 0:1], sc_w[:, SCAN:]))
                own(copy(state[:, bass.ds(m * SCAN + 1, SCAN)], sc_w[:, 1:]))
                own.leave((M - 1) // SCAN, 3 * SCAN + 3)
            own(pool.memset(st_c[:, :, :, 0:1], 0.0))
            with pool.Fori(0, NBLK) as b:
                pool.wait_ge(units_done, 4 * b + (2 + U_GATE + 4 * CH_Y))
                apart(pool)
                for r in range(2):
                    pool.tensor_copy(st_c[:, r, :, 1:M],
                                     state[:, 0:M - 1, r, bass.ds(b * GB, GB)].rearrange("p m g -> p g m")
                                     ).then_inc(st_staged, 1)
                pool.wait_ge(y_stored, 128 * b + 128)

            pool.wait_ge(zz_ready, HT)
            for i in range(2):
                pool.wait_ge(gate_st[i], 16 * 16)
            for i in range(2):
                for e in range(2):
                    pool.dma_start(gate_in[:, i, e, :], gate_s[16 * e + i]).then_inc(gin_here[i], 16)
            with pool.Fori(1, 8) as j:
                for i in range(2):
                    pool.wait_ge(mrg_ready, 2 * j + i - 1)
                    apart(pool)
                    for e in range(2):
                        pool.dma_start(gate_in[:, i, e, :], gate_s[2 * j + (16 * e + i)]).then_inc(gin_here[i], 16)
            pool.wait_ge(units_done, 2 + U_O)
            pool.dma_start(x1[:, :, :], x_v).then_inc(xres_here, 16)
            pool.wait_ge(mlo_ready, KT)
            pool.dma_start(normf[:, :], normf_g.partition_broadcast(P)).then_inc(normf_here, 16)
            pool.wait_ge(normf_here, 16)
            for n in range(NB):
                cols = slice(512 * n, 512 * n + 512)
                for t in range(TT):
                    pool.wait_ge(tok_free, 4 + NB * TT * FB + TT * n + t + 1)
                    pool.tensor_tensor(xg[:, t, cols], x1[:, t, cols], normf[:, cols], ALU.mult
                                       ).then_inc(by_g_ready, 1)

        @block.scalar
        def _(act):
            run = nc.scalar.activation

            def hi(q, p, here, n=UNIT):
                act.wait_ge(raw_here[p], here)
                act.wait_ge(units_done, 2 * q + (p + 1))
                run(w_hi[:, p, 0:n], raw[:, p, 0:n], ACT.Copy).then_inc(hi_ready, 1)

            def unit_done(q, p):
                act.wait_ge(units_done, 2 * q + (p + 3))

            def square(src, t):
                run(act_lo[:, 4 * t:4 * t + 4, :].rearrange("p k n -> p (k n)"), src[:, t, :], ACT.Square,
                    accum_out=stat[:, 0, t:t + 1]).then_inc(ssq_ready, 1)

            def transposed(c, g0):
                for k in range(KT):
                    act.wait_ge(tr_done, c * KT + k + 1)
                    run(act_hi[:, k, :], bank[1 + k % 7][:, :], ACT.Copy, scale=vec_t[:, g0 + k:g0 + k + 1]
                        ).then_inc(nhi_ready, 1)

            def roots(c):
                act.wait_ge(var_ready, c + 1)
                run(stat[:, 2, :], stat[:, 1, :], ACT.Sqrt).then_inc(root_ready, 1)
                act.wait_ge(rstd_ready, c + 1)

            act.dma_start(ident[:, :], ident_c[:, :]).then_inc(ident_here, 16)
            for r0, v, n in ((0, norm1_g[0], KT), (16, norm2_g[0], KT),
                             (32, d_skip[0].rearrange("g c -> (g c)"), HT), (40, b_glu[0], HT)):
                act.dma_start(vec_raw[r0:r0 + n, :], v.rearrange("(k p) -> k p", p=P)).then_inc(const_here, 16)
            act.dma_start(sink_raw[:, :], sinks[0].partition_broadcast(P)).then_inc(const_here, 16)
            act.wait_ge(dt_here, 48)
            run(dt_r[:, :], dt_r[:, :], ACT.Exp).then_inc(dt_exp, 1)
            act.wait_ge(mag_arg, 1)
            run(lam[:, 2], lam[:, 2], ACT.Exp).then_inc(mag_ready, 1)
            act.wait_ge(ang_ready, 1)
            run(lam[:, 5], lam[:, 4], ACT.Sin, scale=0.5)
            run(lam[:, 6], lam[:, 4], ACT.Sin).then_inc(sin_ready, 1)
            for t in range(TT):
                act.wait_ge(x_here[t], 16)
                square(xt, t)
            roots(0)
            for t in (2, 3):
                run(xt[:, t, HALF:], xt[:, t, HALF:], ACT.Copy, scale=stat[:, 3, t:t + 1]).then_inc(xn_ready, 1)
            hi(0, 0, arrived(0, 0))
            act.wait_ge(vec_ready, 1)
            run(b_half[:, :], vec_t[:, 40:48], ACT.Copy, scale=0.5).then_inc(read_out, 2)
            transposed(0, 0)

            def mixer_inputs(b, first):
                def step(i):
                    hi(2 * b + (i + 1) // 2, (i + 1) % 2, arrived(2 * b + (i + 1) // 2, 0))
                    unit_done(2 * b + i // 2, i % 2)

                for i in range(2):
                    step(i)
                    if first and i == 0:
                        for e in (2, 3, 0, 1):
                            act.wait_ge(par_t, 2 + (e + 2) % 4)
                            run((b_sb if e < 2 else c_sb)[:, e % 2].rearrange("p g c -> p c g"),
                                bank[2 + e][:, :].rearrange("p (c g) -> p c g", g=GP), ACT.Copy).then_inc(par_out, 1)
                    run(u_p[:, i].rearrange("p s m -> p m s"), bank[i][:, :].rearrange("p (m s) -> p m s", s=L),
                        ACT.Copy).then_inc(read_out, 1)
                step(2)
                run(q_t[:, 2 * b, :], bank[0][:, :], ACT.Copy).then_inc(read_out, 1)
                for e in range(4):
                    act.wait_ge(bint_done, 4 * b + (e + 1))
                    run(bin_t[:, e // 2, 4 * (e % 2):4 * (e % 2) + 4, :],
                        bank[2 + e][:, :].rearrange("p (g w) -> p g w", w=P), ACT.Copy).then_inc(bint_ready, 1)
                act.wait_ge(k_done, b + 1)
                if first:
                    act.wait_ge(krow_zero, 1)
                else:
                    act.wait_ge(tab_stored, 48 * b)
                for e in range(2):
                    run(k_row[:, 4 * e:4 * e + 4, 7 * GC:], bank[6 + e][0:GP, :].rearrange("p (g w) -> p g w", w=P),
                        ACT.Copy).then_inc(krow_ready, 1)
                step(3)
                run(q_t[:, 2 * b + 1, :], bank[1][:, :], ACT.Copy).then_inc(read_out, 1)
                act.wait_ge(x_done, b + 1)
                for r in range(2):
                    run(state[:, :, r, bass.ds(b * GB, GB)].rearrange("p m g -> p g m"),
                        bank[2 + r][:, :].rearrange("p (g m) -> p g m", m=M), ACT.Copy).then_inc(state_in, 1)

            mixer_inputs(0, True)
            with act.Fori(1, NBLK) as b:
                mixer_inputs(b, False)

            hi(8, 1, arrived(8, 1))
            unit_done(8, 0)
            act.wait_ge(pads, 1)
            run(k_pad[0:64, 0, CH:], bank[0][0:64, :], ACT.Copy).then_inc(kv_ev, 1)
            run(k_pad[64:P, 1, CH:], bank[0][64:P, :], ACT.Copy).then_inc(read_out, 1)
            act.wait_ge(kv_ev, 1)
            act.wait_ge(read_out, U_KV + 3)
            act.dma_start(k_pad[64:P, 0, CH:], k_pad[0:64, 0, CH:]).then_inc(kv_dup, 16)
            act.dma_start(k_pad[0:64, 1, CH:], k_pad[64:P, 1, CH:]).then_inc(kv_dup, 16)
            act.dma_start(bias[:, :, :], alibi_c[:, :, :]).then_inc(bias_here, 16)
            hi(9, 0, arrived(9, 0))
            unit_done(8, 1)
            run(v_t[:, CH:], bank[1][:, :], ACT.Copy).then_inc(read_out, 1)

            def load_y(t):
                h, b = t // NBLK, t % NBLK
                if t == 0:
                    act.wait_ge(y_stored, 16 * L * NBLK)
                elif t >= 2:
                    act.wait_ge(zz_ready, t - 1)
                for dst, src in ((y_in, y_s), (u_in, u_s)):
                    act.dma_start(dst[:, t % 2, :], src[b, h * P:(h + 1) * P].rearrange("c t m -> c (t m)")
                                  ).then_inc(yin_here[t % 2], 16)

            def gates(n, first=False, y=None, z=None):
                q0 = 2 * n + U_GATE // 2

                def gate(i):
                    hi(q0 + (i + 1) // 2, (i + 1) % 2, arrived(q0 + (i + 1) // 2, 0))
                    if z is not None:
                        if z + i == 0:
                            load_y(0)
                        if z + i + 1 < HT:
                            load_y(z + i + 1)
                    unit_done(q0 + i // 2, i % 2)
                    if not (first and i < 2):
                        act.wait_ge(gate_st[i % 2], 32 * n + 16 * (i // 2))
                    run(gate_o[:, i % 2, :], bank[i % 2][:, :], ACT.Tanh, scale=0.5).then_inc(read_out, 1)
                    act.wait_ge(read_out, 4 * n + (U_GATE + i + 3))
                    act.dma_start(gate_s[4 * n + i], gate_o[:, i % 2, :]).then_inc(gate_st[i % 2], 16)
                    if z is not None:
                        act.wait_ge(y_arg, z + i + 1)
                        run(g_v[:, i % 2, :], g_v[:, i % 2, :], ACT.Tanh, scale=GELU_C).then_inc(y_tanh, 1)

                gate(0)
                act.wait_ge(scores_done, n + 1)
                run(v_c[:, :], bank[6][:, 0:P], ACT.Copy).then_inc(vc_ready, 1)
                act.wait_ge(neg_ready, n + 1)
                for j in range(PAIRS):
                    run(prob[:, j, :], score[:, j, :], ACT.Exp, bias=neg_max[:, j:j + 1], accum_out=den[:, j:j + 1])
                run(sink_e[:, :], sink_e[:, :], ACT.Exp).then_inc(exps, 1)
                gate(1)
                if y is not None:
                    y_part(y, 0)
                gate(2)
                for e in range(2):
                    act.wait_ge(pt_done, 2 * n + (e + 1))
                    run(prob_t[:, 4 * e:4 * e + 4, :], bank[4 + e][:, :].rearrange("p (j w) -> p j w", w=P), ACT.Copy
                        ).then_inc(pt_ready, 1)
                if y is not None:
                    y_part(y, 1)
                    act.wait_ge(y_ev, 2 * y + 2)
                    for t in range(L):
                        act.dma_start(y_s[y, :, t, :].rearrange("(j c) m -> c j m", c=GC),
                                      y_sb[16 * t:16 * t + 16].rearrange("p h g m -> p (h g) m")
                                      ).then_inc(y_stored, 16)
                gate(3)

            def y_part(b, h):
                act.wait_ge(y_done, 2 * b + (h + 1))
                run(y_sb[:, h], bank[7][:, :].rearrange("p (g m) -> p g m", m=M), ACT.Copy).then_inc(y_ev, 1)

            gates(0, first=True)
            with act.Fori(1, CH_Y) as n:
                gates(n)
            with act.Fori(CH_Y, CH_Z) as n:
                gates(n, y=n - CH_Y)
            for n in range(CH_Z, NCH):
                gates(n, z=4 * (n - CH_Z))

            for n in range(HT):
                act.wait_ge(zz_ready, n + 1)
                run(act_hi[:, n, :], zz[:, n, :], ACT.Copy, scale=0.5).then_inc(zhi_ready, 1)
            hi(U_GLU // 2, 1, arrived(U_GLU // 2, 1))
            act.wait_ge(yb_ready, NCH)
            for e in range(2):
                run(yb_hi[:, 4 * e:4 * e + 4, :], q_t[:, 4 * e:4 * e + 4, :], ACT.Copy).then_inc(ybhi_ready, 1)
            for i in range(2):
                act.wait_ge(gate_st[i], 16 * 16)
            for i in range(4):
                u = U_GLU + i
                if i > 0:
                    hi((u + 1) // 2, (u + 1) % 2, arrived((u + 1) // 2, 0) + (16 if u + 1 == U_AB else 0))
                unit_done(u // 2, u % 2)
                for e in range(2):
                    n = 2 * i + e
                    if i > 0:
                        act.wait_ge(yalo_ready, n - 1)
                    run(g_v[:, e, :], bank[2 * e + i % 2][:, :], ACT.Tanh, scale=0.5, bias=b_half[:, n:n + 1]
                        ).then_inc(read_out if e else glu_t, 1)
                for e in range(2):
                    n = 2 * i + e
                    act.wait_ge(glu_m, n + 1)
                    run(ya_hi[:, n, :], g_v[:, e, :], ACT.Copy, scale=0.25).then_inc(yahi_ready, 1)

            def merge(j, last=False):
                q = U_AB // 2 + j
                for i in range(2):
                    if i == 0:
                        hi(q, 1, 32 * j + (arrived(U_AB // 2, 1) + 16))
                    elif last:
                        hi(q + 1, 0, arrived(q + 1, 0) + 128)
                    else:
                        hi(q + 1, 0, 32 * j + (arrived(U_AB // 2, 0) + 48))
                    act.wait_ge(mrg_ready, 2 * j + (i + 1))
                    run(act_hi[:, 2 * j + i, :], mrg[:, i, :], ACT.Copy, scale=0.5).then_inc(mhi_ready, 1)

            with act.Fori(0, 7) as j:
                merge(j)
            merge(7, last=True)

            def here(q):
                return 16 * q + (16 + 128)

            with act.Fori(0, NB) as n:
                for i in range(4):
                    q = 2 * n + (U_O + i + 1) // 2
                    hi(q, (i + 1) % 2, here(q))
            for t in range(TT):
                act.wait_ge(tok_free, 4 + (NB - 1) * TT + t + 1)
                square(x1, t)
            roots(1)
            for t in (2, 3):
                run(xn[:, t, :], x1[:, t, :], ACT.Copy, scale=stat[:, 3, t:t + 1]).then_inc(xn_ready, 1)
            transposed(1, KT)

            def ff_block(f, last=False):
                q0 = f * (FB_UNITS // 2) + U_FF // 2
                with act.Fori(0, FT) as j:
                    hi(q0 + j, 1, here(q0 + j))
                    unit_done(q0 + j, 0)
                    run(ff_t[:, :], bank[0][:, :], ACT.Tanh, scale=0.5).then_inc(ff_tanh, 1)
                    hi(q0 + j + 1, 0, here(q0 + j + 1))
                    act.wait_ge(up_read, f * FT + j + 2)
                    run(m_hi[:, j, :], ff_m[:, :], ACT.Copy, scale=0.5).then_inc(ffhi_ready, 1)

                def down(n, very_last=False):
                    for u in range(6):
                        if not (very_last and u == 5):
                            q = q0 + FT + 3 * n + (u + 1) // 2
                            full = u % 3 != 1
                            hi(q, (u + 1) % 2, here(q), UNIT if full else DK[2] * 512)
                        if very_last and u == 2:
                            for t in range(TT):
                                act.wait_ge(tok_free, 4 + NB * TT * (FB + 1) - 2 * TT + t + 1)
                                run(act_lo[:, 4 * t + 4 - 3:4 * t + 4, :].rearrange("p k n -> p (k n)"),
                                    x1[:, t, 0:D - 512], ACT.Square, accum_out=ssq_p[:, 0, t:t + 1]
                                    ).then_inc(ssq_ready, 1)

                if last:
                    down(0)
                    down(1, True)
                else:
                    with act.Fori(0, 2) as n:
                        down(n)

            with act.Fori(0, FB - 1) as f:
                ff_block(f)
            ff_block(FB - 1, last=True)
            for t in range(TT):
                act.wait_ge(tok_free, 4 + NB * TT * (FB + 1) - TT + t + 1)
                run(act_lo[:, t, :], x1[:, t, D - 512:], ACT.Square, accum_out=ssq_p[:, 1, t:t + 1]
                    ).then_inc(ssq_ready, 1)
                act.wait_ge(var_ready, 2 + t + 1)
                run(stat[:, 2, t:t + 1], stat[:, 1, t:t + 1], ACT.Sqrt).then_inc(root_ready, 1)
                act.wait_ge(rstd_ready, 2 + t + 1)
                run(xg[:, t, HALF:], xg[:, t, HALF:], ACT.Copy, scale=stat[:, 3, t:t + 1]).then_inc(out_ready, 1)
                act.wait_ge(out_ready, 2 * t + 2)
                act.dma_start(out_v[:, t, :], xg[:, t, :]).then_inc(out_st, 16)

        @block.vector
        def _(dve):
            v = nc.vector
            own = Chain(dve, dve_own)

            def lo(u, p, n=UNIT):
                dve.wait_ge(hi_ready, u + 1)
                v.tensor_tensor(w_lo[:, p, 0:n], raw[:, p, 0:n], w_hi[:, p, 0:n].bitcast(F32), ALU.subtract
                                ).then_inc(lo_ready, 1)

            def transposed(c, g0):
                for k in range(KT):
                    dve.wait_ge(nhi_ready, c * KT + k + 1)
                    v.scalar_tensor_tensor(act_lo[:, k, :], bank[1 + k % 7][:, :], vec_t[:, g0 + k:g0 + k + 1],
                                           act_hi[:, k, :].bitcast(F32), ALU.mult, ALU.subtract
                                           ).then_inc(nlo_ready, 1)

            def rstd(c):
                dve.wait_ge(ssq_ready, TT * (c + 1))
                v.tensor_scalar(stat[:, 1, :], stat[:, 0, :], 1.0 / D, EPS, ALU.mult, ALU.add).then_inc(var_ready, 1)
                dve.wait_ge(root_ready, c + 1)
                v.reciprocal(stat[:, 3, :], stat[:, 2, :]).then_inc(rstd_ready, 1)
                dve.wait_ge(rstd_ready, c + 1)

            dve.wait_ge(dt_here, 48)
            dve.wait_ge(dt_exp, 1)
            for h in range(2):
                v.tensor_scalar(lam[:, 3, h], lam[:, 1, h], dt_r[:, h:h + 1], None, ALU.mult)
            for h in range(2):
                ins = v.tensor_scalar(lam[:, 2, h], lam[:, 0, h], dt_r[:, h:h + 1], None, ALU.mult)
            ins.then_inc(mag_arg, 1)
            dve.wait_ge(mag_arg, 1)
            own(v.tensor_scalar(lam[:, 4], lam[:, 3], 1.0 / (2.0 * math.pi), ROUND, ALU.mult, ALU.add))
            own(v.tensor_scalar(lam[:, 7], lam[:, 4], -ROUND, None, ALU.add))
            for part in TWO_PI:
                own(v.scalar_tensor_tensor(lam[:, 3], lam[:, 7], -part, lam[:, 3], ALU.mult, ALU.add))
            v.tensor_scalar(lam[:, 4], lam[:, 3], 3.1415925, -3.1415925, ALU.min, ALU.max).then_inc(ang_ready, 1)
            dve.wait_ge(sin_ready, 1)
            dve.wait_ge(mag_ready, 1)
            own(v.tensor_tensor(lam[:, 7], lam[:, 5], lam[:, 5], ALU.mult))
            own(v.tensor_scalar(lam[:, 7], lam[:, 7], -2.0, 1.0, ALU.mult, ALU.add))
            own(v.tensor_tensor(lam[:, 8], lam[:, 2], lam[:, 7], ALU.mult))
            own(v.tensor_tensor(lam[:, 9], lam[:, 2], lam[:, 6], ALU.mult))
            own(v.tensor_scalar(lam[:, 3], lam[:, 8], -1.0, None, ALU.add))
            own(v.tensor_tensor(lam[:, 4], lam[:, 0], lam[:, 0], ALU.mult))
            own(v.tensor_tensor(lam[:, 5], lam[:, 1], lam[:, 1], ALU.mult))
            own(v.tensor_tensor(lam[:, 4], lam[:, 4], lam[:, 5], ALU.add))
            own(v.reciprocal(lam[:, 12], lam[:, 4]))
            for out_, (i0, i1), (i2, i3), op in ((10, (3, 0), (9, 1), ALU.add), (11, (9, 0), (3, 1), ALU.subtract)):
                own(v.tensor_tensor(lam[:, 5], lam[:, i0], lam[:, i1], ALU.mult))
                own(v.tensor_tensor(lam[:, 6], lam[:, i2], lam[:, i3], ALU.mult))
                own(v.tensor_tensor(lam[:, 7], lam[:, 5], lam[:, 6], op))
                ins = v.tensor_tensor(lam[:, out_], lam[:, 7], lam[:, 12], ALU.mult)
                if out_ == 10:
                    own(ins)
            ins.then_inc(af_ready, 1)
            dve.wait_ge(par_t, 1)
            v.tensor_copy(ab_f[:, :, :], bank[0][:, 0:4 * GP].rearrange("p (k g) -> p k g", g=GP)).then_inc(par_out, 1)
            rstd(0)
            for t in range(TT):
                v.tensor_scalar(xt[:, t, 0:HALF], xt[:, t, 0:HALF], stat[:, 3, t:t + 1], None, ALU.mult
                                ).then_inc(xa_ready, 1)
            for t in (0, 1):
                v.tensor_scalar(xt[:, t, HALF:], xt[:, t, HALF:], stat[:, 3, t:t + 1], None, ALU.mult
                                ).then_inc(xn_ready, 1)
            lo(0, 0)
            dve.wait_ge(units_done, 2)
            v.tensor_copy(vec_t[:, :], bank[7][:, 0:48]).then_inc(vec_ready, 1)
            dve.wait_ge(const_here, 80)
            for e in range(2):
                v.tensor_copy(sink[64 * e:64 * e + 64, :], sink_raw[64 * e:64 * e + 64, e::2])
            dve.wait_ge(vec_ready, 1)
            transposed(0, 0)

            own(v.memset(bb_pad[:, :, :, :], 0.0))

            def tables(b, first):
                def blk(tile, r):
                    return tile[:, r, bass.ds(b * GB, GB), :]

                def pw(r, l0, n):
                    return powers[:, l0:l0 + n, r, bass.ds(b * GB, GB)].rearrange("p l g -> p g l")

                def product(out_, a, ar, pr, n, l0):
                    shape = [P, GB, n, GC]
                    return v.tensor_tensor(out_, blk(a, ar).unsqueeze(2).to_broadcast(shape),
                                           pw(pr, l0, n).unsqueeze(3).to_broadcast(shape), ALU.mult)

                lo(4 * b + 1, 1)
                if first:
                    dve.wait_ge(par_out, 5)
                    dve.wait_ge(powers_ready, 1)
                else:
                    dve.wait_ge(k_done, b)
                    dve.wait_ge(tab_stored, 48 * b)
                    apart(dve)
                ct = tmp[:, :].rearrange("p (g l c) -> p g l c", l=L + 1, c=GC)
                own(product(ct, c_sb, 1, 1, L + 1, 0))
                own(product(cout[:, 0], c_sb, 0, 0, L + 1, 0))
                own(v.tensor_tensor(cout[:, 0], cout[:, 0], ct, ALU.subtract))
                own(product(ct, c_sb, 1, 0, L + 1, 0))
                own(product(cout[:, 1], c_sb, 0, 1, L + 1, 0))
                v.scalar_tensor_tensor(cout[:, 1].rearrange("p g l c -> p (g l c)"),
                                       cout[:, 1].rearrange("p g l c -> p (g l c)"), -1.0, tmp[:, :],
                                       ALU.mult, ALU.subtract).then_inc(tab_c, 1)
                lo(4 * b + 2, 0)
                bt = tmp[:, 0:GB * L * GC].rearrange("p (g l c) -> p g l c", l=L, c=GC)
                dve.wait_ge(tab_c, b + 1)
                if first:
                    dve.wait_ge(b_scaled, 1)
                for h in range(2):
                    rows = slice(64 * h, 64 * h + 64)
                    for r in range(2):
                        v.tensor_copy(bb_pad[rows, r, :, GC * h:GC * h + GC], b_sb[rows, r, bass.ds(b * GB, GB), :])
                own(product(bt, b_sb, 1, 1, L, 0))
                own(product(b_in[:, 0], b_sb, 0, 0, L, 0))
                own(v.tensor_tensor(b_in[:, 0], b_in[:, 0], bt, ALU.subtract))
                own(product(bt, b_sb, 1, 0, L, 0))
                own(product(b_in[:, 1], b_sb, 0, 1, L, 0))
                v.tensor_tensor(b_in[:, 1], b_in[:, 1], bt, ALU.add).then_inc(tab_b, 1)
                lo(4 * b + 3, 1)
                lo(4 * b + 4, 0)

            tables(0, True)
            with dve.Fori(1, NBLK) as b:
                own.enter(b - 1, 10)
                tables(b, False)
                own.leave(NBLK - 1, 10)

            lo(U_KV + 1, 1)
            dve.wait_ge(units_done, 2 + U_KV)
            dve.wait_ge(tab_stored, 16 * 3 * NBLK)
            v.memset(v_t[:, 0:CH], 0.0)
            v.memset(k_pad[:, :, 0:CH], 0.0).then_inc(pads, 1)
            lo(U_KV + 2, 0)
            dve.wait_ge(bias_here, 16)
            dve.wait_ge(kv_dup, 32)
            dve.wait_ge(read_out, U_GATE + 2)

            def gelu_arg(t):
                i = t % 2
                dve.wait_ge(yin_here[i], 32 * (t // 2 + 1))
                own(v.scalar_tensor_tensor(y_in[:, i, :], u_in[:, i, :], vec_t[:, 32 + t:33 + t], y_in[:, i, :],
                                           ALU.mult, ALU.add))
                own(v.tensor_tensor(g_v[:, i, :], y_in[:, i, :], y_in[:, i, :], ALU.mult))
                own(v.tensor_scalar(g_v[:, i, :], g_v[:, i, :], 0.044715, 1.0, ALU.mult, ALU.add))
                v.tensor_tensor(g_v[:, i, :], g_v[:, i, :], y_in[:, i, :], ALU.mult).then_inc(y_arg, 1)

            def gelu(t):
                i = t % 2
                dve.wait_ge(y_tanh, t + 1)
                v.scalar_tensor_tensor(zz[:, t, :].rearrange("p (m t) -> p t m", t=L),
                                       g_v[:, i, :].rearrange("p (t m) -> p t m", t=L), 1.0,
                                       y_in[:, i, :].rearrange("p (t m) -> p t m", t=L), ALU.add, ALU.mult
                                       ).then_inc(zz_ready, 1)

            def attend(n, first=False, z=None):
                u0 = 4 * n + U_GATE

                def lo_gelu(i):
                    lo(u0 + i + 1, (i + 1) % 2)
                    if z is not None:
                        if i > 0:
                            gelu(z + i - 1)
                        gelu_arg(z + i)

                v.tensor_scalar(q_c[:, :, :], q_t[:, :, bass.ds(n * CH, CH)], HD ** -0.5, None, ALU.mult)
                v.tensor_copy(k_c[:, :, :], k_pad[:, :, bass.ds(n * CH, KEYS)])
                v.tensor_copy(v_ct[:, :], v_t[:, bass.ds(n * CH, KEYS)]).then_inc(staged, 1)
                lo_gelu(0)
                dve.wait_ge(scores_done, n + 1)
                for e in range(2):
                    own(v.tensor_tensor(score[:, 4 * e:4 * e + 4, :],
                                        bank[2 + e][:, :].rearrange("p (j w) -> p j w", w=KEYS),
                                        bias[:, 4 * e:4 * e + 4, :], ALU.add))
                if first:
                    own(v.memset(score[:, :, 0:CH], NEG))
                own(v.tensor_reduce(row_max[:, :], score[:, :, :], AX.X, ALU.max))
                own(v.tensor_tensor(row_max[:, :], row_max[:, :], sink[:, :], ALU.max))
                own(v.tensor_tensor(sink_e[:, :], sink[:, :], row_max[:, :], ALU.subtract))
                v.tensor_scalar(neg_max[:, :], row_max[:, :], -1.0, None, ALU.mult).then_inc(neg_ready, 1)
                lo_gelu(1)
                dve.wait_ge(exps, n + 1)
                own(v.tensor_tensor(den[:, :], den[:, :], sink_e[:, :], ALU.add))
                own(v.reciprocal(den[:, :], den[:, :]))
                v.tensor_tensor(prob[:, :, :], prob[:, :, :], den[:, :].unsqueeze(2).to_broadcast([P, PAIRS, KEYS]),
                                ALU.mult).then_inc(prob_ready, 1)
                lo_gelu(2)
                lo_gelu(3)
                dve.wait_ge(pv_done, n + 1)
                v.tensor_scalar(q_t[:, :, bass.ds(n * CH, CH)], bank[6][:, :].rearrange("p (j w) -> p j w", w=CH),
                                1.0, None, ALU.mult).then_inc(yb_ready, 1)
                if z is not None:
                    gelu(z + 3)

            attend(0, True)
            with dve.Fori(1, CH_Z) as n:
                own.enter(n - 1, 7)
                attend(n)
                own.leave(CH_Z - 1, 7)
            for n in range(CH_Z, NCH):
                attend(n, z=4 * (n - CH_Z))

            for n in range(HT):
                dve.wait_ge(zhi_ready, n + 1)
                v.scalar_tensor_tensor(act_lo[:, n, :], zz[:, n, :], 0.5, act_hi[:, n, :].bitcast(F32),
                                       ALU.mult, ALU.subtract).then_inc(zlo_ready, 1)
            lo(U_GLU + 1, 1)
            for e in range(2):
                dve.wait_ge(ybhi_ready, e + 1)
                part = slice(4 * e, 4 * e + 4)
                v.tensor_tensor(yb_lo[:, part, :], q_t[:, part, :], yb_hi[:, part, :].bitcast(F32), ALU.subtract
                                ).then_inc(yblo_ready, 1)
            for i in range(2):
                dve.wait_ge(gate_st[i], 16 * 16)
            for i in range(4):
                u = U_GLU + i
                if i > 0:
                    lo(u + 1, (u + 1) % 2)
                for e in range(2):
                    n = 2 * i + e
                    if e == 0:
                        dve.wait_ge(glu_t, i + 1)
                    else:
                        dve.wait_ge(read_out, u + 3)
                    v.scalar_tensor_tensor(g_v[:, e, :], g_v[:, e, :], 1.0, zz[:, n, :], ALU.add, ALU.mult
                                           ).then_inc(glu_m, 1)
                for e in range(2):
                    n = 2 * i + e
                    dve.wait_ge(yahi_ready, n + 1)
                    v.scalar_tensor_tensor(ya_lo[:, n, :], g_v[:, e, :], 0.25, ya_hi[:, n, :].bitcast(F32),
                                           ALU.mult, ALU.subtract).then_inc(yalo_ready, 1)
            with dve.Fori(0, 8) as j:
                own.enter(j, 2)
                for i in range(2):
                    u = 2 * j + (U_AB + i)
                    lo(u + 1, (i + 1) % 2)
                    dve.wait_ge(gin_here[i], 32 * j + 32)
                    dve.wait_ge(units_done, u + 3)
                    own(v.scalar_tensor_tensor(mrg[:, i, :], gate_in[:, i, 0, :], 1.0, bank[i][:, :],
                                               ALU.add, ALU.mult))
                    v.scalar_tensor_tensor(gate_in[:, i, 1, :], gate_in[:, i, 1, :], 1.0, bank[2 + i][:, :],
                                           ALU.add, ALU.mult).then_inc(read_out, 1)
                    dve.wait_ge(read_out, u + 3)
                    v.tensor_tensor(mrg[:, i, :], mrg[:, i, :], gate_in[:, i, 1, :], ALU.add).then_inc(mrg_ready, 1)
                    dve.wait_ge(mhi_ready, 2 * j + (i + 1))
                    v.scalar_tensor_tensor(act_lo[:, 2 * j + i, :], mrg[:, i, :], 0.5,
                                           act_hi[:, 2 * j + i, :].bitcast(F32), ALU.mult, ALU.subtract
                                           ).then_inc(mlo_ready, 1)
                own.leave(8, 2)

            def add_tile(t, n, w, done):
                if t < TT - 1:
                    dve.wait_ge(tok_done, 3 * done + (t + 1))
                else:
                    dve.wait_ge(units_done, w)
                cols = bass.ds(n * 512, 512)
                v.tensor_tensor(x1[:, t, cols], x1[:, t, cols], bank[4 + t][:, :], ALU.add).then_inc(tok_free, 1)

            def add_up(n, w, done):
                for t in range(TT):
                    add_tile(t, n, w, done)

            def last_norm(t):
                dve.wait_ge(ssq_ready, 2 * TT + TT + t + 1)
                own(v.tensor_tensor(stat[:, 0, t:t + 1], ssq_p[:, 0, t:t + 1], ssq_p[:, 1, t:t + 1], ALU.add))
                v.tensor_scalar(stat[:, 1, t:t + 1], stat[:, 0, t:t + 1], 1.0 / D, EPS, ALU.mult, ALU.add
                                ).then_inc(var_ready, 1)
                dve.wait_ge(root_ready, 2 + t + 1)
                dve.wait_ge(by_g_ready, NB * TT - TT + t + 1)
                v.reciprocal(stat[:, 3, t:t + 1], stat[:, 2, t:t + 1]).then_inc(rstd_ready, 1)
                dve.wait_ge(rstd_ready, 2 + t + 1)
                v.tensor_scalar(xg[:, t, 0:HALF], xg[:, t, 0:HALF], stat[:, 3, t:t + 1], None, ALU.mult
                                ).then_inc(out_ready, 1)

            v.memset(stat[:, 2, :], 0.0).then_inc(tok_free, 4)
            dve.wait_ge(xres_here, 16)
            with dve.Fori(0, NB) as n:
                for i in range(4):
                    lo(4 * n + (U_O + i + 1), (i + 1) % 2)
                add_up(n, 4 * n + (U_O + 4 + 2), n)
            dve.wait_ge(tok_free, 4 + NB * TT)
            rstd(1)
            for t in (0, 1):
                v.tensor_scalar(xn[:, t, :], x1[:, t, :], stat[:, 3, t:t + 1], None, ALU.mult).then_inc(xn_ready, 1)
            transposed(1, KT)
            v.memset(stat[:, 0, :], 0.0).then_inc(ff_read, 1)
            v.memset(stat[:, 1, :], 0.0).then_inc(up_read, 1)

            def ff_block(f, last=False):
                u0 = f * FB_UNITS + U_FF
                with dve.Fori(0, FT) as j:
                    t = f * FT + j
                    lo(2 * j + u0 + 1, 1)
                    dve.wait_ge(ff_tanh, t + 1)
                    v.scalar_tensor_tensor(ff_m[:, :], ff_t[:, :], 1.0, bank[0][:, :], ALU.add, ALU.mult
                                           ).then_inc(ff_read, 1)
                    lo(2 * j + u0 + 2, 0)
                    dve.wait_ge(units_done, 2 * j + u0 + 4)
                    dve.wait_ge(ff_read, t + 2)
                    v.tensor_tensor(ff_m[:, :], ff_m[:, :], bank[1][:, :], ALU.mult).then_inc(up_read, 1)
                    dve.wait_ge(up_read, t + 2)
                    dve.wait_ge(ffhi_ready, t + 1)
                    v.scalar_tensor_tensor(m_lo[:, j, :], ff_m[:, :], 0.5, m_hi[:, j, :].bitcast(F32),
                                           ALU.mult, ALU.subtract).then_inc(fflo_ready, 1)
                    dve.wait_ge(fflo_ready, t + 1)

                def down(n, very_last=False):
                    for i in range(2):
                        for e in range(3):
                            x_ = 3 * i + e
                            if not (very_last and x_ == 5):
                                lo(6 * n + (x_ + 1) + u0 + 2 * FT, (x_ + 1) % 2, DK[2] * 512 if e == 1 else UNIT)
                        c = 2 * n + i
                        w, done = 6 * n + (3 * i + 3 + 2) + u0 + 2 * FT, f * NB + 2 * n + (i + NB)
                        if very_last and i == 1:
                            for t in range(TT):
                                add_tile(t, c, w, done)
                                last_norm(t)
                        else:
                            add_up(c, w, done)

                if last:
                    down(0)
                    down(1, True)
                else:
                    with dve.Fori(0, 2) as n:
                        down(n)

            with dve.Fori(0, FB - 1) as f:
                ff_block(f)
            ff_block(FB - 1, last=True)
        @block.tensor
        def _(pe):
            mm = nc.tensor.matmul

            def three(out_, a_hi, a_lo, b_hi, b_lo, first, last):
                mm(out_, a_hi, b_hi, start=first, stop=False)
                mm(out_, a_hi, b_lo, start=False, stop=False)
                return mm(out_, a_lo, b_hi, start=False, stop=last)

            def unit_here(u):
                pe.wait_ge(lo_ready, u + 1)

            def tile_unit(u, p, out_):
                unit_here(u)
                for k in range(KT):
                    ins = three(out_, slot(w_hi, p, P)[:, k], slot(w_lo, p, P)[:, k], act_hi[:, k], act_lo[:, k],
                                k == 0, k == KT - 1)
                ins.then_inc(units_done, 1)

            def in_unit(u, p):
                pe.wait_ge(read_out, u + 1)
                tile_unit(u, p, bank[p][:, :])

            def transposes(src, c, k):
                for t in range(TT):
                    ins = nc.tensor.transpose(bank[1 + k % 7][:, t * P:(t + 1) * P], src[:, t, k * P:(k + 1) * P],
                                              ident[:, :])
                ins.then_inc(tr_done, 1)

            def norm_and_unit(src, c, u):
                for k in range(7):
                    transposes(src, c, k)
                for k in range(KT):
                    pe.wait_ge(nlo_ready, c * KT + k + 1)
                    if k == 0:
                        unit_here(u)
                    ins = three(bank[0][:, :], slot(w_hi, 0, P)[:, k], slot(w_lo, 0, P)[:, k], act_hi[:, k],
                                act_lo[:, k], k == 0, k == KT - 1)
                    if k == 1 and c == 0:
                        pe.wait_ge(xn_ready, TT)
                    if 1 <= k <= KT - 7:
                        transposes(src, c, k + 6)
                ins.then_inc(units_done, 1)

            pe.wait_ge(ident_here, 16)
            pe.wait_ge(af_ready, 1)
            for i in range(4):
                ins = nc.tensor.transpose(bank[0][:, i * GP:(i + 1) * GP],
                                          lam[:, 8 + i].rearrange("g h p -> g (h p)"), ident[0:GP, 0:GP])
            ins.then_inc(par_t, 1)
            pe.wait_ge(const_here, 80)
            nc.tensor.transpose(bank[7][:, 0:48], vec_raw[:, :], ident[0:48, 0:48]).then_inc(units_done, 2)
            pe.wait_ge(vec_ready, 1)
            pe.wait_ge(par_out, 1)
            pe.wait_ge(xa_ready, TT)
            norm_and_unit(xt, 0, 0)
            pe.wait_ge(par_here, 96)
            for i in (2, 3, 0, 1):
                for c in range(GC):
                    if i < 2:
                        src = par[:, i].rearrange("g h (p c) -> g (h p) c", c=GC)[:, :, c]
                    else:
                        src = par[:, i].rearrange("g a n -> g (a n)")[:, c * P:(c + 1) * P]
                    ins = nc.tensor.transpose(bank[2 + i][:, c * GP:(c + 1) * GP], src, ident[0:GP, 0:GP])
                ins.then_inc(par_t, 1)

            def mixer_inputs(b, first=False):
                for i in range(3):
                    if not (first and i == 0):
                        in_unit(4 * b + i, i % 2)
                pe.wait_ge(tab_b, b + 1)
                for e in range(4):
                    for g in range(4):
                        ins = nc.tensor.transpose(bank[2 + e][:, g * P:(g + 1) * P],
                                                  b_in[:, e // 2, 4 * (e % 2) + g].rearrange("p l c -> p (l c)"),
                                                  ident[:, :])
                    ins.then_inc(bint_done, 1)
                for g in range(GB):
                    for r in range(2):
                        ins = mm(bank[6 + g // 4][0:GP, (g % 4) * P:(g % 4 + 1) * P], bb_pad[:, r, g, :],
                                 cout[:, r, g, 0:L, :].rearrange("p l c -> p (l c)"), start=r == 0, stop=r == 1)
                ins.then_inc(k_done, 1)
                in_unit(4 * b + 3, 1)
                pe.wait_ge(bint_ready, 4 * b + 4)
                pe.wait_ge(u2_here, 128 * b + 128)
                for h in range(2):
                    for g in range(GB):
                        for r in range(2):
                            ins = mm(bank[2 + r][64 * h:64 * h + 64, g * M:(g + 1) * M],
                                     bin_t[:, r, g, 64 * h:64 * h + 64], u2[:, GB * h + g, :], start=True, stop=True)
                ins.then_inc(x_done, 1)

            mixer_inputs(0, first=True)
            with pe.Fori(1, NBLK) as b:
                mixer_inputs(b)

            in_unit(U_KV, 0)
            in_unit(U_KV + 1, 1)

            def gates(n, y=None):
                u0 = 4 * n + U_GATE
                in_unit(u0, 0)
                pe.wait_ge(staged, n + 1)
                nc.tensor.transpose(bank[6][:, 0:P], v_ct[:, :], ident[:, :])
                for j in range(PAIRS):
                    for e in range(2):
                        rows = slice(64 * e, 64 * e + 64)
                        ins = mm(bank[2 + j // 4][rows, (j % 4) * KEYS:(j % 4 + 1) * KEYS], q_c[rows, j, :],
                                 k_c[rows, j // 4, :], start=True, stop=True)
                ins.then_inc(scores_done, 1)
                in_unit(u0 + 1, 1)
                if y is not None:
                    y_part(y, 0)
                in_unit(u0 + 2, 0)
                pe.wait_ge(prob_ready, n + 1)
                for j in range(PAIRS):
                    ins = nc.tensor.transpose(bank[4 + j // 4][:, (j % 4) * P:(j % 4 + 1) * P], prob[:, j, :],
                                              ident[:, :])
                    if j % 4 == 3:
                        ins.then_inc(pt_done, 1)
                if y is not None:
                    y_part(y, 1)
                in_unit(u0 + 3, 1)
                pe.wait_ge(pt_ready, 2 * n + 2)
                pe.wait_ge(vc_ready, n + 1)
                for kv in range(2):
                    for e in range(2):
                        ins = mm(bank[6][64 * e:64 * e + 64, 256 * kv:256 * kv + 256], v_c[:, 64 * kv:64 * kv + 64],
                                 prob_t[:, 4 * kv:4 * kv + 4, 64 * e:64 * e + 64], start=True, stop=True)
                ins.then_inc(pv_done, 1)

            def y_part(b, h):
                if h == 0:
                    pe.wait_ge(ytab_here, 16 * 17 * b + 16 * 17)
                    pe.wait_ge(st_staged, 2 * b + 2)
                else:
                    pe.wait_ge(y_ev, 2 * b + 1)
                rows = slice(64 * h, 64 * h + 64)
                for g in range(GB):
                    o = bank[7][:, g * M:(g + 1) * M]
                    mm(o, toe[:, GB * h + g, :], u2y[:, GB * h + g, :], start=True, stop=False)
                    mm(o, cy[rows, 0, g, :], st_c[rows, 0, g, :], start=False, stop=False)
                    ins = mm(o, cy[rows, 1, g, :], st_c[rows, 1, g, :], start=False, stop=True)
                ins.then_inc(y_done, 1)

            with pe.Fori(0, CH_Y) as n:
                gates(n)
            with pe.Fori(CH_Y, CH_Z) as n:
                gates(n, y=n - CH_Y)
            with pe.Fori(CH_Z, NCH) as n:
                gates(n)

            for i in range(4):
                u, p = U_GLU + i, i % 2
                unit_here(u)
                pe.wait_ge(read_out, u + 1)
                for k in range(HT):
                    if i == 0:
                        pe.wait_ge(zlo_ready, k + 1)
                    for e in range(2):
                        cols = slice(e * P, (e + 1) * P)
                        ins = three(bank[2 * e + p][:, :], slot(w_hi, p, 256)[:, k, cols],
                                    slot(w_lo, p, 256)[:, k, cols], act_hi[:, k], act_lo[:, k], k == 0, k == HT - 1)
                ins.then_inc(units_done, 1)
            pe.wait_ge(yblo_ready, 2)
            with pe.Fori(0, 8) as j:
                for i in range(2):
                    u = 2 * j + (U_AB + i)
                    unit_here(u)
                    pe.wait_ge(read_out, u + 1)
                    for e, (a_hi, a_lo) in ((1, (yb_hi, yb_lo)), (0, (ya_hi, ya_lo))):
                        if e == 0:
                            pe.wait_ge(yalo_ready, HT)
                        for k in range(HT):
                            ins = three(bank[2 * e + i][:, :], slot(w_hi, i, P)[:, HT * e + k],
                                        slot(w_lo, i, P)[:, HT * e + k], a_hi[:, k], a_lo[:, k], k == 0, k == HT - 1)
                    ins.then_inc(units_done, 1)

            def tok_unit(u, p, kt0, kn, s_hi, s_lo, first, last, w):
                unit_here(u)
                for t in range(TT):
                    if first:
                        pe.wait_ge(tok_free, w + (t + 1))
                    for k in range(kn):
                        toks = slice(t * P, (t + 1) * P)
                        ins = three(bank[4 + t][:, :], s_hi[:, kt0 + k, toks], s_lo[:, kt0 + k, toks],
                                    slot(w_hi, p, 512)[:, k], slot(w_lo, p, 512)[:, k],
                                    first and k == 0, last and k == kn - 1)
                    if t == TT - 1:
                        ins.then_inc(units_done, 1)
                    elif last:
                        ins.then_inc(tok_done, 1)

            with pe.Fori(0, NB) as n:
                for i in range(4):
                    pe.wait_ge(mlo_ready, 4 * i + 4)
                    tok_unit(4 * n + (U_O + i), i % 2, 4 * i, 4, act_hi, act_lo, i == 0, i == 3, 4 * n)
            pe.wait_ge(xn_ready, 2 * TT)
            norm_and_unit(xn, 1, U_FF)

            def ff_tiles(f, j, first=False):
                u0 = f * FB_UNITS + U_FF
                if not first:
                    pe.wait_ge(ff_read, f * FT + j + 1)
                    tile_unit(2 * j + u0, 0, bank[0][:, :])
                pe.wait_ge(up_read, f * FT + j + 1)
                tile_unit(2 * j + u0 + 1, 1, bank[1][:, :])

            def ff_down(f):
                u0 = f * FB_UNITS + U_FF
                with pe.Fori(0, 2) as n:
                    for i in range(2):
                        for e in range(3):
                            x_ = 3 * i + e
                            pe.wait_ge(fflo_ready, f * FT + min(4 * e + 4, FT))
                            tok_unit(6 * n + x_ + u0 + 2 * FT, x_ % 2, 4 * e, DK[e], m_hi, m_lo, e == 0, e == 2,
                                     TT * NB + f * (TT * NB) + n * (2 * TT) + i * TT)

            ff_tiles(0, 0, first=True)
            with pe.Fori(1, FT) as j:
                ff_tiles(0, j)
            ff_down(0)
            with pe.Fori(1, FB) as f:
                with pe.Fori(0, FT) as j:
                    ff_tiles(f, j)
                ff_down(f)


_INS = ["x", "norm1_g", "w_in", "lam_re", "lam_im", "log_dt", "b_re", "b_im", "c_re", "c_im", "d_skip", "w_glu",
        "b_glu", "sinks", "w_a", "w_b", "w_o", "norm2_g", "w_gate", "w_up", "w_down", "normf_g"]


def alibi():
    dist = np.abs(np.arange(CH)[:, None] + (KEYS - CH) - np.arange(KEYS)[None, :]).astype(np.float32)
    heads = 2 * PAIRS
    slopes = (2.0 ** (-8.0 * np.arange(1, heads + 1) / heads)).astype(np.float32)
    b = -(slopes.reshape(PAIRS, 2)[:, :, None, None] * dist)
    return np.ascontiguousarray(b.transpose(1, 2, 0, 3).reshape(P, PAIRS, KEYS), dtype=np.float32)


def kernel(**inputs):
    import concourse.bacc as _bacc
    from concourse.bass_utils import run_bass_kernel_spmd as _run

    nc = _bacc.Bacc("TRN2", target_bir_lowering=False, num_devices=1)
    arrays = {n: np.ascontiguousarray(inputs[n]) for n in _INS}
    arrays["ident_c"] = np.eye(P, dtype=np.float32)
    arrays["alibi_c"] = alibi()
    args = [nc.dram_tensor(n, a.shape, F32, kind="ExternalInput").ap() for n, a in arrays.items()]
    for n, shape in (("u_s", (NBLK, 2 * P, L, M)), ("cout_s", (NBLK, P, 2, GB, P)),
                     ("kp_s", (NBLK, GC, 2, GB, KPAD)), ("y_s", (NBLK, 2 * P, L, M)), ("gate_s", (32, P, T))):
        args.append(nc.dram_tensor(n, shape, F32).ap())
    args.append(nc.dram_tensor("out", (1, T, D), F32, kind="ExternalOutput").ap())
    build(nc, *args)
    r = _run(nc, [arrays], core_ids=[0])
    return r.results[0]["out"]
```

```python
import math
from contextlib import ExitStack

import numpy as np

import concourse.bass as bass
from concourse import mybir

F32 = mybir.dt.float32
F32R = mybir.dt.float32r
ACT = mybir.ActivationFunctionType
ALU = mybir.AluOpType
AX = mybir.AxisListType

P = 128
D = 2048
T = 512
TT = T // P
KT = D // P
HALF = 1024
HT = HALF // P
OFF_Q, OFF_K, OFF_V, OFF_GATE = 1024, 2048, 2176, 2304
UNIT = KT * P
GC, NS = 16, 64
L = 8
M = T // L
GP = HALF // GC // 2
GB = 8
SCAN = 7
NBLK = GP // GB
NCH, CH = 8, 64
CH_Y, CH_Z = 2, 6
PAIRS, HD = 8, 64
KEYS = 128
FB, FT = 4, 11
DK = [4, 4, 3]
NB = D // 512
EPS = 1e-6
NEG = -1e30
GELU_C = math.sqrt(2.0 / math.pi)
ROUND = 1.5 * 2.0 ** 23
TWO_PI = [6.28125, 0.0019340515136718750, 1.2556659146e-6]
KPAD = 7 * GC + L * GC

U_KV = 16
U_GATE = 18
U_GLU = 50
U_AB = 54
U_O = 70
U_FF = 86
FB_UNITS = 2 * FT + NB * len(DK)


class Chain:

    def __init__(self, eng, sem):
        self.eng, self.sem, self.base, self.n, self.saved = eng, sem, 0, 0, []

    def count(self, ins):
        ins.then_inc(self.sem, 1)
        self.n += 1

    def __call__(self, ins):
        self.count(ins)
        self.eng.wait_ge(self.sem, self.base + self.n)

    def enter(self, j, per):
        self.saved.append(self.base + self.n)
        self.base, self.n = self.saved[-1] + j * per, 0

    def leave(self, times, per):
        assert self.n == per, (self.n, per)
        self.base, self.n = self.saved.pop() + times * per, 0


def build(nc, x, norm1_g, w_in, lam_re, lam_im, log_dt, b_re, b_im, c_re, c_im, d_skip, w_glu, b_glu,
          sinks, w_a, w_b, w_o, norm2_g, w_gate, w_up, w_down, normf_g, ident_c, alibi_c,
          u_s, cout_s, kp_s, y_s, gate_s, out):
    ctx = ExitStack()
    with ctx:
        base = -(-nc.sbuf_base // 32) * 32
        end = nc.sbuf_usable_end

        def at(name, shape, kb, dt=F32):
            off = base + int(kb * 1024)
            assert off + 4 * int(np.prod(shape[1:])) <= end, name
            return nc.alloc_sbuf_tensor_at(name, shape, dt, offset=off)

        def sem(name):
            return ctx.enter_context(nc.semaphore(name))

        raw = at("raw", [P, 2, UNIT], 0)
        w_hi = at("w_hi", [P, 2, UNIT], 16, F32R)
        w_lo = at("w_lo", [P, 2, UNIT], 32, F32R)
        act_hi = at("act_hi", [P, KT, T], 48, F32R)
        act_lo = at("act_lo", [P, KT, T], 80, F32R)
        ident = at("ident", [P, P], 112)
        vec_t = at("vec_t", [P, 48], 112.5)
        b_half = at("b_half", [P, HT], 112.6875)
        stat = at("stat", [P, 4, TT], 112.71875)
        sink = at("sink", [P, PAIRS], 112.78125)
        sink_raw = at("sink_raw", [P, 2 * PAIRS], 112.9375)
        row_max = at("row_max", [P, PAIRS], 112.8125)
        neg_max = at("neg_max", [P, PAIRS], 112.84375)
        den = at("den", [P, PAIRS], 112.875)
        sink_e = at("sink_e", [P, PAIRS], 112.90625)
        vec_raw = at("vec_raw", [48, P], 113)
        ssq_p = at("ssq_p", [P, 2, TT], 113)
        a8 = at("a8", [P, 2, 2, GP], 113.5)
        A = 114
        xt = at("xt", [P, TT, D], A)
        x1 = at("x1", [P, TT, D], A)
        q_t = at("q_t", [P, PAIRS, T], A)
        cout = at("cout", [P, 2, GB, L + 1, GC], A + 16)
        tmp = at("tmp", [P, GB * (L + 1) * GC], A + 25)
        bb_pad = at("bb_pad", [P, 2, GB, 2 * GC], A + 29.5)
        k_pad = at("k_pad", [P, 2, CH + T], A + 16)
        v_t = at("v_t", [P, CH + T], A + 20.5)
        q_c = at("q_c", [P, PAIRS, CH], A + 22.75)
        k_c = at("k_c", [P, 2, KEYS], A + 24.75)
        v_ct = at("v_ct", [P, KEYS], A + 25.75)
        v_c = at("v_c", [P, P], A + 26.25)
        gate_o = at("gate_o", [P, 2, T], A + 27)
        state = at("state", [P, M, 2, GP], A + 32)
        b_sb = at("b_sb", [P, 2, GP, GC], A + 48)
        c_sb = at("c_sb", [P, 2, GP, GC], A + 52)
        powers = at("powers", [P, L + 1, 2, GP], A + 56)
        ab_f = at("ab_f", [P, 4, GP], A + 58.25)
        p_tmp = at("p_tmp", [P, 5, GP], A + 58.75)
        sc_w = at("sc_w", [P, SCAN + 1, 2, GP], A + 88)
        sc_t = at("sc_t", [P, 2, 2, GP], A + 90)
        sc_one = at("sc_one", [P, 1, 1, 1], A + 90.5)
        par = at("par", [GP, 4, 2, NS * GC], A + 60)
        lam = at("lam", [GP, 16, 2, NS], A + 32)
        dt_r = at("dt_r", [GP, 2], A + 92)
        root_t = at("root_t", [P, 1], A + 93)
        bs_t = at("bs_t", [P, 2, GP, GC], A + 64)
        bin_t = at("bin_t", [P, 2, GB, P], A + 60)
        k_row = at("k_row", [GP, GB, KPAD], A + 68)
        u2 = at("u2", [P, 2 * GB, M], A + 76)
        u_p = at("u_p", [P, 2, L, M], A + 80)
        b_in = at("b_in", [P, 2, GB, L, GC], A + 84)
        bias = at("bias", [P, PAIRS, KEYS], A + 48)
        score = at("score", [P, PAIRS, KEYS], A + 52)
        prob = at("prob", [P, PAIRS, KEYS], A + 56)
        prob_t = at("prob_t", [P, PAIRS, P], A + 60)
        cy = at("cy", [P, 2, GB, P], A + 64)
        toe = at("toe", [P, 2 * GB, P], A + 72)
        u2y = at("u2y", [P, 2 * GB, M], A + 80)
        y_sb = at("y_sb", [P, 2, GB, M], A + 84)
        st_c = at("st_c", [P, 2, GB, M], A + 88)
        swap = y_sb[:, 0]
        yb_hi = at("yb_hi", [P, HT, T], A + 32, F32R)
        yb_lo = at("yb_lo", [P, HT, T], A + 48, F32R)
        ya_hi = at("ya_hi", [P, HT, T], A, F32R)
        ya_lo = at("ya_lo", [P, HT, T], A + 16, F32R)
        zz = at("zz", [P, HT, T], A + 64)
        y_in = at("y_in", [P, 2, T], A + 80)
        u_in = at("u_in", [P, 2, T], A + 84)
        g_v = at("g_v", [P, 2, T], A + 88)
        gate_in = at("gate_in", [P, 2, 2, T], A + 80)
        mrg = at("mrg", [P, 2, T], A + 88)
        xn = at("xn", [P, TT, D], A + 32)
        m_hi = at("m_hi", [P, FT, T], A + 32, F32R)
        m_lo = at("m_lo", [P, FT, T], A + 54, F32R)
        ff_t = at("ff_t", [P, T], A + 76)
        ff_m = at("ff_m", [P, T], A + 78)
        normf = at("normf", [P, D], A + 84)
        xg = at("xg", [P, TT, D], 48)

        bank = [ctx.enter_context(nc.psum_tensor(f"bank{i}", [P, 512], F32)) for i in range(8)]

        raw_here = [sem("raw_here0"), sem("raw_here1")]
        hi_ready = sem("hi_ready")
        lo_ready = sem("lo_ready")
        units_done = sem("units_done")
        read_out = sem("read_out")
        x_here = [sem(f"x_here{t}") for t in range(TT)]
        ident_here, const_here, par_here, dt_here = (sem("ident_here"), sem("const_here"), sem("par_here"),
                                                     sem("dt_here"))
        dve_own, pool_own = sem("dve_own"), sem("pool_own")
        ssq_ready, var_ready = sem("ssq_ready"), sem("var_ready")
        root_ready, rstd_ready = sem("root_ready"), sem("rstd_ready")
        xa_ready = sem("xa_ready")
        xn_ready = sem("xn_ready")
        tr_done = sem("tr_done")
        nhi_ready, nlo_ready = sem("nhi_ready"), sem("nlo_ready")
        par_t, par_out = sem("par_t"), sem("par_out")
        dt_exp, mag_arg, mag_ready = sem("dt_exp"), sem("mag_arg"), sem("mag_ready")
        ang_ready, sin_ready, af_ready = sem("ang_ready"), sem("sin_ready"), sem("af_ready")
        vec_ready = sem("vec_ready")
        powers_ready, b_scaled = sem("powers_ready"), sem("b_scaled")
        tab_c, tab_b = sem("tab_c"), sem("tab_b")
        bint_done, bint_ready = sem("bint_done"), sem("bint_ready")
        k_done, krow_ready, krow_zero = sem("k_done"), sem("krow_ready"), sem("krow_zero")
        u_stored, u2_here, tab_stored = sem("u_stored"), sem("u2_here"), sem("tab_stored")
        x_done, state_in = sem("x_done"), sem("state_in")
        pads, kv_ev, kv_dup, bias_here = sem("pads"), sem("kv_ev"), sem("kv_dup"), sem("bias_here")
        staged, scores_done, neg_ready = sem("staged"), sem("scores_done"), sem("neg_ready")
        exps, vc_ready, prob_ready = sem("exps"), sem("vc_ready"), sem("prob_ready")
        pt_done, pt_ready, pv_done, yb_ready = sem("pt_done"), sem("pt_ready"), sem("pv_done"), sem("yb_ready")
        gate_st = [sem("gate_st0"), sem("gate_st1")]
        ytab_here, st_staged, st_here = sem("ytab_here"), sem("st_staged"), sem("st_here")
        y_done, y_ev, y_stored = sem("y_done"), sem("y_ev"), sem("y_stored")
        yin_here = [sem("yin_here0"), sem("yin_here1")]
        y_arg, y_tanh, zz_ready = sem("y_arg"), sem("y_tanh"), sem("zz_ready")
        zhi_ready, zlo_ready = sem("zhi_ready"), sem("zlo_ready")
        ybhi_ready, yblo_ready = sem("ybhi_ready"), sem("yblo_ready")
        glu_t, glu_m = sem("glu_t"), sem("glu_m")
        yahi_ready, yalo_ready = sem("yahi_ready"), sem("yalo_ready")
        gin_here = [sem("gin_here0"), sem("gin_here1")]
        mrg_ready, mhi_ready, mlo_ready = sem("mrg_ready"), sem("mhi_ready"), sem("mlo_ready")
        xres_here, normf_here = sem("xres_here"), sem("normf_here")
        tok_done = sem("tok_done")
        tok_free = sem("tok_free")
        ff_read, up_read = sem("ff_read"), sem("up_read")
        ff_tanh = sem("ff_tanh")
        ffhi_ready, fflo_ready = sem("ffhi_ready"), sem("fflo_ready")
        by_g_ready = sem("by_g_ready")
        out_ready, out_st = sem("out_ready"), sem("out_st")

        def k_rows(w):
            return w[0].rearrange("(k p) n -> p k n", p=P)

        win_v, glu_v, wa_v, wb_v = k_rows(w_in), k_rows(w_glu), k_rows(w_a), k_rows(w_b)
        wo_v, wg_v, wu_v, wd_v = k_rows(w_o), k_rows(w_gate), k_rows(w_up), k_rows(w_down)
        x_v = x[0].rearrange("(t p) n -> p t n", p=P)
        out_v = out[0].rearrange("(t p) n -> p t n", p=P)

        def slot(tile, p, width):
            return tile[:, p, :].rearrange("p (k n) -> p k n", n=width)

        def arrived(q, p):
            return 16 * q + 16

        block = ctx.enter_context(nc.Block())

        def apart(eng):
            eng.wait_ge(vec_ready, 1)

        @block.sync
        def _(sp):
            for i, v in enumerate((lam_re, lam_im)):
                sp.dma_start(lam[:, i], v[0].rearrange("(h g) p -> g h p", h=2)).then_inc(dt_here, 16)
            with nc.allow_non_contiguous_dma(reason="64 step sizes"):
                sp.dma_start(dt_r[:, :], log_dt[0].rearrange("(h g) -> g h", h=2)).then_inc(dt_here, 16)
            for t in range(TT):
                sp.dma_start(xt[:, t, :], x_v[:, t, :]).then_inc(x_here[t], 16)

            def load(u, p, src, dst, first=False):
                if not first:
                    sp.wait_ge(lo_ready, u - 1)
                sp.dma_start(dst, src).then_inc(raw_here[p], 16)

            def load_in(b, first=False):
                cols = [b * P, b * P + NBLK * P, b * (2 * P) + OFF_Q, b * (2 * P) + (OFF_Q + P)]
                for i, c in enumerate(cols):
                    load(4 * b + i, i % 2, win_v[:, :, bass.ds(c, P)], slot(raw, i % 2, P), first=first and i < 2)

            load_in(0, True)
            with sp.Fori(1, NBLK) as b:
                load_in(b)
            load(U_KV, 0, win_v[:, :, OFF_K:OFF_K + P], slot(raw, 0, P))
            load(U_KV + 1, 1, win_v[:, :, OFF_V:OFF_V + P], slot(raw, 1, P))

            def load_gates(n, y=None, first=False):
                for i in range(4):
                    load(4 * n + (U_GATE + i), i % 2, win_v[:, :, bass.ds(n * (4 * P) + (OFF_GATE + i * P), P)],
                         slot(raw, i % 2, P))
                    if y is not None and i == 2:
                        if not first:
                            sp.wait_ge(y_done, 2 * y)
                        for r in range(2):
                            sp.dma_start(cy[64 * r:64 * r + 64],
                                         cout_s[y].rearrange("(h p) r g w -> p r h g w", h=2)[:, r]
                                         ).then_inc(ytab_here, 16)
                        for r in range(L):
                            sp.dma_start(toe[16 * r:16 * r + 16],
                                         kp_s[y, :, :, :, 16 * r:16 * r + P].rearrange("c h g w -> c (h g) w")
                                         ).then_inc(ytab_here, 16)
                            sp.dma_start(u2y[16 * r:16 * r + 16, :, :],
                                         u_s[y, :, L - 1 - r, :].rearrange("(j c) m -> c j m", c=GC)
                                         ).then_inc(ytab_here, 16)

            with sp.Fori(0, CH_Y) as n:
                load_gates(n)
            sp.wait_ge(tab_stored, 16 * 3 * NBLK)
            load_gates(CH_Y, y=0, first=True)
            with sp.Fori(CH_Y + 1, CH_Z) as n:
                load_gates(n, y=n - CH_Y)
            with sp.Fori(CH_Z, NCH) as n:
                load_gates(n)
            for i in range(4):
                load(U_GLU + i, i % 2, glu_v[:, :, i * 256:(i + 1) * 256], slot(raw, i % 2, 256))
            with sp.Fori(0, 8) as j:
                for i in range(2):
                    cols = bass.ds(j * (2 * P) + i * P, P)
                    load(U_AB + 2 * j + i, i, wa_v[:, :, cols], slot(raw, i, P)[:, 0:HT])
                    sp.dma_start(slot(raw, i, P)[:, HT:KT], wb_v[:, :, cols]).then_inc(raw_here[i], 16)
            with sp.Fori(0, NB) as n:
                for i in range(4):
                    load(U_O + 4 * n + i, i % 2, wo_v[:, 4 * i:4 * i + 4, bass.ds(n * 512, 512)],
                         slot(raw, i % 2, 512))
            with sp.Fori(0, FB) as f:
                with sp.Fori(0, FT) as j:
                    for i, w in enumerate((wg_v, wu_v)):
                        load(U_FF + i + f * FB_UNITS + j * 2, i, w[:, :, bass.ds(f * (FT * P) + j * P, P)],
                             slot(raw, i, P))
                with sp.Fori(0, 2) as n:
                    for u in range(6):
                        i, e = u // 3, u % 3
                        load(U_FF + 2 * FT + u + f * FB_UNITS + n * 6, u % 2,
                             wd_v[:, bass.ds(f * FT + 4 * e, DK[e]), bass.ds(n * 1024 + i * 512, 512)],
                             slot(raw, u % 2, 512)[:, 0:DK[e]])
            sp.wait_ge(out_st, 16 * TT)

        @block.gpsimd
        def _(pool):
            own = Chain(pool, pool_own)
            pool.wait_ge(x_here[TT - 1], 16)
            for i, w in enumerate((b_re, b_im)):
                pool.dma_start(par[:, i], w[0].rearrange("(h g) p c -> g h (p c)", h=2)).then_inc(par_here, 16)
            for i, w in enumerate((c_re, c_im)):
                for h in range(2):
                    pool.dma_start(par[:, 2 + i].rearrange("g a (c h p) -> g (a c) h p", h=2, p=NS)[:, :, h],
                                   w[0, GP * h:GP * h + GP]).then_inc(par_here, 16)
            pool.wait_ge(par_out, 1)
            v = nc.gpsimd
            v.memset(powers[:, 0, 0, :], 1.0)
            v.memset(powers[:, 0, 1, :], 0.0)
            own(v.tensor_copy(powers[:, 1], ab_f[:, 0:2, :]))

            def times(dst, n, xs, ys):
                def part(x0, r):
                    return powers[:, x0:x0 + n, r, :]

                def one(r):
                    return powers[:, ys:ys + 1, r, :].to_broadcast([P, n, GP])

                t = p_tmp[:, 0:n, :]
                own(v.tensor_tensor(t, part(xs, 1), one(1), ALU.mult))
                own(v.tensor_tensor(part(dst, 0), part(xs, 0), one(0), ALU.mult))
                own(v.tensor_tensor(part(dst, 0), part(dst, 0), t, ALU.subtract))
                own(v.tensor_tensor(t, part(xs, 1), one(0), ALU.mult))
                own(v.tensor_tensor(part(dst, 1), part(xs, 0), one(1), ALU.mult))
                own(v.tensor_tensor(part(dst, 1), part(dst, 1), t, ALU.add))

            times(2, 1, 1, 1)
            times(3, 2, 1, 2)
            times(5, 4, 1, 4)
            for r in range(2):
                v.tensor_copy(a8[:, 0, r], powers[:, L, 0, :])
            v.tensor_copy(a8[:, 1, 0], powers[:, L, 1, :])
            v.tensor_tensor(a8[:, 1, 1], powers[:, 0, 1, :], powers[:, L, 1, :], ALU.subtract
                            ).then_inc(powers_ready, 1)
            pool.wait_ge(par_out, 5)
            bshape = [P, GP, GC]
            f_re = ab_f[:, 2, :].unsqueeze(2).to_broadcast(bshape)
            f_im = ab_f[:, 3, :].unsqueeze(2).to_broadcast(bshape)
            t0, t1 = bs_t[:, 0], bs_t[:, 1]
            own.count(v.tensor_tensor(t0, b_sb[:, 0], f_im, ALU.mult))
            own(v.tensor_tensor(t1, b_sb[:, 1], f_im, ALU.mult))
            own.count(v.tensor_tensor(b_sb[:, 0], b_sb[:, 0], f_re, ALU.mult))
            own(v.tensor_tensor(b_sb[:, 1], b_sb[:, 1], f_re, ALU.mult))
            own(v.tensor_tensor(b_sb[:, 0], b_sb[:, 0], t1, ALU.subtract))
            v.tensor_tensor(b_sb[:, 1], b_sb[:, 1], t0, ALU.add).then_inc(b_scaled, 1)
            pool.memset(k_row[:, :, 0:7 * GC], 0.0).then_inc(krow_zero, 1)

            with pool.Fori(0, NBLK) as b:
                for i in range(2):
                    pool.wait_ge(read_out, 4 * b + (i + 3))
                    apart(pool)
                    pool.dma_start(u_s[b, i * P:(i + 1) * P], u_p[:, i]).then_inc(u_stored, 16)
                pool.wait_ge(u_stored, 32 * b + 32)
                pool.wait_ge(units_done, 4 * b + 3)
                apart(pool)
                for r in range(L):
                    pool.dma_start(u2[16 * r:16 * r + 16, :, :],
                                   u_s[b, :, L - 1 - r, :].rearrange("(j c) m -> c j m", c=GC)).then_inc(u2_here, 16)
                pool.wait_ge(tab_c, b + 1)
                apart(pool)
                pool.dma_start(cout_s[b].rearrange("p r g (l c) -> p (r g) (l c)", c=GC),
                               cout[:, :, :, 1:, :].rearrange("p r g l c -> p (r g) (l c)")).then_inc(tab_stored, 16)
                pool.wait_ge(krow_ready, 2 * b + 2)
                apart(pool)
                for h in range(2):
                    pool.dma_start(kp_s[b, :, h], k_row[16 * h:16 * h + 16]).then_inc(tab_stored, 16)

            pool.wait_ge(state_in, 2 * NBLK)
            pool.wait_ge(powers_ready, 1)
            def copy(dst, src):
                shape = [P] + [int(n) for n in dst.shape[1:]]
                return pool.tensor_tensor(dst, src, sc_one[:, :, :, :].to_broadcast(shape), ALU.mult)

            own(pool.memset(sc_one[:, :, :, :], 1.0))
            own(copy(sc_w[:, 0:1], state[:, 0:1]))
            with pool.Fori(0, (M - 1) // SCAN) as m:
                own.enter(m, 3 * SCAN + 3)
                apart(pool)
                own(copy(sc_w[:, 1:], state[:, bass.ds(m * SCAN + 1, SCAN)]))
                for i in range(SCAN):
                    prev, cur = sc_w[:, i], sc_w[:, i + 1]
                    own(pool.tensor_tensor(sc_t[:, :], prev.unsqueeze(1).to_broadcast([P, 2, 2, GP]), a8[:, :],
                                           ALU.mult))
                    own(pool.tensor_tensor(cur, cur, sc_t[:, 0], ALU.add))
                    own(pool.tensor_tensor(cur, cur, sc_t[:, 1, ::-1, :], ALU.add))
                own.count(copy(sc_w[:, 0:1], sc_w[:, SCAN:]))
                own(copy(state[:, bass.ds(m * SCAN + 1, SCAN)], sc_w[:, 1:]))
                own.leave((M - 1) // SCAN, 3 * SCAN + 3)
            own(pool.memset(st_c[:, :, :, 0:1], 0.0))
            with pool.Fori(0, NBLK) as b:
                pool.wait_ge(units_done, 4 * b + (2 + U_GATE + 4 * CH_Y))
                apart(pool)
                for h in range(2):
                    rows = slice(64 * h, 64 * h + 64)
                    for r in range(2):
                        pool.tensor_copy((st_c[rows, h] if r == h else swap[rows])[:, :, 1:M],
                                         state[rows, 0:M - 1, r, bass.ds(b * GB, GB)].rearrange("p m g -> p g m")
                                         ).then_inc(st_staged, 1)
                pool.wait_ge(y_stored, 128 * b + 128)

            pool.wait_ge(zz_ready, HT)
            for i in range(2):
                pool.wait_ge(gate_st[i], 16 * 16)
            for i in range(2):
                for e in range(2):
                    pool.dma_start(gate_in[:, i, e, :], gate_s[16 * e + i]).then_inc(gin_here[i], 16)
            with pool.Fori(1, 8) as j:
                for i in range(2):
                    pool.wait_ge(mrg_ready, 2 * j + i - 1)
                    apart(pool)
                    for e in range(2):
                        pool.dma_start(gate_in[:, i, e, :], gate_s[2 * j + (16 * e + i)]).then_inc(gin_here[i], 16)
            for t in range(TT):
                pool.wait_ge(units_done, 2 + U_O + t)
                pool.dma_start(x1[:, t, :], x_v[:, t, :]).then_inc(xres_here, 16)
            pool.wait_ge(mlo_ready, KT)
            pool.dma_start(normf[:, :], normf_g.partition_broadcast(P)).then_inc(normf_here, 16)
            pool.wait_ge(normf_here, 16)
            for n in range(NB):
                cols = slice(512 * n, 512 * n + 512)
                for t in range(TT):
                    pool.wait_ge(tok_free, 4 + NB * TT * FB + TT * n + t + 1)
                    pool.tensor_tensor(xg[:, t, cols], x1[:, t, cols], normf[:, cols], ALU.mult
                                       ).then_inc(by_g_ready, 1)

        @block.scalar
        def _(act):
            run = nc.scalar.activation

            def hi(q, p, here, n=UNIT):
                act.wait_ge(raw_here[p], here)
                act.wait_ge(units_done, 2 * q + (p + 1))
                run(w_hi[:, p, 0:n], raw[:, p, 0:n], ACT.Copy).then_inc(hi_ready, 1)

            def unit_done(q, p):
                act.wait_ge(units_done, 2 * q + (p + 3))

            def root_table(x_):
                run(root_t[0:x_.shape[0], :], x_, ACT.Sqrt)

            def square(src, t, cols, scratch, sums):
                run(scratch, src[:, t, cols], ACT.Square, accum_out=sums[:, t:t + 1]).then_inc(ssq_ready, 1)

            def early_squares(c, src, scratch):
                root_table(stat[:, 1, 0:1])
                for t in range(TT):
                    act.wait_ge(tok_free, 4 + NB * TT * (FB if c == 2 else 0) + TT * (NB - 2) + t + 1)
                    square(src, t, slice(0, D - 512), scratch[:, t, 0:D - 512], ssq_p[:, 0])

            def norm_tile(c, t, dst, done):
                act.wait_ge(ssq_ready, TT * 2 * c + t + 1)
                act.wait_ge(var_ready, TT * (c + 1))
                run(stat[:, 2, t:t + 1], ssq_p[:, 1, t:t + 1], ACT.Sqrt, scale=1.0 / D, bias=stat[:, 1, t:t + 1]
                    ).then_inc(root_ready, 1)
                act.wait_ge(rstd_ready, TT * c + t + 1)
                src = x1 if c == 1 else dst
                if c == 2:
                    act.wait_ge(by_g_ready, NB * TT - TT + t + 1)
                run(dst[:, t, HALF:], src[:, t, HALF:], ACT.Copy, scale=stat[:, 3, t:t + 1]).then_inc(done, 1)

            def transposed(c, g0, q, here):
                for k in range(KT):
                    act.wait_ge(tr_done, c * KT + k + 1)
                    run(act_hi[:, k, :], bank[1 + k % 7][:, :], ACT.Copy, scale=vec_t[:, g0 + k:g0 + k + 1]
                        ).then_inc(nhi_ready, 1)
                    if k == KT // 2:
                        hi(q, 1, here)

            scratch = act_lo[:, :, :].rearrange("p (t k) n -> p t (k n)", t=TT)
            act.dma_start(ident[:, :], ident_c[:, :]).then_inc(ident_here, 16)
            for r0, v, n in ((0, norm1_g[0], KT), (16, norm2_g[0], KT),
                             (32, d_skip[0].rearrange("g c -> (g c)"), HT), (40, b_glu[0], HT)):
                act.dma_start(vec_raw[r0:r0 + n, :], v.rearrange("(k p) -> k p", p=P)).then_inc(const_here, 16)
            act.dma_start(sink_raw[:, :], sinks[0].partition_broadcast(P)).then_inc(const_here, 16)
            act.wait_ge(dt_here, 48)
            run(dt_r[:, :], dt_r[:, :], ACT.Exp).then_inc(dt_exp, 1)
            act.wait_ge(mag_arg, 1)
            run(lam[:, 2], lam[:, 2], ACT.Exp).then_inc(mag_ready, 1)
            act.wait_ge(ang_ready, 1)
            run(lam[:, 5], lam[:, 4], ACT.Sin, scale=0.5)
            run(lam[:, 6], lam[:, 4], ACT.Sin).then_inc(sin_ready, 1)
            act.wait_ge(mag_ready, 1)
            root_table(lam[:, 2, 0, 0:1])
            for t in range(TT):
                act.wait_ge(x_here[t], 16)
                square(xt, t, slice(0, D), scratch[:, t], stat[:, 0])
            act.wait_ge(var_ready, TT)
            run(stat[:, 2, :], stat[:, 1, :], ACT.Sqrt).then_inc(root_ready, TT)
            act.wait_ge(rstd_ready, TT)
            for t in (2, 3):
                run(xt[:, t, HALF:], xt[:, t, HALF:], ACT.Copy, scale=stat[:, 3, t:t + 1]).then_inc(xn_ready, 1)
            hi(0, 0, arrived(0, 0))
            act.wait_ge(vec_ready, 1)
            run(b_half[:, :], vec_t[:, 40:48], ACT.Copy, scale=0.5).then_inc(read_out, 2)
            transposed(0, 0, 0, arrived(0, 1))

            def mixer_inputs(b, first):
                def step(i):
                    if not (first and i == 0):
                        hi(2 * b + (i + 1) // 2, (i + 1) % 2, arrived(2 * b + (i + 1) // 2, 0))
                    unit_done(2 * b + i // 2, i % 2)

                for i in range(2):
                    step(i)
                    if first and i == 0:
                        for e in (2, 3, 0, 1):
                            act.wait_ge(par_t, 2 + (e + 2) % 4)
                            run((b_sb if e < 2 else c_sb)[:, e % 2].rearrange("p g c -> p c g"),
                                bank[2 + e][:, :].rearrange("p (c g) -> p c g", g=GP), ACT.Copy).then_inc(par_out, 1)
                    run(u_p[:, i].rearrange("p s m -> p m s"), bank[i][:, :].rearrange("p (m s) -> p m s", s=L),
                        ACT.Copy).then_inc(read_out, 1)
                step(2)
                run(q_t[:, 2 * b, :], bank[0][:, :], ACT.Copy).then_inc(read_out, 1)
                for e in range(4):
                    act.wait_ge(bint_done, 4 * b + (e + 1))
                    run(bin_t[:, e // 2, 4 * (e % 2):4 * (e % 2) + 4, :],
                        bank[2 + e][:, :].rearrange("p (g w) -> p g w", w=P), ACT.Copy).then_inc(bint_ready, 1)
                act.wait_ge(k_done, b + 1)
                if first:
                    act.wait_ge(krow_zero, 1)
                else:
                    act.wait_ge(tab_stored, 48 * b)
                for e in range(2):
                    run(k_row[:, 4 * e:4 * e + 4, 7 * GC:], bank[6 + e][0:GP, :].rearrange("p (g w) -> p g w", w=P),
                        ACT.Copy).then_inc(krow_ready, 1)
                step(3)
                run(q_t[:, 2 * b + 1, :], bank[1][:, :], ACT.Copy).then_inc(read_out, 1)
                act.wait_ge(x_done, b + 1)
                for r in range(2):
                    run(state[:, :, r, bass.ds(b * GB, GB)].rearrange("p m g -> p g m"),
                        bank[2 + r][:, :].rearrange("p (g m) -> p g m", m=M), ACT.Copy).then_inc(state_in, 1)

            mixer_inputs(0, True)
            with act.Fori(1, NBLK) as b:
                mixer_inputs(b, False)

            hi(8, 1, arrived(8, 1))
            unit_done(8, 0)
            act.wait_ge(pads, 1)
            run(k_pad[0:64, 0, CH:], bank[0][0:64, :], ACT.Copy).then_inc(kv_ev, 1)
            run(k_pad[64:P, 1, CH:], bank[0][64:P, :], ACT.Copy).then_inc(read_out, 1)
            act.wait_ge(kv_ev, 1)
            act.wait_ge(read_out, U_KV + 3)
            act.dma_start(k_pad[64:P, 0, CH:], k_pad[0:64, 0, CH:]).then_inc(kv_dup, 16)
            act.dma_start(k_pad[0:64, 1, CH:], k_pad[64:P, 1, CH:]).then_inc(kv_dup, 16)
            act.dma_start(bias[:, :, :], alibi_c[:, :, :]).then_inc(bias_here, 16)
            hi(9, 0, arrived(9, 0))
            unit_done(8, 1)
            run(v_t[:, CH:], bank[1][:, :], ACT.Copy).then_inc(read_out, 1)

            def load_y(t):
                h, b = t // NBLK, t % NBLK
                if t == 0:
                    act.wait_ge(y_stored, 16 * L * NBLK)
                elif t >= 2:
                    act.wait_ge(zz_ready, t - 1)
                for dst, src in ((y_in, y_s), (u_in, u_s)):
                    act.dma_start(dst[:, t % 2, :], src[b, h * P:(h + 1) * P].rearrange("c t m -> c (t m)")
                                  ).then_inc(yin_here[t % 2], 16)

            def z_hi(tiles):
                for n in tiles:
                    act.wait_ge(zz_ready, n + 1)
                    run(act_hi[:, n, :], zz[:, n, :], ACT.Copy, scale=0.5).then_inc(zhi_ready, 1)

            def gates(n, first=False, y=None, z=None):
                q0 = 2 * n + U_GATE // 2

                def ahead(i):
                    hi(q0 + (i + 1) // 2, (i + 1) % 2, arrived(q0 + (i + 1) // 2, 0))

                def gate(i):
                    if i != 1:
                        ahead(i)
                    if y is not None and i == 1:
                        act.wait_ge(st_staged, 4 * y + 4)
                        for h in range(2):
                            act.dma_start(st_c[64 - 64 * h:P - 64 * h, h, :, 1:M], swap[64 * h:64 * h + 64, :, 1:M]
                                          ).then_inc(st_here, 16)
                    if y is not None and i >= 2:
                        y_part(y, i - 2)
                    if z is not None:
                        if z + i == 0:
                            load_y(0)
                        if z + i + 1 < HT:
                            load_y(z + i + 1)
                    unit_done(q0 + i // 2, i % 2)
                    if z == HT - 4 and i == 3:
                        z_hi((0, 1))
                    if not (first and i < 2):
                        act.wait_ge(gate_st[i % 2], 32 * n + 16 * (i // 2))
                    run(gate_o[:, i % 2, :], bank[i % 2][:, :], ACT.Tanh, scale=0.5).then_inc(read_out, 1)
                    act.wait_ge(read_out, 4 * n + (U_GATE + i + 3))
                    act.dma_start(gate_s[4 * n + i], gate_o[:, i % 2, :]).then_inc(gate_st[i % 2], 16)
                    if z is not None:
                        act.wait_ge(y_arg, z + i + 1)
                        run(g_v[:, i % 2, :], g_v[:, i % 2, :], ACT.Tanh, scale=GELU_C).then_inc(y_tanh, 1)

                gate(0)
                act.wait_ge(scores_done, n + 1)
                run(v_c[:, :], bank[6][:, 0:P], ACT.Copy).then_inc(vc_ready, 1)
                ahead(1)
                act.wait_ge(neg_ready, n + 1)
                for j in range(PAIRS):
                    run(prob[:, j, :], score[:, j, :], ACT.Exp, bias=neg_max[:, j:j + 1], accum_out=den[:, j:j + 1])
                run(sink_e[:, :], sink_e[:, :], ACT.Exp).then_inc(exps, 1)
                gate(1)
                gate(2)
                for e in range(2):
                    act.wait_ge(pt_done, 2 * n + (e + 1))
                    run(prob_t[:, 4 * e:4 * e + 4, :], bank[4 + e][:, :].rearrange("p (j w) -> p j w", w=P), ACT.Copy
                        ).then_inc(pt_ready, 1)
                gate(3)

            def y_part(b, h):
                act.wait_ge(y_done, 2 * b + (h + 1))
                run(y_sb[:, h], bank[7][:, :].rearrange("p (g m) -> p g m", m=M), ACT.Copy).then_inc(y_ev, 1)
                if h == 1:
                    act.wait_ge(y_ev, 2 * b + 2)
                    for t in range(L):
                        act.dma_start(y_s[b, :, t, :].rearrange("(j c) m -> c j m", c=GC),
                                      y_sb[16 * t:16 * t + 16].rearrange("p h g m -> p (h g) m")
                                      ).then_inc(y_stored, 16)

            gates(0, first=True)
            with act.Fori(1, CH_Y) as n:
                gates(n)
            with act.Fori(CH_Y, CH_Z) as n:
                gates(n, y=n - CH_Y)
            for n in range(CH_Z, NCH):
                gates(n, z=4 * (n - CH_Z))

            z_hi(range(2, HT))
            hi(U_GLU // 2, 1, arrived(U_GLU // 2, 1))
            act.wait_ge(yb_ready, NCH)
            for e in range(2):
                run(yb_hi[:, 4 * e:4 * e + 4, :], q_t[:, 4 * e:4 * e + 4, :], ACT.Copy).then_inc(ybhi_ready, 1)
            for i in range(2):
                act.wait_ge(gate_st[i], 16 * 16)
            for i in range(4):
                u = U_GLU + i
                if i > 0:
                    hi((u + 1) // 2, (u + 1) % 2, arrived((u + 1) // 2, 0) + (16 if u + 1 == U_AB else 0))
                unit_done(u // 2, u % 2)
                for e in range(2):
                    n = 2 * i + e
                    if i > 0:
                        act.wait_ge(yalo_ready, n - 1)
                    run(g_v[:, e, :], bank[2 * e + i % 2][:, :], ACT.Tanh, scale=0.5, bias=b_half[:, n:n + 1]
                        ).then_inc(read_out if e else glu_t, 1)
                for e in range(2):
                    n = 2 * i + e
                    act.wait_ge(glu_m, n + 1)
                    run(ya_hi[:, n, :], g_v[:, e, :], ACT.Copy, scale=0.25).then_inc(yahi_ready, 1)

            def merge(j, last=False):
                q = U_AB // 2 + j
                for i in range(2):
                    if i == 0:
                        hi(q, 1, 32 * j + (arrived(U_AB // 2, 1) + 16))
                    elif last:
                        hi(q + 1, 0, arrived(q + 1, 0) + 128)
                    else:
                        hi(q + 1, 0, 32 * j + (arrived(U_AB // 2, 0) + 48))
                    act.wait_ge(mrg_ready, 2 * j + (i + 1))
                    run(act_hi[:, 2 * j + i, :], mrg[:, i, :], ACT.Copy, scale=0.5).then_inc(mhi_ready, 1)

            with act.Fori(0, 7) as j:
                merge(j)
            merge(7, last=True)

            def here(q):
                return 16 * q + (16 + 128)

            def out_block(n, last=False):
                for i in range(4):
                    q = 2 * n + (U_O + i + 1) // 2
                    hi(q, (i + 1) % 2, here(q))
                    if last and i == 2:
                        early_squares(1, x1, xn)

            with act.Fori(0, NB - 1) as n:
                out_block(n)
            out_block(NB - 1, last=True)
            for t in range(TT):
                act.wait_ge(tok_free, 4 + (NB - 1) * TT + t + 1)
                square(x1, t, slice(D - 512, D), xn[:, t, D - 512:], ssq_p[:, 1])
                norm_tile(1, t, xn, xn_ready)
            transposed(1, KT, U_FF // 2, here(U_FF // 2))

            def ff_block(f, first=False, last=False):
                q0 = f * (FB_UNITS // 2) + U_FF // 2

                def tiles(j, first=False):
                    if not first:
                        hi(q0 + j, 1, here(q0 + j))
                    unit_done(q0 + j, 0)
                    run(ff_t[:, :], bank[0][:, :], ACT.Tanh, scale=0.5).then_inc(ff_tanh, 1)
                    hi(q0 + j + 1, 0, here(q0 + j + 1))
                    act.wait_ge(up_read, f * FT + j + 2)
                    run(m_hi[:, j, :], ff_m[:, :], ACT.Copy, scale=0.5).then_inc(ffhi_ready, 1)

                if first:
                    tiles(0, first=True)
                with act.Fori(1 if first else 0, FT) as j:
                    tiles(j)

                def down(n, very_last=False):
                    for u in range(6):
                        if not (very_last and u == 5):
                            q = q0 + FT + 3 * n + (u + 1) // 2
                            full = u % 3 != 1
                            hi(q, (u + 1) % 2, here(q), UNIT if full else DK[2] * 512)
                        if very_last and u == 2:
                            early_squares(2, x1, scratch)

                if last:
                    down(0)
                    down(1, True)
                else:
                    with act.Fori(0, 2) as n:
                        down(n)

            ff_block(0, first=True)
            with act.Fori(1, FB - 1) as f:
                ff_block(f)
            ff_block(FB - 1, last=True)
            for t in range(TT):
                act.wait_ge(tok_free, 4 + NB * TT * (FB + 1) - TT + t + 1)
                square(x1, t, slice(D - 512, D), scratch[:, t, D - 512:], ssq_p[:, 1])
                norm_tile(2, t, xg, out_ready)
                act.wait_ge(out_ready, 2 * t + 2)
                act.dma_start(out_v[:, t, :], xg[:, t, :]).then_inc(out_st, 16)

        @block.vector
        def _(dve):
            v = nc.vector
            own = Chain(dve, dve_own)

            def lo(u, p, n=UNIT):
                dve.wait_ge(hi_ready, u + 1)
                v.tensor_tensor(w_lo[:, p, 0:n], raw[:, p, 0:n], w_hi[:, p, 0:n].bitcast(F32), ALU.subtract
                                ).then_inc(lo_ready, 1)

            def transposed(c, g0, u):
                for k in range(KT):
                    dve.wait_ge(nhi_ready, c * KT + k + 1)
                    v.scalar_tensor_tensor(act_lo[:, k, :], bank[1 + k % 7][:, :], vec_t[:, g0 + k:g0 + k + 1],
                                           act_hi[:, k, :].bitcast(F32), ALU.mult, ALU.subtract
                                           ).then_inc(nlo_ready, 1)
                    if k == KT // 2:
                        lo(u, 1)

            def early_var(c):
                dve.wait_ge(ssq_ready, TT * 2 * c)
                v.tensor_scalar(stat[:, 1, :], ssq_p[:, 0, :], 1.0 / D, EPS, ALU.mult, ALU.add
                                ).then_inc(var_ready, TT)

            def norm_tile(c, t, dst, done):
                dve.wait_ge(root_ready, TT * c + t + 1)
                v.reciprocal(stat[:, 3, t:t + 1], stat[:, 2, t:t + 1]).then_inc(rstd_ready, 1)
                dve.wait_ge(rstd_ready, TT * c + t + 1)
                src = x1 if c == 1 else dst
                v.tensor_scalar(dst[:, t, 0:HALF], src[:, t, 0:HALF], stat[:, 3, t:t + 1], None, ALU.mult
                                ).then_inc(done, 1)

            dve.wait_ge(dt_here, 48)
            dve.wait_ge(dt_exp, 1)
            for h in range(2):
                v.tensor_scalar(lam[:, 3, h], lam[:, 1, h], dt_r[:, h:h + 1], None, ALU.mult)
            for h in range(2):
                ins = v.tensor_scalar(lam[:, 2, h], lam[:, 0, h], dt_r[:, h:h + 1], None, ALU.mult)
            ins.then_inc(mag_arg, 1)
            dve.wait_ge(mag_arg, 1)
            own(v.tensor_scalar(lam[:, 4], lam[:, 3], 1.0 / (2.0 * math.pi), ROUND, ALU.mult, ALU.add))
            own(v.tensor_scalar(lam[:, 7], lam[:, 4], -ROUND, None, ALU.add))
            for part in TWO_PI:
                own(v.scalar_tensor_tensor(lam[:, 3], lam[:, 7], -part, lam[:, 3], ALU.mult, ALU.add))
            v.tensor_scalar(lam[:, 4], lam[:, 3], 3.1415925, -3.1415925, ALU.min, ALU.max).then_inc(ang_ready, 1)
            dve.wait_ge(sin_ready, 1)
            dve.wait_ge(mag_ready, 1)
            own(v.tensor_tensor(lam[:, 7], lam[:, 5], lam[:, 5], ALU.mult))
            own(v.tensor_scalar(lam[:, 7], lam[:, 7], -2.0, 1.0, ALU.mult, ALU.add))
            own(v.tensor_tensor(lam[:, 8], lam[:, 2], lam[:, 7], ALU.mult))
            own(v.tensor_tensor(lam[:, 9], lam[:, 2], lam[:, 6], ALU.mult))
            own(v.tensor_scalar(lam[:, 3], lam[:, 8], -1.0, None, ALU.add))
            own(v.tensor_tensor(lam[:, 4], lam[:, 0], lam[:, 0], ALU.mult))
            own(v.tensor_tensor(lam[:, 5], lam[:, 1], lam[:, 1], ALU.mult))
            own(v.tensor_tensor(lam[:, 4], lam[:, 4], lam[:, 5], ALU.add))
            own(v.reciprocal(lam[:, 12], lam[:, 4]))
            for out_, (i0, i1), (i2, i3), op in ((10, (3, 0), (9, 1), ALU.add), (11, (9, 0), (3, 1), ALU.subtract)):
                own(v.tensor_tensor(lam[:, 5], lam[:, i0], lam[:, i1], ALU.mult))
                own(v.tensor_tensor(lam[:, 6], lam[:, i2], lam[:, i3], ALU.mult))
                own(v.tensor_tensor(lam[:, 7], lam[:, 5], lam[:, 6], op))
                ins = v.tensor_tensor(lam[:, out_], lam[:, 7], lam[:, 12], ALU.mult)
                if out_ == 10:
                    own(ins)
            ins.then_inc(af_ready, 1)
            dve.wait_ge(par_t, 1)
            v.tensor_copy(ab_f[:, :, :], bank[0][:, 0:4 * GP].rearrange("p (k g) -> p k g", g=GP)).then_inc(par_out, 1)
            dve.wait_ge(units_done, 2)
            v.tensor_copy(vec_t[:, :], bank[7][:, 0:48]).then_inc(vec_ready, 1)
            dve.wait_ge(const_here, 80)
            for e in range(2):
                v.tensor_copy(sink[64 * e:64 * e + 64, :], sink_raw[64 * e:64 * e + 64, e::2])
            dve.wait_ge(ssq_ready, TT)
            v.tensor_scalar(stat[:, 1, :], stat[:, 0, :], 1.0 / D, EPS, ALU.mult, ALU.add).then_inc(var_ready, TT)
            dve.wait_ge(root_ready, TT)
            v.reciprocal(stat[:, 3, :], stat[:, 2, :]).then_inc(rstd_ready, TT)
            dve.wait_ge(rstd_ready, TT)
            for t in range(TT):
                v.tensor_scalar(xt[:, t, 0:HALF], xt[:, t, 0:HALF], stat[:, 3, t:t + 1], None, ALU.mult
                                ).then_inc(xa_ready, 1)
            for t in (0, 1):
                v.tensor_scalar(xt[:, t, HALF:], xt[:, t, HALF:], stat[:, 3, t:t + 1], None, ALU.mult
                                ).then_inc(xn_ready, 1)
            lo(0, 0)
            dve.wait_ge(vec_ready, 1)
            transposed(0, 0, 1)

            own(v.memset(bb_pad[:, :, :, :], 0.0))

            def tables(b, first):
                def blk(tile, r):
                    return tile[:, r, bass.ds(b * GB, GB), :]

                def pw(r, l0, n):
                    return powers[:, l0:l0 + n, r, bass.ds(b * GB, GB)].rearrange("p l g -> p g l")

                def product(out_, a, ar, pr, n, l0):
                    shape = [P, GB, n, GC]
                    return v.tensor_tensor(out_, blk(a, ar).unsqueeze(2).to_broadcast(shape),
                                           pw(pr, l0, n).unsqueeze(3).to_broadcast(shape), ALU.mult)

                if not first:
                    lo(4 * b + 1, 1)
                if first:
                    dve.wait_ge(par_out, 5)
                    dve.wait_ge(powers_ready, 1)
                else:
                    dve.wait_ge(k_done, b)
                    dve.wait_ge(tab_stored, 48 * b)
                    apart(dve)
                ct = tmp[:, :].rearrange("p (g l c) -> p g l c", l=L + 1, c=GC)
                own(product(ct, c_sb, 1, 1, L + 1, 0))
                own(product(cout[:, 0], c_sb, 0, 0, L + 1, 0))
                own(v.tensor_tensor(cout[:, 0], cout[:, 0], ct, ALU.subtract))
                own(product(ct, c_sb, 1, 0, L + 1, 0))
                own(product(cout[:, 1], c_sb, 0, 1, L + 1, 0))
                v.scalar_tensor_tensor(cout[:, 1].rearrange("p g l c -> p (g l c)"),
                                       cout[:, 1].rearrange("p g l c -> p (g l c)"), -1.0, tmp[:, :],
                                       ALU.mult, ALU.subtract).then_inc(tab_c, 1)
                lo(4 * b + 2, 0)
                bt = tmp[:, 0:GB * L * GC].rearrange("p (g l c) -> p g l c", l=L, c=GC)
                dve.wait_ge(tab_c, b + 1)
                if first:
                    dve.wait_ge(b_scaled, 1)
                for h in range(2):
                    rows = slice(64 * h, 64 * h + 64)
                    for r in range(2):
                        v.tensor_copy(bb_pad[rows, r, :, GC * h:GC * h + GC], b_sb[rows, r, bass.ds(b * GB, GB), :])
                own(product(bt, b_sb, 1, 1, L, 0))
                own(product(b_in[:, 0], b_sb, 0, 0, L, 0))
                own(v.tensor_tensor(b_in[:, 0], b_in[:, 0], bt, ALU.subtract))
                own(product(bt, b_sb, 1, 0, L, 0))
                own(product(b_in[:, 1], b_sb, 0, 1, L, 0))
                v.tensor_tensor(b_in[:, 1], b_in[:, 1], bt, ALU.add).then_inc(tab_b, 1)
                lo(4 * b + 3, 1)
                lo(4 * b + 4, 0)

            tables(0, True)
            with dve.Fori(1, NBLK) as b:
                own.enter(b - 1, 10)
                tables(b, False)
                own.leave(NBLK - 1, 10)

            lo(U_KV + 1, 1)
            dve.wait_ge(units_done, 2 + U_KV)
            dve.wait_ge(tab_stored, 16 * 3 * NBLK)
            v.memset(v_t[:, 0:CH], 0.0)
            v.memset(k_pad[:, :, 0:CH], 0.0).then_inc(pads, 1)
            lo(U_KV + 2, 0)
            dve.wait_ge(bias_here, 16)
            dve.wait_ge(kv_dup, 32)
            dve.wait_ge(read_out, U_GATE + 2)

            def gelu_arg(t):
                i = t % 2
                dve.wait_ge(yin_here[i], 32 * (t // 2 + 1))
                own(v.scalar_tensor_tensor(y_in[:, i, :], u_in[:, i, :], vec_t[:, 32 + t:33 + t], y_in[:, i, :],
                                           ALU.mult, ALU.add))
                own(v.tensor_tensor(g_v[:, i, :], y_in[:, i, :], y_in[:, i, :], ALU.mult))
                own(v.tensor_scalar(g_v[:, i, :], g_v[:, i, :], 0.044715, 1.0, ALU.mult, ALU.add))
                v.tensor_tensor(g_v[:, i, :], g_v[:, i, :], y_in[:, i, :], ALU.mult).then_inc(y_arg, 1)

            def gelu(t):
                i = t % 2
                dve.wait_ge(y_tanh, t + 1)
                v.scalar_tensor_tensor(zz[:, t, :].rearrange("p (m t) -> p t m", t=L),
                                       g_v[:, i, :].rearrange("p (t m) -> p t m", t=L), 1.0,
                                       y_in[:, i, :].rearrange("p (t m) -> p t m", t=L), ALU.add, ALU.mult
                                       ).then_inc(zz_ready, 1)

            def z_lo(tiles):
                for n in tiles:
                    dve.wait_ge(zhi_ready, n + 1)
                    v.scalar_tensor_tensor(act_lo[:, n, :], zz[:, n, :], 0.5, act_hi[:, n, :].bitcast(F32),
                                           ALU.mult, ALU.subtract).then_inc(zlo_ready, 1)

            def attend(n, first=False, z=None):
                u0 = 4 * n + U_GATE

                def lo_gelu(i):
                    lo(u0 + i + 1, (i + 1) % 2)
                    if z is not None:
                        if i > 0:
                            gelu(z + i - 1)
                        gelu_arg(z + i)

                v.tensor_scalar(q_c[:, :, :], q_t[:, :, bass.ds(n * CH, CH)], HD ** -0.5, None, ALU.mult)
                v.tensor_copy(k_c[:, :, :], k_pad[:, :, bass.ds(n * CH, KEYS)])
                v.tensor_copy(v_ct[:, :], v_t[:, bass.ds(n * CH, KEYS)]).then_inc(staged, 1)
                lo_gelu(0)
                dve.wait_ge(scores_done, n + 1)
                for e in range(2):
                    own(v.tensor_tensor(score[:, 4 * e:4 * e + 4, :],
                                        bank[2 + e][:, :].rearrange("p (j w) -> p j w", w=KEYS),
                                        bias[:, 4 * e:4 * e + 4, :], ALU.add))
                if first:
                    own(v.memset(score[:, :, 0:CH], NEG))
                own(v.tensor_reduce(row_max[:, :], score[:, :, :], AX.X, ALU.max))
                own(v.tensor_tensor(row_max[:, :], row_max[:, :], sink[:, :], ALU.max))
                own(v.tensor_tensor(sink_e[:, :], sink[:, :], row_max[:, :], ALU.subtract))
                v.tensor_scalar(neg_max[:, :], row_max[:, :], -1.0, None, ALU.mult).then_inc(neg_ready, 1)
                lo_gelu(1)
                dve.wait_ge(exps, n + 1)
                own(v.tensor_tensor(den[:, :], den[:, :], sink_e[:, :], ALU.add))
                own(v.reciprocal(den[:, :], den[:, :]))
                v.tensor_tensor(prob[:, :, :], prob[:, :, :], den[:, :].unsqueeze(2).to_broadcast([P, PAIRS, KEYS]),
                                ALU.mult).then_inc(prob_ready, 1)
                lo_gelu(2)
                lo_gelu(3)
                if z == HT - 4:
                    z_lo((0, 1))
                dve.wait_ge(pv_done, n + 1)
                v.tensor_scalar(q_t[:, :, bass.ds(n * CH, CH)], bank[6][:, :].rearrange("p (j w) -> p j w", w=CH),
                                1.0, None, ALU.mult).then_inc(yb_ready, 1)
                if z is not None:
                    gelu(z + 3)

            attend(0, True)
            with dve.Fori(1, CH_Z) as n:
                own.enter(n - 1, 7)
                attend(n)
                own.leave(CH_Z - 1, 7)
            for n in range(CH_Z, NCH):
                attend(n, z=4 * (n - CH_Z))

            z_lo(range(2, HT))
            lo(U_GLU + 1, 1)
            for e in range(2):
                dve.wait_ge(ybhi_ready, e + 1)
                part = slice(4 * e, 4 * e + 4)
                v.tensor_tensor(yb_lo[:, part, :], q_t[:, part, :], yb_hi[:, part, :].bitcast(F32), ALU.subtract
                                ).then_inc(yblo_ready, 1)
            for i in range(2):
                dve.wait_ge(gate_st[i], 16 * 16)
            for i in range(4):
                u = U_GLU + i
                if i > 0:
                    lo(u + 1, (u + 1) % 2)
                for e in range(2):
                    n = 2 * i + e
                    if e == 0:
                        dve.wait_ge(glu_t, i + 1)
                    else:
                        dve.wait_ge(read_out, u + 3)
                    v.scalar_tensor_tensor(g_v[:, e, :], g_v[:, e, :], 1.0, zz[:, n, :], ALU.add, ALU.mult
                                           ).then_inc(glu_m, 1)
                for e in range(2):
                    n = 2 * i + e
                    dve.wait_ge(yahi_ready, n + 1)
                    v.scalar_tensor_tensor(ya_lo[:, n, :], g_v[:, e, :], 0.25, ya_hi[:, n, :].bitcast(F32),
                                           ALU.mult, ALU.subtract).then_inc(yalo_ready, 1)
            v.memset(stat[:, 2, :], 0.0).then_inc(tok_free, TT)
            with dve.Fori(0, 8) as j:
                own.enter(j, 2)
                for i in range(2):
                    u = 2 * j + (U_AB + i)
                    lo(u + 1, (i + 1) % 2)
                    dve.wait_ge(gin_here[i], 32 * j + 32)
                    dve.wait_ge(units_done, u + 3)
                    own(v.scalar_tensor_tensor(mrg[:, i, :], gate_in[:, i, 0, :], 1.0, bank[i][:, :],
                                               ALU.add, ALU.mult))
                    v.scalar_tensor_tensor(gate_in[:, i, 1, :], gate_in[:, i, 1, :], 1.0, bank[2 + i][:, :],
                                           ALU.add, ALU.mult).then_inc(read_out, 1)
                    dve.wait_ge(read_out, u + 3)
                    v.tensor_tensor(mrg[:, i, :], mrg[:, i, :], gate_in[:, i, 1, :], ALU.add).then_inc(mrg_ready, 1)
                    dve.wait_ge(mhi_ready, 2 * j + (i + 1))
                    v.scalar_tensor_tensor(act_lo[:, 2 * j + i, :], mrg[:, i, :], 0.5,
                                           act_hi[:, 2 * j + i, :].bitcast(F32), ALU.mult, ALU.subtract
                                           ).then_inc(mlo_ready, 1)
                own.leave(8, 2)

            def add_tile(t, n, w, done):
                if t < TT - 1:
                    dve.wait_ge(tok_done, 3 * done + (t + 1))
                else:
                    dve.wait_ge(units_done, w)
                cols = bass.ds(n * 512, 512)
                v.tensor_tensor(x1[:, t, cols], x1[:, t, cols], bank[4 + t][:, :], ALU.add).then_inc(tok_free, 1)

            def add_up(n, w, done):
                for t in range(TT):
                    add_tile(t, n, w, done)

            def add_and_norm(c, n, w, done, dst, scaled):
                for t in range(TT + 1):
                    if t < TT:
                        add_tile(t, n, w, done)
                    if t > 0:
                        norm_tile(c, t - 1, dst, scaled)


            def out_split(n):
                for i in range(4):
                    lo(4 * n + (U_O + i + 1), (i + 1) % 2)

            with dve.Fori(0, NB - 1) as n:
                out_split(n)
                dve.wait_ge(xres_here, 16 * TT)
                add_up(n, 4 * n + (U_O + 4 + 2), n)
            n = NB - 1
            out_split(n)
            early_var(1)
            add_and_norm(1, n, 4 * n + U_O + 4 + 2, n, xn, xa_ready)
            transposed(1, KT, U_FF + 1)
            v.memset(stat[:, 0, :], 0.0).then_inc(ff_read, 1)
            v.memset(stat[:, 1, :], 0.0).then_inc(up_read, 1)

            def ff_block(f, first=False, last=False):
                u0 = f * FB_UNITS + U_FF

                def tiles(j, first=False):
                    t = f * FT + j
                    if not first:
                        lo(2 * j + u0 + 1, 1)
                    dve.wait_ge(ff_tanh, t + 1)
                    v.scalar_tensor_tensor(ff_m[:, :], ff_t[:, :], 1.0, bank[0][:, :], ALU.add, ALU.mult
                                           ).then_inc(ff_read, 1)
                    lo(2 * j + u0 + 2, 0)
                    dve.wait_ge(units_done, 2 * j + u0 + 4)
                    dve.wait_ge(ff_read, t + 2)
                    v.tensor_tensor(ff_m[:, :], ff_m[:, :], bank[1][:, :], ALU.mult).then_inc(up_read, 1)
                    dve.wait_ge(up_read, t + 2)
                    dve.wait_ge(ffhi_ready, t + 1)
                    v.scalar_tensor_tensor(m_lo[:, j, :], ff_m[:, :], 0.5, m_hi[:, j, :].bitcast(F32),
                                           ALU.mult, ALU.subtract).then_inc(fflo_ready, 1)
                    dve.wait_ge(fflo_ready, t + 1)

                if first:
                    tiles(0, first=True)
                with dve.Fori(1 if first else 0, FT) as j:
                    tiles(j)

                def down(n, very_last=False):
                    for i in range(2):
                        for e in range(3):
                            x_ = 3 * i + e
                            if not (very_last and x_ == 5):
                                lo(6 * n + (x_ + 1) + u0 + 2 * FT, (x_ + 1) % 2, DK[2] * 512 if e == 1 else UNIT)
                        c = 2 * n + i
                        w, done = 6 * n + (3 * i + 3 + 2) + u0 + 2 * FT, f * NB + 2 * n + (i + NB)
                        if very_last and i == 1:
                            early_var(2)
                            dve.wait_ge(by_g_ready, 2 * TT)
                            add_and_norm(2, c, w, done, xg, out_ready)
                        else:
                            add_up(c, w, done)

                if last:
                    down(0)
                    down(1, True)
                else:
                    with dve.Fori(0, 2) as n:
                        down(n)

            ff_block(0, first=True)
            with dve.Fori(1, FB - 1) as f:
                ff_block(f)
            ff_block(FB - 1, last=True)
        @block.tensor
        def _(pe):
            mm = nc.tensor.matmul

            def three(out_, a_hi, a_lo, b_hi, b_lo, first, last):
                mm(out_, a_hi, b_hi, start=first, stop=False)
                mm(out_, a_hi, b_lo, start=False, stop=False)
                return mm(out_, a_lo, b_hi, start=False, stop=last)

            def unit_here(u):
                pe.wait_ge(lo_ready, u + 1)

            def tile_unit(u, p, out_, between=None):
                unit_here(u)
                for k in range(KT):
                    if between is not None:
                        between(k)
                    ins = three(out_, slot(w_hi, p, P)[:, k], slot(w_lo, p, P)[:, k], act_hi[:, k], act_lo[:, k],
                                k == 0, k == KT - 1)
                ins.then_inc(units_done, 1)

            def in_unit(u, p, between=None):
                pe.wait_ge(read_out, u + 1)
                tile_unit(u, p, bank[p][:, :], between)

            def transpose(src, t, k):
                return nc.tensor.transpose(bank[1 + k % 7][:, t * P:(t + 1) * P], src[:, t, k * P:(k + 1) * P],
                                           ident[:, :])

            def norm_and_unit(src, c, u):
                for ks in ((range(7),), (range(3), range(3, 7)))[c]:
                    if ks[0] == 3:
                        pe.wait_ge(tok_free, TT + NB * TT)
                    for t in range(TT):
                        pe.wait_ge(xa_ready, TT * c + t + 1)
                        for k in ks:
                            ins = transpose(src, t, k)
                            if t == TT - 1:
                                ins.then_inc(tr_done, 1)
                for k in range(KT):
                    pe.wait_ge(nlo_ready, c * KT + k + 1)
                    if k == 0:
                        unit_here(u)
                    ins = three(bank[0][:, :], slot(w_hi, 0, P)[:, k], slot(w_lo, 0, P)[:, k], act_hi[:, k],
                                act_lo[:, k], k == 0, k == KT - 1)
                    if k == 1:
                        pe.wait_ge(xn_ready, TT * (c + 1))
                    if 1 <= k <= KT - 7:
                        for t in range(TT):
                            tr = transpose(src, t, k + 6)
                        tr.then_inc(tr_done, 1)
                ins.then_inc(units_done, 1)

            pe.wait_ge(ident_here, 16)
            pe.wait_ge(af_ready, 1)
            for i in range(4):
                ins = nc.tensor.transpose(bank[0][:, i * GP:(i + 1) * GP],
                                          lam[:, 8 + i].rearrange("g h p -> g (h p)"), ident[0:GP, 0:GP])
            ins.then_inc(par_t, 1)
            pe.wait_ge(const_here, 80)
            nc.tensor.transpose(bank[7][:, 0:48], vec_raw[:, :], ident[0:48, 0:48]).then_inc(units_done, 2)
            pe.wait_ge(vec_ready, 1)
            pe.wait_ge(par_out, 1)
            norm_and_unit(xt, 0, 0)
            pe.wait_ge(par_here, 96)
            for i in (2, 3, 0, 1):
                for c in range(GC):
                    if i < 2:
                        src = par[:, i].rearrange("g h (p c) -> g (h p) c", c=GC)[:, :, c]
                    else:
                        src = par[:, i].rearrange("g a n -> g (a n)")[:, c * P:(c + 1) * P]
                    ins = nc.tensor.transpose(bank[2 + i][:, c * GP:(c + 1) * GP], src, ident[0:GP, 0:GP])
                ins.then_inc(par_t, 1)

            def mixer_inputs(b, first=False):
                for i in range(3):
                    if not (first and i == 0):
                        in_unit(4 * b + i, i % 2)
                pe.wait_ge(tab_b, b + 1)
                for e in range(4):
                    for g in range(4):
                        ins = nc.tensor.transpose(bank[2 + e][:, g * P:(g + 1) * P],
                                                  b_in[:, e // 2, 4 * (e % 2) + g].rearrange("p l c -> p (l c)"),
                                                  ident[:, :])
                    ins.then_inc(bint_done, 1)
                for g in range(GB):
                    for r in range(2):
                        ins = mm(bank[6 + g // 4][0:GP, (g % 4) * P:(g % 4 + 1) * P], bb_pad[:, r, g, :],
                                 cout[:, r, g, 0:L, :].rearrange("p l c -> p (l c)"), start=r == 0, stop=r == 1)
                ins.then_inc(k_done, 1)
                in_unit(4 * b + 3, 1)
                pe.wait_ge(bint_ready, 4 * b + 4)
                pe.wait_ge(u2_here, 128 * b + 128)
                for h in range(2):
                    for g in range(GB):
                        for r in range(2):
                            ins = mm(bank[2 + r][64 * h:64 * h + 64, g * M:(g + 1) * M],
                                     bin_t[:, r, g, 64 * h:64 * h + 64], u2[:, GB * h + g, :], start=True, stop=True)
                ins.then_inc(x_done, 1)

            mixer_inputs(0, first=True)
            with pe.Fori(1, NBLK) as b:
                mixer_inputs(b)

            in_unit(U_KV, 0)
            in_unit(U_KV + 1, 1)

            def gates(n, y=None):
                u0 = 4 * n + U_GATE
                in_unit(u0, 0)
                pe.wait_ge(staged, n + 1)
                nc.tensor.transpose(bank[6][:, 0:P], v_ct[:, :], ident[:, :])
                for j in range(PAIRS):
                    for e in range(2):
                        rows = slice(64 * e, 64 * e + 64)
                        ins = mm(bank[2 + j // 4][rows, (j % 4) * KEYS:(j % 4 + 1) * KEYS], q_c[rows, j, :],
                                 k_c[rows, j // 4, :], start=True, stop=True)
                ins.then_inc(scores_done, 1)
                in_unit(u0 + 1, 1)
                in_unit(u0 + 2, 0, None if y is None else lambda k: y_part(y, 0, k - 4))
                pe.wait_ge(prob_ready, n + 1)
                for j in range(PAIRS):
                    ins = nc.tensor.transpose(bank[4 + j // 4][:, (j % 4) * P:(j % 4 + 1) * P], prob[:, j, :],
                                              ident[:, :])
                    if j % 4 == 3:
                        ins.then_inc(pt_done, 1)
                in_unit(u0 + 3, 1, None if y is None else lambda k: y_part(y, 1, k - 4))
                pe.wait_ge(pt_ready, 2 * n + 2)
                pe.wait_ge(vc_ready, n + 1)
                for kv in range(2):
                    for e in range(2):
                        ins = mm(bank[6][64 * e:64 * e + 64, 256 * kv:256 * kv + 256], v_c[:, 64 * kv:64 * kv + 64],
                                 prob_t[:, 4 * kv:4 * kv + 4, 64 * e:64 * e + 64], start=True, stop=True)
                ins.then_inc(pv_done, 1)

            def y_part(b, h, g):
                if not 0 <= g < GB:
                    return
                if g == 0 and h == 0:
                    pe.wait_ge(ytab_here, 16 * 18 * b + 16 * 18)
                    pe.wait_ge(st_here, 32 * b + 32)
                elif g == 0:
                    pe.wait_ge(y_ev, 2 * b + 1)
                o = bank[7][:, g * M:(g + 1) * M]
                mm(o, toe[:, GB * h + g, :], u2y[:, GB * h + g, :], start=True, stop=False)
                ins = mm(o, cy[:, h, g, :], st_c[:, h, g, :], start=False, stop=True)
                if g == GB - 1:
                    ins.then_inc(y_done, 1)

            with pe.Fori(0, CH_Y) as n:
                gates(n)
            with pe.Fori(CH_Y, CH_Z) as n:
                gates(n, y=n - CH_Y)
            with pe.Fori(CH_Z, NCH) as n:
                gates(n)

            for i in range(4):
                u, p = U_GLU + i, i % 2
                unit_here(u)
                pe.wait_ge(read_out, u + 1)
                for k in range(HT):
                    if i == 0:
                        pe.wait_ge(zlo_ready, k + 1)
                    for e in range(2):
                        cols = slice(e * P, (e + 1) * P)
                        ins = three(bank[2 * e + p][:, :], slot(w_hi, p, 256)[:, k, cols],
                                    slot(w_lo, p, 256)[:, k, cols], act_hi[:, k], act_lo[:, k], k == 0, k == HT - 1)
                ins.then_inc(units_done, 1)
            pe.wait_ge(yblo_ready, 2)
            with pe.Fori(0, 8) as j:
                for i in range(2):
                    u = 2 * j + (U_AB + i)
                    unit_here(u)
                    pe.wait_ge(read_out, u + 1)
                    for e, (a_hi, a_lo) in ((1, (yb_hi, yb_lo)), (0, (ya_hi, ya_lo))):
                        if e == 0:
                            pe.wait_ge(yalo_ready, HT)
                        for k in range(HT):
                            ins = three(bank[2 * e + i][:, :], slot(w_hi, i, P)[:, HT * e + k],
                                        slot(w_lo, i, P)[:, HT * e + k], a_hi[:, k], a_lo[:, k], k == 0, k == HT - 1)
                    ins.then_inc(units_done, 1)

            def tok_unit(u, p, kt0, kn, s_hi, s_lo, first, last, w):
                unit_here(u)
                for t in range(TT):
                    if first:
                        pe.wait_ge(tok_free, w + (t + 1))
                    for k in range(kn):
                        toks = slice(t * P, (t + 1) * P)
                        ins = three(bank[4 + t][:, :], s_hi[:, kt0 + k, toks], s_lo[:, kt0 + k, toks],
                                    slot(w_hi, p, 512)[:, k], slot(w_lo, p, 512)[:, k],
                                    first and k == 0, last and k == kn - 1)
                    if t == TT - 1:
                        ins.then_inc(units_done, 1)
                    elif last:
                        ins.then_inc(tok_done, 1)

            with pe.Fori(0, NB) as n:
                for i in range(4):
                    pe.wait_ge(mlo_ready, 4 * i + 4)
                    tok_unit(4 * n + (U_O + i), i % 2, 4 * i, 4, act_hi, act_lo, i == 0, i == 3, 4 * n)
            norm_and_unit(xn, 1, U_FF)

            def ff_tiles(f, j, first=False):
                u0 = f * FB_UNITS + U_FF
                if not first:
                    pe.wait_ge(ff_read, f * FT + j + 1)
                    tile_unit(2 * j + u0, 0, bank[0][:, :])
                pe.wait_ge(up_read, f * FT + j + 1)
                tile_unit(2 * j + u0 + 1, 1, bank[1][:, :])

            def ff_down(f):
                u0 = f * FB_UNITS + U_FF
                with pe.Fori(0, 2) as n:
                    for i in range(2):
                        for e in range(3):
                            x_ = 3 * i + e
                            pe.wait_ge(fflo_ready, f * FT + min(4 * e + 4, FT))
                            tok_unit(6 * n + x_ + u0 + 2 * FT, x_ % 2, 4 * e, DK[e], m_hi, m_lo, e == 0, e == 2,
                                     TT * NB + f * (TT * NB) + n * (2 * TT) + i * TT)

            ff_tiles(0, 0, first=True)
            with pe.Fori(1, FT) as j:
                ff_tiles(0, j)
            ff_down(0)
            with pe.Fori(1, FB) as f:
                with pe.Fori(0, FT) as j:
                    ff_tiles(f, j)
                ff_down(f)


_INS = ["x", "norm1_g", "w_in", "lam_re", "lam_im", "log_dt", "b_re", "b_im", "c_re", "c_im", "d_skip", "w_glu",
        "b_glu", "sinks", "w_a", "w_b", "w_o", "norm2_g", "w_gate", "w_up", "w_down", "normf_g"]


def alibi():
    dist = np.abs(np.arange(CH)[:, None] + (KEYS - CH) - np.arange(KEYS)[None, :]).astype(np.float32)
    heads = 2 * PAIRS
    slopes = (2.0 ** (-8.0 * np.arange(1, heads + 1) / heads)).astype(np.float32)
    b = -(slopes.reshape(PAIRS, 2)[:, :, None, None] * dist)
    return np.ascontiguousarray(b.transpose(1, 2, 0, 3).reshape(P, PAIRS, KEYS), dtype=np.float32)


def kernel(**inputs):
    import concourse.bacc as _bacc
    from concourse.bass_utils import run_bass_kernel_spmd as _run

    nc = _bacc.Bacc("TRN2", target_bir_lowering=False, num_devices=1)
    arrays = {n: np.ascontiguousarray(inputs[n]) for n in _INS}
    arrays["ident_c"] = np.eye(P, dtype=np.float32)
    arrays["alibi_c"] = alibi()
    args = [nc.dram_tensor(n, a.shape, F32, kind="ExternalInput").ap() for n, a in arrays.items()]
    for n, shape in (("u_s", (NBLK, 2 * P, L, M)), ("cout_s", (NBLK, P, 2, GB, P)),
                     ("kp_s", (NBLK, GC, 2, GB, KPAD)), ("y_s", (NBLK, 2 * P, L, M)), ("gate_s", (32, P, T))):
        args.append(nc.dram_tensor(n, shape, F32).ap())
    args.append(nc.dram_tensor("out", (1, T, D), F32, kind="ExternalOutput").ap())
    build(nc, *args)
    r = _run(nc, [arrays], core_ids=[0])
    return r.results[0]["out"]
```
